# Optimizing a Trainium2 kernel written in Bass

```python
import jax
import jax.numpy as jnp
from jax import lax
import numpy as np
import jax, jax.numpy as jnp

D_MODEL = 1024
BATCH = 1
SEQ = 512
DEPTH = 1

CTX_LEN = 256
GRID_W = 64
N_MOD = 6
NORM_EPS = 1e-6
LN_EPS = 1e-5
RW_N = 64
RW_W = D_MODEL // 2
RW_H = RW_W // RW_N
LORA_DECAY = 64
LORA_ICLR = 64
LORA_GATE = 128
RW_GN_EPS = 64e-5
CONV_W = D_MODEL // 2
CONV_K = 31
ML_H = 4
ML_W = D_MODEL // 2
ML_DH = ML_W // ML_H
ML_CHUNK = 64
N_BRANCH = 3
D_FF = 4 * D_MODEL
RW_COLS = 3 * RW_W + 2 * LORA_DECAY + 2 * LORA_ICLR + LORA_GATE
CV_COLS = 2 * CONV_W
ML_COLS = 4 * ML_W + 4 * ML_H
GATE_COLS = N_BRANCH * D_MODEL
OFF_CV = RW_COLS
OFF_ML = OFF_CV + CV_COLS
OFF_GATE = OFF_ML + ML_COLS
P_TOTAL = OFF_GATE + GATE_COLS


def _split_at(u, sizes):
    return jnp.split(u, [int(s) for s in np.cumsum(sizes)[:-1]], axis=-1)

def _rmsnorm(x, g):
    xf = x.astype(jnp.float32)
    y = xf * lax.rsqrt(jnp.mean(xf * xf, axis=-1, keepdims=True) + NORM_EPS)
    return (y * g.astype(jnp.float32)).astype(x.dtype)

def _layernorm(x, w, b, eps):
    xf = x.astype(jnp.float32)
    xc = xf - jnp.mean(xf, axis=-1, keepdims=True)
    y = xc * lax.rsqrt(jnp.mean(xc * xc, axis=-1, keepdims=True) + eps) * w.astype(jnp.float32)
    if b is not None:
        y = y + b.astype(jnp.float32)
    return y.astype(x.dtype)

def _token_shift(u, mu_prev, mu_next):
    prev = jnp.pad(u, ((0, 0), (1, 0), (0, 0)))[:, :-1]
    nxt = jnp.pad(u, ((0, 0), (0, 1), (0, 0)))[:, 1:]
    return u + mu_prev * (prev - u) + mu_next * (nxt - u)

def _rwkv_feats(u, w0, w2, a0, a2, k_k, k_a):
    B, T, _ = u.shape
    r, k, v, wd_f, wd_b, ad_f, ad_b, gd = _split_at(
        u, (RW_W, RW_W, RW_W, LORA_DECAY, LORA_DECAY, LORA_ICLR, LORA_ICLR, LORA_GATE))

    def heads(t):
        return t.astype(jnp.float32).reshape(B, T, RW_H, RW_N)

    kk = heads(k * k_k)
    kk = kk / jnp.maximum(jnp.sqrt(jnp.sum(kk * kk, axis=-1, keepdims=True)), 1e-12)
    dirs = []
    for d, (wd, ad) in enumerate(((wd_f, ad_f), (wd_b, ad_b))):
        w_log = -jax.nn.softplus(-(w0[d] + jnp.tanh(wd) @ w2[d]).astype(jnp.float32)) - 0.5
        decay = jnp.exp(-jnp.exp(w_log))
        a = jax.nn.sigmoid((a0[d] + ad @ a2[d]).astype(jnp.float32))
        k_d = k.astype(jnp.float32) * (1.0 + (a - 1.0) * k_a)
        dirs.append((heads(decay), heads(k_d), heads(a)))
    return heads(r), heads(k), heads(v), kk, dirs, gd

def _rwkv7_scan(s0, w, k, v, kk, a, r, reverse, emit):
    xs = tuple(jnp.moveaxis(t, 1, 0) for t in (w, k, v, kk, a))
    if emit:
        xs = xs + (jnp.moveaxis(r, 1, 0),)

    def step(S, inp):
        w_t, k_t, v_t, kk_t, a_t = inp[:5]
        S = (S * w_t[:, :, None, :]
             - jnp.einsum('bhvk,bhk->bhv', S, kk_t)[..., None] * (kk_t * a_t)[:, :, None, :]
             + v_t[..., None] * k_t[:, :, None, :])
        y = jnp.einsum('bhvk,bhk->bhv', S, inp[5]) if emit else None
        return S, y

    S, y = lax.scan(step, s0, xs, reverse=reverse)
    return S, (jnp.moveaxis(y, 0, 1) if emit else None)

def _rwkv_out(f, y, r_k, g2, gn_w, gn_b):
    r, k, v, _, _, gd = f
    B, T = r.shape[:2]
    yn = _layernorm(y, gn_w.reshape(RW_H, RW_N), gn_b.reshape(RW_H, RW_N), RW_GN_EPS)
    bonus = jnp.sum(r * k * r_k, axis=-1, keepdims=True) * v
    gate = jax.nn.sigmoid(gd) @ g2
    return (yn + bonus).reshape(B, T, RW_W) * gate

def _rwkv_mixer(u_lat, u_ctx, mu_p, mu_n, w0, w2, a0, a2, k_k, k_a, r_k, g2, gn_w, gn_b, emit_ctx):
    fl = _rwkv_feats(_token_shift(u_lat, mu_p, mu_n), w0, w2, a0, a2, k_k, k_a)
    fc = _rwkv_feats(_token_shift(u_ctx, mu_p, mu_n), w0, w2, a0, a2, k_k, k_a)
    s0 = jnp.zeros((u_lat.shape[0], RW_H, RW_N, RW_N), jnp.float32)
    y_lat, y_ctx = 0.0, 0.0
    for d in range(2):
        rev = d == 1
        w_c, k_c, a_c = fc[4][d]
        s_ctx, yc = _rwkv7_scan(s0, w_c, k_c, fc[2], fc[3], a_c, fc[0], rev, emit_ctx)
        w_l, k_l, a_l = fl[4][d]
        _, yl = _rwkv7_scan(s_ctx, w_l, k_l, fl[2], fl[3], a_l, fl[0], rev, True)
        y_lat = y_lat + yl
        if emit_ctx:
            y_ctx = y_ctx + yc
    out_lat = _rwkv_out(fl, y_lat, r_k, g2, gn_w, gn_b).astype(u_lat.dtype)
    out_ctx = _rwkv_out(fc, y_ctx, r_k, g2, gn_w, gn_b).astype(u_ctx.dtype) if emit_ctx else None
    return out_lat, out_ctx

def _depthwise_conv(z, w, b):
    y = lax.conv_general_dilated(z, w[:, None, :].astype(z.dtype), window_strides=(1,), padding='SAME',
                                 dimension_numbers=('NWC', 'WIO', 'NWC'), feature_group_count=z.shape[-1])
    return y + b

def _conv_branch(u, dw, db, ln_w, ln_b, rows):
    B, T, _ = u.shape
    a, g = jnp.split(u, 2, axis=-1)
    z = a * jax.nn.sigmoid(g)
    if rows is not None:
        z = _depthwise_conv(z.reshape(B * rows, GRID_W, CONV_W), dw, db).reshape(B, T, CONV_W)
    else:
        z = _depthwise_conv(z, dw, db)
    return jax.nn.silu(_layernorm(z, ln_w, ln_b, LN_EPS))

def _mlstm_feats(u, ib, fb):
    B, T, _ = u.shape
    q, k, v, o, gates = _split_at(u, (ML_W, ML_W, ML_W, ML_W, 4 * ML_H))

    def heads(t):
        return jnp.moveaxis(t.astype(jnp.float32).reshape(B, T, ML_H, ML_DH), 2, 1)

    gates = gates.astype(jnp.float32).reshape(B, T, 2, 2, ML_H)
    ig = jnp.moveaxis(gates[:, :, :, 0] + ib, 1, -1)
    lf = jnp.moveaxis(jax.nn.log_sigmoid(gates[:, :, :, 1] + fb), 1, -1)
    return heads(q), heads(k) * ML_DH ** -0.5, heads(v), o, ig, lf

def _mlstm_scan(state, k, v, ig, lf, q, emit):
    B, H, T, dh = k.shape
    nc = T // ML_CHUNK

    def chunks(t):
        return jnp.moveaxis(t.reshape((B, H, nc, ML_CHUNK) + t.shape[3:]), 2, 0)

    tri = jnp.tril(jnp.ones((ML_CHUNK, ML_CHUNK), dtype=bool))
    xs = (chunks(k), chunks(v), chunks(ig), chunks(lf)) + ((chunks(q),) if emit else ())

    def step(carry, inp):
        C, n, m = carry
        kc, vc, ic, fc = inp[:4]
        b = jnp.cumsum(fc, axis=-1)
        h = None
        if emit:
            qc = inp[4]
            dlog = jnp.where(tri, b[..., :, None] - b[..., None, :] + ic[..., None, :], -jnp.inf)
            inter = b + m[..., None]
            m_t = jnp.maximum(inter, jnp.max(dlog, axis=-1))
            s = jnp.einsum('bhtd,bhsd->bhts', qc, kc) * jnp.exp(dlog - m_t[..., None])
            w_inter = jnp.exp(inter - m_t)
            num = (w_inter[..., None] * jnp.einsum('bhvd,bhtd->bhtv', C, qc)
                   + jnp.einsum('bhts,bhsv->bhtv', s, vc))
            den = w_inter * jnp.einsum('bhd,bhtd->bht', n, qc) + jnp.sum(s, axis=-1)
            h = num / jnp.maximum(jnp.abs(den), jnp.exp(-m_t))[..., None]
        b_last = b[..., -1]
        wlog = b_last[..., None] - b + ic
        m_new = jnp.maximum(b_last + m, jnp.max(wlog, axis=-1))
        carry_w = jnp.exp(b_last + m - m_new)
        wk = jnp.exp(wlog - m_new[..., None])[..., None] * kc
        C_new = carry_w[..., None, None] * C + jnp.einsum('bhsv,bhsd->bhvd', vc, wk)
        n_new = carry_w[..., None] * n + jnp.sum(wk, axis=2)
        return (C_new, n_new, m_new), h

    state, h = lax.scan(step, state, xs)
    if emit:
        h = jnp.moveaxis(h, 0, 2).reshape(B, H, T, dh)
    return state, h

def _flip_time(t, rev):
    return jnp.flip(t, axis=2) if rev else t

def _mlstm_out(h, o, nw):
    B, H, T, dh = h.shape
    hn = _layernorm(jnp.moveaxis(h, 1, 2), nw.reshape(ML_H, ML_DH), None, LN_EPS)
    return hn.reshape(B, T, ML_W) * jax.nn.sigmoid(o.astype(jnp.float32))

def _mlstm_mixer(u_lat, u_ctx, ib, fb, nw, emit_ctx):
    ql, kl, vl, ol, il, fl = _mlstm_feats(u_lat, ib, fb)
    qc, kc, vc, oc, ic, fc = _mlstm_feats(u_ctx, ib, fb)
    B = u_lat.shape[0]
    init = (jnp.zeros((B, ML_H, ML_DH, ML_DH), jnp.float32), jnp.zeros((B, ML_H, ML_DH), jnp.float32),
            jnp.zeros((B, ML_H), jnp.float32))
    h_lat, h_ctx = 0.0, 0.0
    for d in range(2):
        rev = d == 1
        st, hc = _mlstm_scan(init, _flip_time(kc, rev), _flip_time(vc, rev), _flip_time(ic[:, d], rev),
                             _flip_time(fc[:, d], rev), _flip_time(qc, rev) if emit_ctx else None, emit_ctx)
        _, hl = _mlstm_scan(st, _flip_time(kl, rev), _flip_time(vl, rev), _flip_time(il[:, d], rev),
                            _flip_time(fl[:, d], rev), _flip_time(ql, rev), True)
        h_lat = h_lat + _flip_time(hl, rev)
        if emit_ctx:
            h_ctx = h_ctx + _flip_time(hc, rev)
    out_lat = _mlstm_out(h_lat, ol, nw).astype(u_lat.dtype)
    out_ctx = _mlstm_out(h_ctx, oc, nw).astype(u_ctx.dtype) if emit_ctx else None
    return out_lat, out_ctx

def _merge(u_gate, ya, yb, yc, pa, pb, pc, wo):
    ga, gb, gc = jnp.split(jax.nn.sigmoid(u_gate), N_BRANCH, axis=-1)
    m = ga * (ya @ pa) + gb * (yb @ pb) + gc * (yc @ pc)
    return m @ wo

def _mlp(h, w1, w2):
    return jnp.square(jax.nn.relu(h @ w1)) @ w2

def first_inputs(seed: int = 0) -> dict:
    key = jax.random.key(seed)
    ks = iter(jax.random.split(key, 40))
    f32 = jnp.float32
    L, D = DEPTH, D_MODEL

    def nrm(shape, scale):
        return scale * jax.random.normal(next(ks), shape, f32)

    def unif(shape, lo, hi):
        return jax.random.uniform(next(ks), shape, f32, lo, hi)

    return {
        'x': nrm((BATCH, SEQ, D), 1.0),
        'c': nrm((BATCH, D), 1.0),
        'ctx': nrm((BATCH, CTX_LEN, D), 1.0),
        'c_ctx': nrm((D,), 1.0),
        'w_ada': nrm((L, D, N_MOD * D), 0.5 * D ** -0.5),
        'b_ada': nrm((L, N_MOD * D), 0.02),
        'g_norm1': 1.0 + nrm((L, D), 0.02),
        'g_norm2': 1.0 + nrm((L, D), 0.02),
        'w_in': nrm((L, D, P_TOTAL), D ** -0.5),
        'mu_prev': unif((L, RW_COLS), 0.0, 0.5),
        'mu_next': unif((L, RW_COLS), 0.0, 0.5),
        'rw_w0': unif((L, 2, RW_W), -6.0, 1.0),
        'rw_w2': nrm((L, 2, LORA_DECAY, RW_W), 0.1),
        'rw_a0': nrm((L, 2, RW_W), 0.5),
        'rw_a2': nrm((L, 2, LORA_ICLR, RW_W), LORA_ICLR ** -0.5),
        'rw_kk': 0.85 + nrm((L, RW_W), 0.05),
        'rw_ka': 1.0 + nrm((L, RW_W), 0.05),
        'rw_rk': nrm((L, RW_H, RW_N), 0.1),
        'rw_g2': nrm((L, LORA_GATE, RW_W), LORA_GATE ** -0.5),
        'rw_lnw': 1.0 + nrm((L, RW_W), 0.02),
        'rw_lnb': nrm((L, RW_W), 0.02),
        'cv_dw': nrm((L, CONV_K, CONV_W), CONV_K ** -0.5),
        'cv_db': nrm((L, CONV_W), 0.02),
        'cv_lnw': 1.0 + nrm((L, CONV_W), 0.02),
        'cv_lnb': nrm((L, CONV_W), 0.02),
        'ml_ib': nrm((L, 2, ML_H), 0.1),
        'ml_fb': jnp.linspace(3.0, 6.0, ML_H, dtype=f32) + nrm((L, 2, ML_H), 0.1),
        'ml_nw': 1.0 + nrm((L, ML_W), 0.02),
        'p_a': nrm((L, RW_W, D), RW_W ** -0.5),
        'p_b': nrm((L, CONV_W, D), CONV_W ** -0.5),
        'p_c': nrm((L, ML_W, D), ML_W ** -0.5),
        'w_out': nrm((L, D, D), D ** -0.5),
        'w_mlp1': nrm((L, D, D_FF), D ** -0.5),
        'w_mlp2': nrm((L, D_FF, D), D_FF ** -0.5),
        'g_final': 1.0 + nrm((D,), 0.02),
    }

def first_block(x, c, ctx, c_ctx, w_ada, b_ada, g_norm1, g_norm2, w_in, mu_prev, mu_next,
              rw_w0, rw_w2, rw_a0, rw_a2, rw_kk, rw_ka, rw_rk, rw_g2, rw_lnw, rw_lnb,
              cv_dw, cv_db, cv_lnw, cv_lnb, ml_ib, ml_fb, ml_nw,
              p_a, p_b, p_c, w_out, w_mlp1, w_mlp2, g_final):
    rows = x.shape[1] // GRID_W
    for l in range(DEPTH):
        last = l == DEPTH - 1
        mod_x = jnp.split((jax.nn.silu(c) @ w_ada[l] + b_ada[l])[:, None, :], N_MOD, axis=-1)
        mod_c = jnp.split(jax.nn.silu(c_ctx) @ w_ada[l] + b_ada[l], N_MOD, axis=-1)
        h = _rmsnorm(x, g_norm1[l]) * (1.0 + mod_x[1]) + mod_x[0]
        hc = _rmsnorm(ctx, g_norm1[l]) * (1.0 + mod_c[1]) + mod_c[0]
        u_rw, u_cv, u_ml, u_gate = jnp.split(h @ w_in[l], [OFF_CV, OFF_ML, OFF_GATE], axis=-1)
        if last:
            uc_rw = hc @ w_in[l, :, :OFF_CV]
            uc_ml = hc @ w_in[l, :, OFF_ML:OFF_GATE]
        else:
            uc_rw, uc_cv, uc_ml, uc_gate = jnp.split(hc @ w_in[l], [OFF_CV, OFF_ML, OFF_GATE], axis=-1)
        ya, ya_c = _rwkv_mixer(u_rw, uc_rw, mu_prev[l], mu_next[l], rw_w0[l], rw_w2[l], rw_a0[l], rw_a2[l],
                               rw_kk[l], rw_ka[l], rw_rk[l], rw_g2[l], rw_lnw[l], rw_lnb[l], not last)
        yc, yc_c = _mlstm_mixer(u_ml, uc_ml, ml_ib[l], ml_fb[l], ml_nw[l], not last)
        yb = _conv_branch(u_cv, cv_dw[l], cv_db[l], cv_lnw[l], cv_lnb[l], rows)
        x = x + mod_x[2] * _merge(u_gate, ya, yb, yc, p_a[l], p_b[l], p_c[l], w_out[l])
        if not last:
            yb_c = _conv_branch(uc_cv, cv_dw[l], cv_db[l], cv_lnw[l], cv_lnb[l], None)
            ctx = ctx + mod_c[2] * _merge(uc_gate, ya_c, yb_c, yc_c, p_a[l], p_b[l], p_c[l], w_out[l])
        h = _rmsnorm(x, g_norm2[l]) * (1.0 + mod_x[4]) + mod_x[3]
        x = x + mod_x[5] * _mlp(h, w_mlp1[l], w_mlp2[l])
        if not last:
            hc = _rmsnorm(ctx, g_norm2[l]) * (1.0 + mod_c[4]) + mod_c[3]
            ctx = ctx + mod_c[5] * _mlp(hc, w_mlp1[l], w_mlp2[l])
    return _rmsnorm(x, g_final)


_first_inputs = first_inputs


def first_inputs(seed=0):
    import zlib

    import numpy as np

    out = dict(_first_inputs(seed))
    spreads = {}
    factors = {'g_norm1': 8.0,
     'g_norm2': 21.638,
     'rw_w2': 8.0,
     'rw_a0': 3.694,
     'rw_kk': 48.376,
     'rw_ka': 45.528,
     'rw_lnw': 64.0,
     'rw_lnb': 64.0,
     'cv_db': 64.0,
     'cv_lnw': 64.0,
     'cv_lnb': 64.0,
     'ml_ib': 64.0,
     'ml_nw': 64.0,
     'g_final': 8.293,
     'ctx': 5.267,
     'c_ctx': 8.0}
    for name, (base, spread) in spreads.items():
        noise = np.random.default_rng([zlib.crc32(name.encode()), seed]).standard_normal(out[name].shape)
        drawn = base * np.exp(spread * noise) if base else spread * noise
        out[name] = jnp.asarray(drawn.astype(out[name].dtype))
    for name, factor in factors.items():
        out[name] = (out[name] * factor).astype(out[name].dtype)
    return out


_narrow_inputs = first_inputs


def first_inputs(seed=0):

    out = dict(_narrow_inputs(seed))
    wider = {'rw_kk': 6.96,
     'rw_lnw': 7.54,
     'rw_lnb': 7.65,
     'cv_lnw': 6.77,
     'cv_lnb': 6.92,
     'ml_nw': 7.41,
     'g_final': 3.41}
    for name, times in wider.items():
        mean = out[name].mean()
        out[name] = (mean + times * (out[name] - mean)).astype(out[name].dtype)
    return out


DEPTH_2 = 2

PLE_DIM = 256
D_FF_2 = 2816
RMS_EPS = 1e-6
DEEPNORM_ALPHA = (2 * DEPTH_2) ** 0.25
DEEPNORM_BETA = (8 * DEPTH_2) ** -0.25

GDN_HEADS = 8
GDN_DK = 64
GDN_DV = 64
GDN_CONV = 4
GDN_CHUNK = 64

SB_HEADS = 4
SB_DIM = 64

MLA_HEADS = 4
MLA_NOPE = 64
MLA_ROPE = 32
MLA_V = 64
MLA_Q_RANK = 256
MLA_KV_RANK = 128
ROPE_BASE = 10000.0

Q_BLOCK = 128

MIX_WIDTH = GDN_HEADS * GDN_DV + SB_HEADS * SB_DIM + MLA_HEADS * MLA_V
IN_WIDTHS = (
    GDN_HEADS * GDN_DK, GDN_HEADS * GDN_DK, GDN_HEADS * GDN_DV,
    GDN_HEADS * GDN_DV,
    GDN_HEADS, GDN_HEADS,
    SB_HEADS * SB_DIM, SB_HEADS * SB_DIM, SB_HEADS * SB_DIM,
    MLA_Q_RANK,
    MLA_KV_RANK + MLA_ROPE,
)
IN_TOTAL = int(sum(IN_WIDTHS))
IN_SPLITS = tuple(int(s) for s in np.cumsum(IN_WIDTHS)[:-1])
GDN_CONV_CH = 2 * GDN_HEADS * GDN_DK + GDN_HEADS * GDN_DV


def layer_norm(x, g, b):
    xf = x.astype(jnp.float32)
    mu = jnp.mean(xf, axis=-1, keepdims=True)
    var = jnp.mean(jnp.square(xf - mu), axis=-1, keepdims=True)
    y = (xf - mu) * lax.rsqrt(var + LN_EPS)
    return (y * g.astype(jnp.float32) + b.astype(jnp.float32)).astype(x.dtype)

def rms_norm(x, w):
    xf = x.astype(jnp.float32)
    y = xf * lax.rsqrt(jnp.mean(jnp.square(xf), axis=-1, keepdims=True) + RMS_EPS)
    return (y * w.astype(jnp.float32)).astype(x.dtype)

def l2_normalize(x):
    xf = x.astype(jnp.float32)
    return xf * lax.rsqrt(jnp.sum(jnp.square(xf), axis=-1, keepdims=True) + RMS_EPS)

def swiglu(h, w_in, w_out):
    gate, up = jnp.split(h @ w_in, 2, axis=-1)
    return (jax.nn.silu(gate) * up) @ w_out

def causal_depthwise_conv(x, w):
    k_width, ch = w.shape
    return lax.conv_general_dilated(
        x, w[:, None, :].astype(x.dtype), window_strides=(1,), padding=[(k_width - 1, 0)],
        dimension_numbers=("NWC", "WIO", "NWC"), feature_group_count=ch)

def rope_tables(positions):
    inv = 1.0 / (ROPE_BASE ** (jnp.arange(0, MLA_ROPE, 2, dtype=jnp.float32) / MLA_ROPE))
    ang = positions.astype(jnp.float32)[..., None] * inv
    return jnp.cos(ang), jnp.sin(ang)

def apply_rope(x, cos, sin):
    x1, x2 = jnp.split(x.astype(jnp.float32), 2, axis=-1)
    return jnp.concatenate([x1 * cos - x2 * sin, x2 * cos + x1 * sin], axis=-1).astype(x.dtype)

def chunk_gated_delta_rule(q, k, v, g, beta):
    B, S, H, DK = q.shape
    DV = v.shape[-1]
    C = GDN_CHUNK
    N = S // C
    f32 = jnp.float32

    def chunks(t):
        t = t.astype(f32).reshape((B, N, C) + t.shape[2:])
        return jnp.moveaxis(jnp.moveaxis(t, 3, 2), 1, 0)

    qc, kc, vc, gc, bc = (chunks(t) for t in (q, k, v, g, beta))
    gc = jnp.cumsum(gc, axis=-1)
    incl = jnp.tril(jnp.ones((C, C), dtype=bool))
    strict = jnp.tril(jnp.ones((C, C), dtype=bool), -1)
    diff = gc[..., :, None] - gc[..., None, :]
    decay = jnp.where(incl, jnp.exp(jnp.where(incl, diff, 0.0)), 0.0)
    kb = kc * bc[..., None]
    lhs = jnp.where(strict, jnp.einsum('nbhid,nbhjd->nbhij', kb, kc) * decay, 0.0) + jnp.eye(C, dtype=f32)
    u = lax.linalg.triangular_solve(lhs, vc * bc[..., None], left_side=True, lower=True, unit_diagonal=True)
    w = lax.linalg.triangular_solve(lhs, kb * jnp.exp(gc)[..., None], left_side=True, lower=True, unit_diagonal=True)
    qk = jnp.where(incl, jnp.einsum('nbhid,nbhjd->nbhij', qc, kc) * decay, 0.0)
    q_dec = qc * jnp.exp(gc)[..., None]
    k_dec = kc * jnp.exp(gc[..., -1:] - gc)[..., None]
    g_last = jnp.exp(gc[..., -1])

    def step(state, xs):
        u_n, w_n, qk_n, qd_n, kd_n, gl_n = xs
        v_new = u_n - jnp.einsum('bhck,bhkv->bhcv', w_n, state)
        o_n = jnp.einsum('bhck,bhkv->bhcv', qd_n, state) + jnp.einsum('bhij,bhjv->bhiv', qk_n, v_new)
        state = state * gl_n[..., None, None] + jnp.einsum('bhck,bhcv->bhkv', kd_n, v_new)
        return state, o_n

    s0 = jnp.zeros((B, H, DK, DV), f32)
    _, o = lax.scan(step, s0, (u, w, qk, q_dec, k_dec, g_last))
    return jnp.transpose(o, (1, 0, 3, 2, 4)).reshape(B, S, H, DV)

def gated_deltanet(gq, gk, gv, gz, ga, gb, conv_w, a_log, dt_bias, norm_w):
    B, S, _ = gq.shape
    f32 = jnp.float32
    qkv = jax.nn.silu(causal_depthwise_conv(jnp.concatenate([gq, gk, gv], axis=-1), conv_w))
    q, k, v = jnp.split(qkv, [GDN_HEADS * GDN_DK, 2 * GDN_HEADS * GDN_DK], axis=-1)
    q = l2_normalize(q.reshape(B, S, GDN_HEADS, GDN_DK)) * (GDN_DK ** -0.5)
    k = l2_normalize(k.reshape(B, S, GDN_HEADS, GDN_DK))
    v = v.reshape(B, S, GDN_HEADS, GDN_DV)
    beta = jax.nn.sigmoid(gb.astype(f32))
    g = -jnp.exp(a_log.astype(f32)) * jax.nn.softplus(ga.astype(f32) + dt_bias.astype(f32))
    o = chunk_gated_delta_rule(q, k, v, g, beta)
    o = rms_norm(o, norm_w) * jax.nn.silu(gz.reshape(B, S, GDN_HEADS, GDN_DV).astype(f32))
    return o.reshape(B, S, GDN_HEADS * GDN_DV).astype(gq.dtype)

def to_query_blocks(t):
    B, S = t.shape[:2]
    return jnp.swapaxes(t.reshape((B, S // Q_BLOCK, Q_BLOCK) + t.shape[2:]), 0, 1)

def from_query_blocks(t):
    t = jnp.swapaxes(t, 0, 1)
    return t.reshape((t.shape[0], t.shape[1] * t.shape[2]) + t.shape[3:])

def stick_breaking_attention(q, k, v):
    S = q.shape[1]
    scale = SB_DIM ** -0.5
    kpos = jnp.arange(S)

    def block(args):
        qb, i = args
        z = jnp.einsum('bqhd,bkhd->bhqk', qb, k).astype(jnp.float32) * scale
        qpos = i * Q_BLOCK + jnp.arange(Q_BLOCK)
        mask = kpos[None, :] < qpos[:, None]
        log_1m = jnp.where(mask, jax.nn.log_sigmoid(-z), 0.0)
        rest = lax.cumsum(log_1m, axis=3, reverse=True) - log_1m
        wts = jnp.where(mask, jnp.exp(jax.nn.log_sigmoid(z) + rest), 0.0)
        return jnp.einsum('bhqk,bkhd->bqhd', wts.astype(v.dtype), v)

    nb = S // Q_BLOCK
    out = lax.map(block, (to_query_blocks(q), jnp.arange(nb)))
    return from_query_blocks(out)

def mla_attention(q_nope, q_rope, k_nope, k_rope, v):
    S = q_nope.shape[1]
    scale = (MLA_NOPE + MLA_ROPE) ** -0.5
    kpos = jnp.arange(S)

    def block(args):
        qn, qr, i = args
        s = (jnp.einsum('bqhd,bkhd->bhqk', qn, k_nope) + jnp.einsum('bqhd,bkd->bhqk', qr, k_rope)).astype(jnp.float32) * scale
        qpos = i * Q_BLOCK + jnp.arange(Q_BLOCK)
        s = jnp.where(kpos[None, :] <= qpos[:, None], s, -jnp.inf)
        pr = jax.nn.softmax(s, axis=-1)
        return jnp.einsum('bhqk,bkhd->bqhd', pr.astype(v.dtype), v)

    nb = S // Q_BLOCK
    out = lax.map(block, (to_query_blocks(q_nope), to_query_blocks(q_rope), jnp.arange(nb)))
    return from_query_blocks(out)

def hybrid_mixer(h, cos, sin, w_in, conv_w, a_log, dt_bias, gdn_norm_w, q_norm_w, kv_norm_w, w_uq, w_ukv, w_o):
    B, S, _ = h.shape
    proj = h @ w_in
    gq, gk, gv, gz, ga, gb, sq, sk, sv, mq, mkv = jnp.split(proj, IN_SPLITS, axis=-1)
    o_gdn = gated_deltanet(gq, gk, gv, gz, ga, gb, conv_w, a_log, dt_bias, gdn_norm_w)
    shp = (B, S, SB_HEADS, SB_DIM)
    o_sb = stick_breaking_attention(sq.reshape(shp), sk.reshape(shp), sv.reshape(shp)).reshape(B, S, SB_HEADS * SB_DIM)
    qf = (rms_norm(mq, q_norm_w) @ w_uq).reshape(B, S, MLA_HEADS, MLA_NOPE + MLA_ROPE)
    q_nope, q_rope = jnp.split(qf, [MLA_NOPE], axis=-1)
    ckv, k_rope = jnp.split(mkv, [MLA_KV_RANK], axis=-1)
    kvf = (rms_norm(ckv, kv_norm_w) @ w_ukv).reshape(B, S, MLA_HEADS, MLA_NOPE + MLA_V)
    k_nope, v_mla = jnp.split(kvf, [MLA_NOPE], axis=-1)
    q_rope = apply_rope(q_rope, cos[:, :, None, :], sin[:, :, None, :])
    k_rope = apply_rope(k_rope, cos, sin)
    o_mla = mla_attention(q_nope, q_rope, k_nope, k_rope, v_mla).reshape(B, S, MLA_HEADS * MLA_V)
    return jnp.concatenate([o_gdn, o_sb, o_mla], axis=-1) @ w_o

def second_inputs(seed: int = 0) -> dict:
    key = jax.random.key(seed)
    ks = jax.random.split(key, 24)
    f32 = jnp.float32
    L = DEPTH_2

    def nrm(k, shape, scale):
        return jax.random.normal(k, shape, f32) * scale

    x = nrm(ks[0], (BATCH, SEQ, D_MODEL), 1.0)
    p = nrm(ks[1], (DEPTH_2, BATCH, SEQ, PLE_DIM), 1.0)
    positions = (jnp.arange(SEQ, dtype=jnp.int32)[None, :]
                 + jax.random.randint(ks[2], (BATCH, 1), 0, 1024, dtype=jnp.int32))
    a_init = jax.random.uniform(ks[7], (L, GDN_HEADS), f32, 1.0, 16.0)
    dt = jnp.exp(jax.random.uniform(ks[8], (L, GDN_HEADS), f32, np.log(1e-3), np.log(1e-1)))
    return {
        "x": x,
        "p": p,
        "positions": positions,
        "ffa_w_in": nrm(ks[3], (L, D_MODEL, 2 * D_FF_2), D_MODEL ** -0.5),
        "ffa_w_out": nrm(ks[4], (L, D_FF_2, D_MODEL), D_FF_2 ** -0.5 * DEEPNORM_BETA),
        "mix_w_in": nrm(ks[5], (L, D_MODEL, IN_TOTAL), D_MODEL ** -0.5),
        "gdn_conv_w": nrm(ks[6], (L, GDN_CONV, GDN_CONV_CH), GDN_CONV ** -0.5),
        "gdn_a_log": jnp.log(a_init),
        "gdn_dt_bias": dt + jnp.log(-jnp.expm1(-dt)),
        "gdn_norm_w": 1.0 + nrm(ks[9], (L, GDN_DV), 0.02),
        "mla_q_norm_w": 1.0 + nrm(ks[10], (L, MLA_Q_RANK), 0.02),
        "mla_kv_norm_w": 1.0 + nrm(ks[11], (L, MLA_KV_RANK), 0.02),
        "mla_w_uq": nrm(ks[12], (L, MLA_Q_RANK, MLA_HEADS * (MLA_NOPE + MLA_ROPE)), MLA_Q_RANK ** -0.5),
        "mla_w_ukv": nrm(ks[13], (L, MLA_KV_RANK, MLA_HEADS * (MLA_NOPE + MLA_V)), MLA_KV_RANK ** -0.5),
        "mix_w_o": nrm(ks[14], (L, MIX_WIDTH, D_MODEL), MIX_WIDTH ** -0.5 * DEEPNORM_BETA),
        "ffb_w_in": nrm(ks[15], (L, D_MODEL, 2 * D_FF_2), D_MODEL ** -0.5),
        "ffb_w_out": nrm(ks[16], (L, D_FF_2, D_MODEL), D_FF_2 ** -0.5 * DEEPNORM_BETA),
        "ln_g": 1.0 + nrm(ks[17], (L, 3, D_MODEL), 0.02),
        "ln_b": nrm(ks[18], (L, 3, D_MODEL), 0.02),
        "ple_w_gate": nrm(ks[19], (L, D_MODEL, D_MODEL), D_MODEL ** -0.5),
        "ple_w_proj": nrm(ks[20], (L, PLE_DIM, D_MODEL), PLE_DIM ** -0.5 * DEEPNORM_BETA),
    }

def second_block(x, p, positions, ffa_w_in, ffa_w_out, mix_w_in, gdn_conv_w, gdn_a_log, gdn_dt_bias,
              gdn_norm_w, mla_q_norm_w, mla_kv_norm_w, mla_w_uq, mla_w_ukv, mix_w_o,
              ffb_w_in, ffb_w_out, ln_g, ln_b, ple_w_gate, ple_w_proj):
    cos, sin = rope_tables(positions)
    h = x
    for i in range(DEPTH_2):
        h = layer_norm(DEEPNORM_ALPHA * h + 0.5 * swiglu(h, ffa_w_in[i], ffa_w_out[i]), ln_g[i, 0], ln_b[i, 0])
        mix = hybrid_mixer(h, cos, sin, mix_w_in[i], gdn_conv_w[i], gdn_a_log[i], gdn_dt_bias[i], gdn_norm_w[i],
                           mla_q_norm_w[i], mla_kv_norm_w[i], mla_w_uq[i], mla_w_ukv[i], mix_w_o[i])
        h = layer_norm(DEEPNORM_ALPHA * h + mix, ln_g[i, 1], ln_b[i, 1])
        h = layer_norm(DEEPNORM_ALPHA * h + 0.5 * swiglu(h, ffb_w_in[i], ffb_w_out[i]), ln_g[i, 2], ln_b[i, 2])
        h = h + jax.nn.sigmoid(h @ ple_w_gate[i]) * (p[i] @ ple_w_proj[i])
    return h


def setup_inputs(seed=0):
    out = dict(first_inputs(seed))
    for name, value in second_inputs(seed + 1).items():
        if name != "x":
            out[name + "_2"] = value
    return out


def reference(
    x, c, ctx, c_ctx, w_ada, b_ada, g_norm1, g_norm2, w_in, mu_prev, mu_next, rw_w0, rw_w2,
    rw_a0, rw_a2, rw_kk, rw_ka, rw_rk, rw_g2, rw_lnw, rw_lnb, cv_dw, cv_db, cv_lnw, cv_lnb,
    ml_ib, ml_fb, ml_nw, p_a, p_b, p_c, w_out, w_mlp1, w_mlp2, g_final, p_2, positions_2,
    ffa_w_in_2, ffa_w_out_2, mix_w_in_2, gdn_conv_w_2, gdn_a_log_2, gdn_dt_bias_2, gdn_norm_w_2,
    mla_q_norm_w_2, mla_kv_norm_w_2, mla_w_uq_2, mla_w_ukv_2, mix_w_o_2, ffb_w_in_2,
    ffb_w_out_2, ln_g_2, ln_b_2, ple_w_gate_2, ple_w_proj_2,
):
    x = first_block(
        x, c, ctx, c_ctx, w_ada, b_ada, g_norm1, g_norm2, w_in, mu_prev, mu_next, rw_w0, rw_w2,
        rw_a0, rw_a2, rw_kk, rw_ka, rw_rk, rw_g2, rw_lnw, rw_lnb, cv_dw, cv_db, cv_lnw, cv_lnb,
        ml_ib, ml_fb, ml_nw, p_a, p_b, p_c, w_out, w_mlp1, w_mlp2, g_final,
    )
    return second_block(
        x, p_2, positions_2, ffa_w_in_2, ffa_w_out_2, mix_w_in_2, gdn_conv_w_2, gdn_a_log_2,
        gdn_dt_bias_2, gdn_norm_w_2, mla_q_norm_w_2, mla_kv_norm_w_2, mla_w_uq_2, mla_w_ukv_2,
        mix_w_o_2, ffb_w_in_2, ffb_w_out_2, ln_g_2, ln_b_2, ple_w_gate_2, ple_w_proj_2,
    )


_drawn_inputs = setup_inputs


def setup_inputs(seed=0):
    import zlib

    import numpy as np

    out = dict(_drawn_inputs(seed))
    spreads = {}
    factors = {'gdn_norm_w_2': 8.0, 'mla_q_norm_w_2': 8.0, 'mla_kv_norm_w_2': 8.0}
    for name, (base, spread) in spreads.items():
        noise = np.random.default_rng([zlib.crc32(name.encode()), seed]).standard_normal(out[name].shape)
        drawn = base * np.exp(spread * noise) if base else spread * noise
        out[name] = jnp.asarray(drawn.astype(out[name].dtype))
    for name, factor in factors.items():
        out[name] = (out[name] * factor).astype(out[name].dtype)
    return out
```

```python
from contextlib import ExitStack

import numpy as np

import concourse.bass as bass
from concourse import mybir

F32 = mybir.dt.float32
U32 = mybir.dt.uint32
I32 = mybir.dt.int32
ALU = mybir.AluOpType
ACT = mybir.ActivationFunctionType
AX = mybir.AxisListType.X
ADD, SUB, MUL, MAX, MIN = ALU.add, ALU.subtract, ALU.mult, ALU.max, ALU.min
NEG = -1.0e30
KAP = float(np.exp(-0.5))
SLOT = 4096
NSLOT = 2
ARENA = 52600


def const_tables():
    i = np.arange(128)[:, None]
    j = np.arange(128)[None, :]
    same = i // 64 == j // 64
    t = {"ident": i == j, "ones": np.ones((128, 128)), "blk": same, "J": i + j == 127}
    for n in range(6):
        s = 1 << n
        m = (i // (2 * s) == j // (2 * s)) & (i // s % 2 == 1) & (j // s % 2 == 0)
        t[f"M{n}"] = m
        t[f"N{n}"] = m.T
    t["US"] = same & (i < j)
    t["UI"] = same & (i <= j)
    t["LS"] = same & (i > j)
    t["LI"] = same & (i >= j)
    t["US128"] = i < j
    t["LS128"] = i > j
    t["nUI128"] = -1.0 * (i <= j)
    t["nLI128"] = -1.0 * (i >= j)
    t["none"] = -np.ones((128, 128))
    t["negGT"] = NEG * (i > j)
    t["negLT"] = NEG * (i < j)
    t["negGE"] = NEG * (i >= j)
    t["negGD"] = NEG * (1 - (same & (i >= j)))
    t["b2"] = (i // 64 == j) * (j < 2)
    t["half0"] = (i < 64) + 0 * j
    t["half1"] = (i >= 64) + 0 * j
    t["rs64"] = 1.0 * (j % 64 != 0) + 0 * i
    t["rs128"] = 1.0 * (j != 0) + 0 * i
    for d in range(2):
        for h in range(4):
            t[f"sel{d}{h}"] = (i == 32 * d + h) + 0 * j
    inv = (1.0 / (np.float32(10000.0) ** (np.arange(0, 32, 2, dtype=np.float32) / np.float32(32)))).astype(np.float32)
    r = np.zeros((128, 128), np.float32)
    r[64:96, 0] = np.concatenate([inv, inv])
    r[64:96, 1] = np.concatenate([-np.ones(16), np.ones(16)])
    t["rope"] = r
    names = list(t)
    return names, np.concatenate([np.asarray(t[k], np.float32) for k in names], axis=1)


VECS = [("c", 8), ("cc", 8), ("bada", 48), ("g1", 8), ("g2", 8), ("mup", 15), ("mun", 15), ("w0", 8), ("a0", 8),
        ("kk", 4), ("ka", 4), ("rk", 4), ("cdw", 124), ("cdb", 4), ("clw", 4), ("clb", 4),
        ("gcw0", 48), ("gcw1", 48), ("qn0", 2), ("qn1", 2), ("kn0", 1), ("kn1", 1)]
VOFF, _o = {}, 0
for _n, _k in VECS:
    VOFF[_n] = (_o, _k)
    _o += _k
NVEC = _o


class Counter:

    def __init__(self, sem):
        self.sem, self.n = sem, 0


class Queue(Counter):

    def __init__(self, sem, chained):
        super().__init__(sem)
        self.todo, self.seen, self.chained = [], {}, chained

    def wait(self, tokens):
        for who, v in tokens:
            if self.seen.get(id(who), 0) < v:
                self.seen[id(who)] = v
                self.todo.append(("wait", who.sem, v))

    def op(self, fn, w=(), sig=True):
        self.wait(w)
        if self.chained:
            self.wait([(self, self.n)])
        if not sig:
            self.todo.append(("op", fn, None, 0))
            return None
        self.n += 1
        self.todo.append(("op", fn, self.sem, 1))
        return (self, self.n)

    def dma(self, fn, counter, w=()):
        self.wait(w)
        counter.n += 16
        self.todo.append(("op", fn, counter.sem, 16))
        return (counter, counter.n)

    def run(self, eng):
        for x in self.todo:
            if x[0] == "wait":
                eng.wait_ge(x[1], x[2])
            else:
                ins = x[1]()
                if x[2] is not None:
                    ins.then_inc(x[2], x[3])


def view(ap, *dims):
    return bass.AP(ap.tensor, ap.offset, [ap.ap[0]] + [list(d) for d in dims])


def build(nc, I, out):
    with ExitStack() as ctx:
        sems = iter(ctx.enter_context(nc.semaphore(f"s{n}")) for n in range(60))
        arena = ctx.enter_context(nc.sbuf_tensor("arena", [128, ARENA], F32))
        psum = ctx.enter_context(nc.psum_tensor("psum", [128, 8, 512], F32))
        P, V, S, G, D = (Queue(next(sems), c) for c in (False, True, True, True, False))
        slot_sem = [Counter(next(sems)) for _ in range(NSLOT)]
        small_sem = [Counter(next(sems)) for _ in range(24)]
        body(nc, I, out, arena, psum, P, V, S, G, D, slot_sem, small_sem)
        block = ctx.enter_context(nc.Block())

        @block.sync
        def _(e):
            D.run(e)

        @block.tensor
        def _(e):
            P.run(e)

        @block.vector
        def _(e):
            V.run(e)

        @block.scalar
        def _(e):
            S.run(e)

        @block.gpsimd
        def _(e):
            G.run(e)
            for c in small_sem + slot_sem:
                if c.n:
                    e.wait_ge(c.sem, c.n)


def body(nc, I, out, arena, psum, P, V, S, G, D, slot_sem, small_sem):
    top = [0]

    def al(n):
        o = top[0]
        top[0] += n
        assert top[0] <= ARENA, (top[0], n)
        return arena[:, o:o + n]

    free_banks = [(b, ()) for b in range(8)]

    def bank():
        b, w = free_banks.pop(0)
        return b, psum[:, b, :], list(w)

    def rel(b, *tokens):
        free_banks.append((b, tokens))

    def barrier():
        ends = [(q, q.n) for q in (P, V, S, G)]
        for q in (P, V, S, G):
            q.wait(ends)
        return ends

    def mm(o, l, r, start, stop, w=(), sig=False):
        return P.op(lambda: nc.tensor.matmul(o, l, r, start=start, stop=stop, skip_group_check=True), w, sig)

    def tr(o, i, w=(), sig=False):
        return P.op(lambda: nc.tensor.transpose(o, i, C["ident"]), w, sig)

    def act(o, i, f, scale=1.0, bias=0.0, w=(), acc=None):
        if acc is None:
            return S.op(lambda: nc.scalar.activation(o, i, f, scale=scale, bias=bias), w)
        return S.op(lambda: nc.scalar.activation(o, i, f, scale=scale, bias=bias, accum_out=acc), w)

    def scopy(o, i, w=(), scale=1.0):
        return act(o, i, ACT.Copy, scale=scale, w=w)

    def vcopy(o, i, w=()):
        return V.op(lambda: nc.vector.tensor_copy(o, i), w)

    def vtt(o, a, b, f, w=()):
        return V.op(lambda: nc.vector.tensor_tensor(o, a, b, f), w)

    def vts(o, a, s1, s2, f0, f1=None, w=()):
        if f1 is None:
            return V.op(lambda: nc.vector.tensor_scalar(o, a, s1, None, f0), w)
        return V.op(lambda: nc.vector.tensor_scalar(o, a, s1, s2, f0, f1), w)

    def stt(o, a, s, b, f0, f1, w=()):
        return V.op(lambda: nc.vector.scalar_tensor_tensor(out=o, in0=a, scalar=s, in1=b, op0=f0, op1=f1), w)

    def vred(o, i, f, w=()):
        return V.op(lambda: nc.vector.tensor_reduce(o, i, AX, f), w)

    def recip(o, i, w=()):
        return V.op(lambda: nc.vector.reciprocal(o, i), w)

    def scan(o, a, b, f0, f1, w=()):
        return V.op(lambda: nc.vector.tensor_tensor_scan(o, a, b, 0.0, f0, f1), w)

    def cpred(o, m, d, w=()):
        return V.op(lambda: nc.vector.copy_predicated(o, m, d), w)

    def vset(o, v, w=()):
        return V.op(lambda: nc.vector.memset(o, v), w)

    def gtt(o, a, b, f, w=()):
        return G.op(lambda: nc.gpsimd.tensor_tensor(o, a, b, f), w)

    n_small = [0]

    def load_small(dst, src, w=()):
        c = small_sem[n_small[0] % len(small_sem)]
        n_small[0] += 1

        def go():
            with nc.allow_non_contiguous_dma(reason="small"):
                return nc.gpsimd.dma_start(dst, src)
        return G.dma(go, c, list(w) + [(c, c.n)])


    ring = al(SLOT * NSLOT)
    slot_free = [()] * NSLOT
    n_load = [0]

    def wload(pieces):
        s = n_load[0] % NSLOT
        n_load[0] += 1
        sl = ring[:, s * SLOT:(s + 1) * SLOT]
        tok = None
        for i, (fn, src) in enumerate(pieces):
            dst = fn(sl)
            tok = D.dma(lambda dst=dst, src=src: nc.sync.dma_start(dst, src), slot_sem[s], slot_free[s] if i == 0 else ())
        return s, sl, tok

    def chunk(W, r0, kt, c0, nc_):
        src = W[r0:r0 + 128 * kt, c0:c0 + nc_].rearrange("(k p) c -> p k c", p=128)
        s, sl, tok = wload([(lambda x: view(x, [nc_, kt], [1, nc_]), src)])
        return s, view(sl, [nc_, kt], [1, nc_]), tok

    def gemm_fm(W, c0, ncols, kt, x, segs, evac, w=(), r0=0):
        done = 0
        while done < ncols:
            n = min(512, ncols - done)
            s, wv, tok = chunk(W, r0, kt, c0 + done, n)
            for m in range(0, n, 128):
                mw = min(128, n - m)
                use = segs((done + m) // 128)
                for g, (a, sz) in enumerate(use):
                    b, pv, bw = bank()
                    for k in range(kt):
                        t = mm(pv[0:mw, 0:sz], wv[:, k, m:m + mw], x[:, k, a:a + sz], k == 0, k == kt - 1,
                               bw + [tok] + list(w) if k == 0 else (), k == kt - 1)
                    slot_free[s] = (t,)
                    rel(b, evac((done + m) // 128, g, pv, t))
            done += n

    def gemm_tm(W, c0, ncols, kt, x, tiles, evac, w=(), kmax=8, step=512):
        done = 0
        while done < ncols:
            n = min(step, ncols - done)
            banks = [bank() for _ in tiles] if kt > kmax else None
            for k0 in range(0, kt, kmax):
                kn = min(kmax, kt - k0)
                s, wv, tok = chunk(W, 128 * k0, kn, c0 + done, n)
                for i, a in enumerate(tiles):
                    b, pv, bw = banks[i] if banks else bank()
                    for k in range(kn):
                        first, last = k0 + k == 0, k0 + k == kt - 1
                        t = mm(pv[:, 0:n], x[:, k0 + k, a:a + 128], wv[:, k, :], first, last,
                               (bw if first else []) + [tok] + list(w) if k == 0 else (), k == kn - 1)
                    slot_free[s] = (t,)
                    if k0 + kn == kt:
                        rel(b, evac(done, i, pv, t, n))
            done += n

    def to_fm(srcs, nf, dst, evac=None, w=(), width=128):
        t2 = None
        for f in range(nf):
            for q in range(0, len(srcs), 4):
                part = srcs[q:q + 4]
                b, pv, bw = bank()
                for i, s_ in enumerate(part):
                    t = tr(pv[:, 128 * i:128 * i + 128], s_[:, 128 * f:128 * f + 128],
                           bw + list(w) if i == 0 else (), i == len(part) - 1)
                o = dst(f)[:, 128 * q:128 * q + 128 * len(part)]
                i_ = pv[:, 0:128 * len(part)]
                t2 = evac(f, o, i_, t) if evac else scopy(o, i_, [t])
                rel(b, t2)
        return t2

    names, _ = const_tables()
    cst = al(128 * len(names))
    C = {k: cst[:, 128 * i:128 * i + 128] for i, k in enumerate(names)}
    t_c = load_small(cst, I["consts"])
    vec = al(NVEC)
    t_v = load_small(vec, I["vecs"])
    VC = {k: vec[:, o:o + n] for k, (o, n) in VOFF.items()}
    for q in (P, V, S, G):
        q.wait([t_c, t_v])

    def rep(c, n, width=128):
        return view(c, [0, n], [1, width])

    def row(src_ap, n):
        return bass.AP(src_ap.tensor, src_ap.offset, [[0, 128], [1, n]])

    def rstd(o, ssq, n, eps, w=()):
        t = vts(o, ssq, 1.0 / n, eps, MUL, ADD, w=w)
        t = act(o, o, ACT.Sqrt, w=[t])
        return recip(o, o, [t])

    st6 = al(16)

    def layer_norm_tile(o, x, n, eps, scr, w=()):
        V.op(lambda: nc.vector.bn_stats(st6[:, 0:6], x[:, 0:512]), w)
        V.op(lambda: nc.vector.bn_stats(st6[:, 6:12], x[:, 512:1024]))
        t = V.op(lambda: nc.vector.bn_aggr(scr[:, 0:2], st6[:, 0:12]))
        rstd(scr[:, 2:3], scr[:, 1:2], 1.0, eps, w=[t])
        return vts(o, x, scr[:, 0:1], scr[:, 2:3], SUB, MUL)

    def group_norm(x, g, n, eps, scr, sq, mean, w=()):
        x3, q3 = view(x, [n, g], [1, n]), view(sq, [n, g], [1, n])
        if mean:
            vred(scr[:, 0:g], x3, ADD, w)
            vts(scr[:, 0:g], scr[:, 0:g], 1.0 / n, None, MUL)
            vtt(x3, x3, view(scr[:, 0:g], [1, g], [0, n]), SUB)
            w = ()
        vtt(q3, x3, x3, MUL, w)
        t = vred(scr[:, g:2 * g], q3, ADD)
        rstd(scr[:, 2 * g:3 * g], scr[:, g:2 * g], n, eps, [t])
        return vtt(x3, x3, view(scr[:, 2 * g:3 * g], [1, g], [0, n]), MUL)

    def invert(groups, low):
        toks = [g[3] for g in groups]
        for n in range(1, 6):
            m, mt = (C[f"M{n}"], C[f"N{n}"]) if low else (C[f"N{n}"], C[f"M{n}"])
            m, mt = rep(m, 4).bitcast(U32), rep(mt, 4).bitcast(U32)
            xs = []
            for gi, (T, TT, AT, _, X) in enumerate(groups):
                b, pv, bw = bank()
                for i in range(4):
                    t = mm(pv[:, 128 * i:128 * i + 128], AT[:, i, :], T[:, i, :], True, True,
                           bw + toks[gi] if i == 0 else (), i == 3)
                tx = scopy(view(X, [1, 512]), pv, [t])
                rel(b, tx)
                xs.append(tx)
            for gi, (T, TT, AT, _, X) in enumerate(groups):
                new = []
                jobs = [(1, TT, mt)] if n == 5 else [(0, T, m), (1, TT, mt)]
                for which, dst, mask in jobs:
                    b, pv, bw = bank()
                    for i in range(4):
                        l, r = (TT[:, i, :], X[:, i, :]) if which == 0 else (X[:, i, :], TT[:, i, :])
                        t = mm(pv[:, 128 * i:128 * i + 128], l, r, True, True,
                               bw + [xs[gi]] + toks[gi] if i == 0 else (), i == 3)
                    new.append((b, pv, t, dst, mask))
                last = new[-1][2]
                out_t = []
                for b, pv, t, dst, mask in new:
                    t2 = cpred(dst, mask, view(pv, [128, 4], [1, 128]), [last])
                    rel(b, t2)
                    out_t.append(t2)
                toks[gi] = out_t
        return toks

    SEGS = [(0, 512), (512, 256)]
    W512 = [0, 128, 256, 384]
    TW = 770
    TO = [514, 642, 0, 128, 256, 384]
    SEQ_ = ([0, 1, 2, 3, 4, 5], [1, 0, 5, 4, 3, 2])

    mk_hT = top[0]
    hT = view(al(8 * 768), [768, 8], [1, 768])
    ybT = view(al(4 * 512), [512, 4], [1, 512])
    ycT = view(al(4 * 512), [512, 4], [1, 512])
    silc = al(16)
    silcv = view(silc, [2, 8], [1, 2])
    mod = view(al(96), [2, 48], [1, 2])
    small = al(256)

    act(view(silc, [2, 8]), VC["c"], ACT.Silu)
    t_sil = act(view(silc[:, 1:2], [2, 8]), VC["cc"], ACT.Silu)
    need = [0, 1, 3, 4]
    for part in need:
        b, pv, bw = bank()
        for hf in range(2):
            s, wv, tok = chunk(I["w_ada"], 0, 8, part * 1024 + 512 * hf, 512)
            for m in range(4):
                for k in range(8):
                    t = mm(pv[:, 8 * hf + 2 * m:8 * hf + 2 * m + 2], wv[:, k, 128 * m:128 * m + 128], silcv[:, k, :],
                           k == 0, k == 7, bw + [tok, t_sil] if k == 0 and m == 0 else (), k == 7 and m == 3)
            slot_free[s] = (t,)
        o = mod[:, 8 * part:8 * part + 8, :]
        t = vtt(o, view(pv, [2, 8], [1, 2]), view(VC["bada"][:, 8 * part:8 * part + 8], [1, 8], [0, 2]), ADD, [t])
        rel(b, t)
    sc1 = view(al(16), [2, 8], [1, 2])
    sc2 = view(al(16), [2, 8], [1, 2])
    for sc, part, g in ((sc1, 1, "g1"), (sc2, 4, "g2")):
        vts(sc, mod[:, 8 * part:8 * part + 8, :], 1.0, None, ADD)
        t_sc = vtt(sc, sc, view(VC[g], [1, 8], [0, 2]), MUL)

    def bcast_rows(dst, part):
        m_ = top[0]
        lt = view(al(1024), [128, 8], [1, 128])
        bi = al(1024)
        t0 = load_small(bi, row(I["b_ada"][0, 1024 * part:1024 * part + 1024], 1024), barrier())
        t1 = vcopy(lt, view(silc, [2, 8], [0, 128]))
        for hf in range(2):
            s, wv, tok = chunk(I["w_ada"], 0, 8, part * 1024 + 512 * hf, 512)
            b, pv, bw = bank()
            for k in range(8):
                t = mm(pv, lt[:, k, :], wv[:, k, :], k == 0, k == 7, bw + [tok, t1] if k == 0 else (), k == 7)
            slot_free[s] = (t,)
            t = vtt(dst[:, 512 * hf:512 * hf + 512], pv, bi[:, 512 * hf:512 * hf + 512], ADD, [t, t0])
            rel(b, t)
        barrier()
        top[0] = m_
        return t

    def rms_scales(o, x, scr, w=()):
        t = act(scr, x, ACT.Square, w=w, acc=o)
        return rstd(o, o, 1024, 1e-6, [t])

    def norm_mod_fm(xs, cols, sc, sh, col0, scr, w=()):
        xn = []
        for i, x in enumerate(xs):
            r = small[:, i:i + 1]
            t = rms_scales(r, x, scr, w[i] if w else ())
            t = vts(x, x, r, None, MUL, w=[t])
            xn.append(x)

        def ev(f, o, i_, tt):
            return act(o, i_, ACT.Identity, scale=sc[:, f, cols:cols + 1], bias=sh[:, f, cols:cols + 1], w=[tt, t_sc])
        return to_fm(xn, 8, lambda f: hT[:, f, col0:col0 + 128 * len(xs)], ev, [t])

    mk = top[0]
    xs_all = al(6 * 1024)
    scr = al(1024)
    tk = []
    for i in range(4):
        tk.append([load_small(xs_all[:, 1024 * i:1024 * i + 1024], I["x"][0, 128 * i:128 * i + 128, :])])
    for i in range(2):
        tk.append([load_small(xs_all[:, 1024 * (4 + i):1024 * (5 + i)], I["ctx"][0, 128 * i:128 * i + 128, :])])
    tiles = [xs_all[:, 1024 * i:1024 * i + 1024] for i in range(6)]
    norm_mod_fm(tiles[0:4], 0, sc1, mod[:, 0:8, :], 0, scr, tk[0:4])
    norm_mod_fm(tiles[4:6], 1, sc1, mod[:, 0:8, :], 512, scr, tk[4:6])
    barrier()
    top[0] = mk

    CVO, MLO, GO = 1920, 2944, 5008
    z = view(al(4 * 8 * 94), [8 * 94, 4], [94, 8], [1, 94])
    cga = view(al(4 * 512), [512, 4], [1, 512])
    t_z = vset(z, 0.0)

    def ev_a(m, g, pv, t):
        return scopy(cga[:, m, :], pv, [t])

    def ev_g(m, g, pv, t):
        t = act(sq4[:, m, :], pv, ACT.Sigmoid, w=[t])
        t1 = vtt(z[:, m, :, 15:79], view(cga[:, m, :], [64, 8], [1, 64]), view(sq4[:, m, :], [64, 8], [1, 64]), MUL, [t])
        return t1
    sq4 = view(al(4 * 512), [512, 4], [1, 512])
    gemm_fm(I["w_in"], CVO, 512, 8, hT, lambda m: [(0, 512)], ev_a)
    gemm_fm(I["w_in"], CVO + 512, 512, 8, hT, lambda m: [(0, 512)], ev_g)
    cacc = view(al(4 * 512), [512, 4], [1, 512])
    for f in range(4):
        o = view(cacc[:, f, :], [64, 8], [1, 64])
        cd = VC["cdw"][:, 31 * f:31 * f + 31]
        vts(o, z[:, f, :, 0:64], cd[:, 0:1], VC["cdb"][:, f:f + 1], MUL, ADD)
        for k in range(1, 31):
            t = stt(o, z[:, f, :, k:k + 64], cd[:, k:k + 1], o, MUL, ADD)
    b, pv, bw = bank()
    for f in range(4):
        t = mm(pv, C["ones"], cacc[:, f, :], f == 0, f == 3, bw + [t] if f == 0 else (), f == 3)
    mean = cga[:, 0, :]
    t = scopy(mean, pv, [t], scale=1.0 / 512)
    rel(b, t)
    t = vtt(cacc, cacc, rep(mean, 4, 512), SUB, [t])
    t = vtt(sq4, cacc, cacc, MUL)
    b, pv, bw = bank()
    for f in range(4):
        t = mm(pv, C["ones"], sq4[:, f, :], f == 0, f == 3, bw + [t] if f == 0 else (), f == 3)
    rs = cga[:, 1, :]
    t = vts(rs, pv, 1.0 / 512, 1e-5, MUL, ADD, w=[t])
    rel(b, t)
    t = act(rs, rs, ACT.Sqrt, w=[t])
    t = recip(rs, rs, [t])
    t = vtt(cacc, cacc, rep(rs, 4, 512), MUL)
    for f in range(4):
        act(ybT[:, f, :], cacc[:, f, :], ACT.Silu, scale=VC["clw"][:, f:f + 1], bias=VC["clb"][:, f:f + 1], w=[t])
    barrier()
    top[0] = mk

    q = view(al(4 * 512), [512, 4], [1, 512])
    kx = view(al(4 * 768), [768, 4], [1, 768])
    v1 = view(al(6 * 4 * 129), [4 * 129, 6], [129, 4], [1, 129])
    og = view(al(4 * 512), [512, 4], [1, 512])
    gates = view(al(6 * 16), [16, 6], [1, 16])
    gb = al(16)
    t_gb = load_small(gb, row(I["mlgb"], 16))
    vset(v1, 1.0)
    KT = [512, 640, 0, 128, 256, 384]
    gemm_fm(I["w_in"], MLO, 512, 8, hT, lambda m: [(0, 512)], lambda m, g, pv, t: scopy(q[:, m, :], pv, [t]))
    gemm_fm(I["w_in"], MLO + 512, 512, 8, hT, lambda m: SEGS,
            lambda m, g, pv, t: scopy(kx[:, m, SEGS[g][0]:SEGS[g][0] + SEGS[g][1]], pv[:, 0:SEGS[g][1]], [t],
                                      scale=128 ** -0.5))
    gemm_tm(I["w_in"], MLO + 1024, 512, 8, hT, KT,
            lambda c, i, pv, t, n: vcopy(v1[:, i, :, 0:128], view(pv, [128, 4], [1, 128]), [t]))
    gemm_tm(I["w_in"], MLO + 1536, 512, 8, hT, KT[2:],
            lambda c, i, pv, t, n: act(og[:, i, :], pv, ACT.Sigmoid, w=[t]))
    gemm_tm(I["w_in"], MLO + 2048, 16, 8, hT, KT,
            lambda c, i, pv, t, n: vtt(gates[:, i, :], pv[:, 0:16], gb, ADD, [t, t_gb]))
    g4 = view(gates, [16, 6], [8, 2], [1, 8])
    IG = view(al(48), [8, 6], [4, 2], [1, 4])
    LF = view(al(48), [8, 6], [4, 2], [1, 4])
    tA = view(al(48), [8, 6], [4, 2], [1, 4])
    vcopy(IG, g4[:, :, :, 0:4])
    vcopy(LF, g4[:, :, :, 4:8])
    t = vcopy(tA, LF)
    act(tA, tA, ACT.Abs, w=[t])
    act(tA, tA, ACT.Exp, scale=-1.0)
    t = act(tA, tA, ACT.Ln, bias=1.0)
    vts(LF, LF, 0.0, None, MIN, w=[t])
    t_lf = vtt(LF, LF, tA, SUB)
    lfr = al(768)
    igr = al(768)
    cumr = al(768)
    mr = al(768)
    for x in (lfr, igr):
        vset(x, 0.0)
    for d in range(2):
        for X, R in ((LF, lfr), (IG, igr)):
            for half, n in ((0, 4), (4, 2)):
                b, pv, bw = bank()
                for i in range(n):
                    ti = SEQ_[d][half + i]
                    t = mm(pv[32 * d:32 * d + 4, 128 * i:128 * i + 128], X[:, ti, d, :], C["J" if d else "ident"],
                           True, True, bw + [t_lf] if i == 0 else (), i == n - 1)
                t = vcopy(R[32 * d:32 * d + 4, 128 * half:128 * (half + n)], pv[32 * d:32 * d + 4, 0:128 * n], [t])
                rel(b, t)
    rsm = al(768)
    vcopy(view(rsm, [128, 6], [1, 128]), rep(C["rs128"], 6))
    scan(mr[0:64], lfr[0:64], igr[0:64], ADD, MAX)
    scan(cumr[0:64], rsm[0:64], lfr[0:64], MUL, ADD)
    t_R = vtt(cumr[0:64], cumr[0:64], mr[0:64], SUB)
    Rn = al(512)
    t = vset(Rn, 0.0)
    em = view(al(4 * 8), [8, 4], [1, 8])
    id4 = C["ident"]
    cR = view(al(4 * 8), [8, 4], [1, 8])
    vcopy(Rn[0:4, :], cumr[0:4, 256:768])
    b, pv, bw = bank()
    for i in range(4):
        t = mm(pv[:, 4 * i:4 * i + 4], mr[0:4, 256 + 128 * i:384 + 128 * i], id4[0:4, 0:4], True, True,
               bw + [t_R] if i == 0 else (), i == 3)
    t = vcopy(em[:, :, 0:4], view(pv, [4, 4], [1, 4]), [t])
    rel(b, t)
    b, pv, bw = bank()
    for i in range(4):
        ps = 3 - i
        for j, X in enumerate((cumr, mr)):
            t = mm(pv[:, 8 * i + 4 * j:8 * i + 4 * j + 4], X[32:36, 256 + 128 * ps:384 + 128 * ps], id4[32:36, 32:36],
                   True, True, bw + [t_R] if i + j == 0 else (), i == 3 and j == 1)
    t_cR = vcopy(cR, view(pv, [8, 4], [1, 8]), [t])
    rel(b, t_cR)
    b, pv, bw = bank()
    b2_, pv2, bw2 = bank()
    for i in range(4):
        mm(pv[:, 4 * i:4 * i + 4], C["J"], cR[:, i, 4:8], True, True, bw + [t_cR] if i == 0 else ())
        t = mm(pv2[32:36, 128 * i:128 * i + 128], cR[:, i, 0:4], C["J"], True, True, bw2 if i == 0 else (), i == 3)
    t1 = vcopy(em[:, :, 4:8], view(pv, [4, 4], [1, 4]), [t])
    rel(b, t1)
    t_Rn = vcopy(Rn[32:36, :], pv2[32:36, :], [t])
    rel(b2_, t_Rn)
    t_em = act(em, em, ACT.Exp, scale=-1.0, w=[t1])
    bias = view(al(36 * 4), [4, 36], [1, 4])
    pair = {}
    b, pv, bw = bank()
    n_p = 0
    for d in range(2):
        for a in range(2, 6):
            for s_ in range(a + 1):
                T_, S_ = SEQ_[d][a], SEQ_[d][s_]
                pair[d, T_, S_] = n_p
                o = pv[:, 4 * n_p:4 * n_p + 4]
                if s_ == a:
                    terms = [(C["nUI128"] if d == 0 else C["nLI128"], S_)]
                else:
                    terms = [(C["LS128"] if d == 0 else C["US128"], S_)] + [(C["ones"], SEQ_[d][m_]) for m_ in range(s_ + 1, a)]
                for e, (mat, ti) in enumerate(terms):
                    t = mm(o, mat, LF[:, ti, d, :], e == 0, e == len(terms) - 1, bw + [t_lf] if n_p + e == 0 else (),
                           n_p == 35 and e == len(terms) - 1)
                n_p += 1
    for (d, T_, S_), n_ in pair.items():
        tb = vtt(bias[:, n_, :], pv[:, 4 * n_:4 * n_ + 4], IG[:, S_, d, :], ADD, [t])
    rel(b, tb)
    t_bias = tb
    Hm = view(al(4 * 512), [512, 4], [1, 512])
    QK = view(al(6 * 512), [512, 6], [1, 512])
    EE = view(al(2 * 6 * 512), [6 * 512, 2], [512, 6], [1, 512])
    dn = al(16)
    ee_free = [(), ()]
    qk_free = ()
    for h in range(4):
        tq = None
        for s_ in range(6):
            kc = KT[s_]
            b, pv, bw = bank()
            t = mm(pv, kx[:, h, kc:kc + 128], q[:, h, :], True, True, bw, True)
            tq = scopy(QK[:, s_, :], pv, [t] + list(qk_free))
            rel(b, tq)
        for d in range(2):
            E_ = EE[:, d]
            b, pv, bw = bank()
            b2_, pv2, bw2 = bank()
            mm(pv, C[f"sel{d}{h}"][0:64], Rn[0:64], True, True, bw + [t_Rn])
            mm(pv2, C[f"sel{d}{h}"][0:64], Rn[0:64], True, False, bw2)
            t = mm(pv2, C["ident"], rep(C["negGT" if d == 0 else "negLT"], 4), False, True, (), True)
            for (dd, T_, S_), n_ in pair.items():
                if dd != d:
                    continue
                c0 = 128 * (T_ - 2)
                src = (pv2 if S_ == T_ else pv)[:, c0:c0 + 128]
                te = act(E_[:, S_, c0:c0 + 128], src, ACT.Exp, bias=bias[:, n_, h:h + 1],
                         w=[t, t_bias] + list(ee_free[d]))
            rel(b, te)
            rel(b2_, te)
            for S_ in range(6):
                if S_ < 2:
                    lo, hi = 0, 512
                elif d == 0:
                    lo, hi = 128 * (S_ - 2), 512
                else:
                    lo, hi = 0, 128 * (S_ - 1)
                te2 = vtt(E_[:, S_, lo:hi], E_[:, S_, lo:hi], QK[:, S_, lo:hi], MUL, [te, tq])
            qk_free = (te2,)
            for a in range(2, 6):
                T_ = SEQ_[d][a]
                c0 = 128 * (T_ - 2)
                b, pv, bw = bank()
                ks = SEQ_[d][0:a + 1]
                for e, S_ in enumerate(ks):
                    t = mm(pv[:, 0:129], E_[:, S_, c0:c0 + 128], v1[:, S_, h, :], e == 0, e == len(ks) - 1,
                           bw + [te2] if e == 0 else (), e == len(ks) - 1)
                vts(dn[:, 0:1], pv[:, 128:129], -1.0, em[:, T_ - 2, 4 * d + h:4 * d + h + 1], MUL, MAX, w=[t, t_em])
                vtt(dn[:, 0:1], dn[:, 0:1], pv[:, 128:129], MAX)
                recip(dn[:, 1:2], dn[:, 0:1])
                ho = Hm[:, T_ - 2, 128 * h:128 * h + 128]
                if d == 0:
                    tv = vts(ho, pv[:, 0:128], dn[:, 1:2], None, MUL)
                else:
                    tv = stt(ho, pv[:, 0:128], dn[:, 1:2], ho, MUL, ADD)
                rel(b, tv)
            ee_free[d] = (t,)
    barrier()
    nwr = al(512)
    t_nw = load_small(nwr, row(I["ml_nw"][0, :], 512))
    sqs = EE[:, 0, 0, :]
    for i in range(4):
        x_ = Hm[:, i, :]
        group_norm(x_, 4, 128, 1e-5, small, sqs, True)
        vtt(x_, x_, nwr, MUL, [t_nw])
        t = vtt(x_, x_, og[:, i, :], MUL)
    to_fm([Hm[:, i, :] for i in range(4)], 4, lambda f: ycT[:, f, :], None, [t])
    barrier()
    top[0] = mk

    yaT = view(al(4 * 512), [512, 4], [1, 512])
    mk = top[0]
    rT = view(al(4 * 512), [512, 4], [1, 512])
    kT = view(al(4 * TW), [TW, 4], [1, TW])
    kkT = view(al(4 * TW), [TW, 4], [1, TW])
    lo3 = view(al(3 * TW), [TW, 3], [1, TW])
    vt = view(al(6 * 512), [512, 6], [1, 512])
    bonus = view(al(32), [8, 4], [1, 8])
    w2s = al(512)
    a2s = al(512)
    cm = al(15)
    kam = al(4)
    t_w2 = load_small(w2s, I["rw_w2"].rearrange("l d k c -> (l d k) c"))
    t_a2 = load_small(a2s, I["rw_a2"].rearrange("l d k c -> (l d k) c"))
    mk2 = top[0]
    ub = view(al(2 * 772), [772, 2], [1, 772])
    vv = al(TW)
    sqk = al(TW)
    t_ub = vset(ub, 0.0)
    vts(cm, VC["mup"], -1.0, 1.0, MUL, ADD)
    vtt(cm, cm, VC["mun"], SUB)
    t_km = vts(kam, VC["ka"], -1.0, 1.0, MUL, ADD)
    ub_free = [(t_ub,), (t_ub,)]
    vv_free = [()]

    def shift(m, o, n):
        u = ub[:, m % 2, :]
        vts(o, u[:, 1:1 + n], cm[:, m:m + 1], None, MUL)
        stt(o, u[:, 0:n], VC["mup"][:, m:m + 1], o, MUL, ADD)
        t = stt(o, u[:, 2:2 + n], VC["mun"][:, m:m + 1], o, MUL, ADD)
        ub_free[m % 2] = (t,)
        return t

    def ev_u(m, g, pv, t):
        n = 512 if g == 0 else 256
        o = ub[:, m % 2, 1:513] if g == 0 else ub[:, m % 2, 515:771]
        tc = scopy(o, pv[:, 0:n], [t] + list(ub_free[m % 2]))
        if m < 4:
            V.wait([tc])
            shift(m, rT[:, m, :], 512)
        elif g == 1:
            V.wait([tc])
            if m < 8:
                f = m - 4
                o = kT[:, f, :]
                shift(m, o, TW)
                kr = kkT[:, f, :]
                vts(kr, o, VC["kk"][:, f:f + 1], None, MUL)
                tk_ = vtt(sqk, kr, kr, MUL)
                b1, p1, w1 = bank()
                b2, p2, w2 = bank()
                mm(p1, C["blk"], sqk[:, 0:512], True, True, w1 + [tk_])
                tm = mm(p2[:, 0:TW - 512], C["blk"], sqk[:, 512:TW], True, True, w2, True)
                act(sqk[:, 0:512], p1, ACT.Sqrt, w=[tm])
                ta = act(sqk[:, 512:TW], p2[:, 0:TW - 512], ACT.Sqrt)
                rel(b1, ta)
                rel(b2, ta)
                vts(sqk, sqk, 1e-12, None, MAX, w=[ta])
                recip(sqk, sqk)
                vtt(kr, kr, sqk, MUL)
            elif m < 12:
                f = m - 8
                tv = V.op(lambda: nc.vector.memset(vv[:, 0:1], 0.0), vv_free[0])
                tv = shift(m, vv, TW)
                for q0, n in ((0, 4), (4, 2)):
                    b1, p1, w1 = bank()
                    for i in range(n):
                        a = TO[q0 + i]
                        tm = tr(p1[:, 128 * i:128 * i + 128], vv[:, a:a + 128], w1 + [tv] if i == 0 else (), i == n - 1)
                    ta = scopy(vt[:, q0:q0 + n, 128 * f:128 * f + 128], view(p1, [128, n], [1, 128]), [tm])
                    rel(b1, ta)
                vv_free[0] = (tm,)
            else:
                o = lo3[:, m - 12, :]
                ts_ = shift(m, o, TW)
                if m == 12:
                    act(o, o, ACT.Tanh, w=[ts_])
                if m == 14:
                    act(o, o, ACT.Sigmoid, w=[ts_])
        return tc
    gemm_fm(I["w_in"], 0, 1920, 8, hT, lambda m: SEGS[0:1] if m < 4 else SEGS, ev_u)
    b, pv, bw = bank()
    for f in range(4):
        rk = ub[:, f % 2, 0:512]
        vtt(rk, rT[:, f, :], kT[:, f, 0:512], MUL, ub_free[f % 2])
        tv = vts(rk, rk, VC["rk"][:, f:f + 1], None, MUL)
        for i in range(4):
            t = mm(pv[:, 8 * i + 2 * f:8 * i + 2 * f + 2], rk[:, 128 * i:128 * i + 128], C["b2"][:, 0:2], True, True,
                   bw + [tv] if i == 0 else (), i == 3)
        ub_free[f % 2] = (t,)
    t = vcopy(bonus, view(pv, [8, 4], [1, 8]), [t])
    rel(b, t)
    barrier()
    top[0] = mk2

    Ya = view(al(4 * 512), [512, 4], [1, 512])
    Sg, La, Ep, En, Aa = (view(al(512), [128, 4], [1, 128]) for _ in range(5))
    KKp, Rp, Bn, Kn = (view(al(512), [128, 4], [1, 128]) for _ in range(4))
    Bt, Kt_ = al(512), al(512)
    spare = iter(ring[:, 512 * n:512 * n + 512] for n in range(16))
    AkT, BbT, BkT, TTm, Tm, ATm, Xm = ([view(next(spare), [128, 4], [1, 128]) for _ in range(2)] for _ in range(7))
    St = [al(512) for _ in range(2)]
    PCM = view(al(512), [128, 4], [1, 128])
    Xs, Us = next(spare), next(spare)
    rsw = al(512)
    vcopy(view(rsw, [128, 4], [1, 128]), rep(C["rs64"], 4))
    for d in range(2):
        vset(St[0], 0.0)
        cur = 0
        for pos in range(6):
            ti = SEQ_[d][pos]
            a0_ = TO[ti]
            lat = ti >= 2
            barrier()
            b, pv, bw = bank()
            b2, pv2, bw2 = bank()
            for f in range(4):
                mm(pv[:, 128 * f:128 * f + 128], w2s[64 * d:64 * d + 64, 128 * f:128 * f + 128],
                   lo3[64 * d:64 * d + 64, 0, a0_:a0_ + 128], True, True, bw + [t_w2] if f == 0 else ())
            for f in range(4):
                t = mm(pv2[:, 128 * f:128 * f + 128], a2s[64 * d:64 * d + 64, 128 * f:128 * f + 128],
                       lo3[64 * d:64 * d + 64, 1, a0_:a0_ + 128], True, True, bw2 + [t_a2] if f == 0 else (), f == 3)
            for f in range(4):
                act(Sg[:, f, :], pv[:, 128 * f:128 * f + 128], ACT.Sigmoid, bias=VC["w0"][:, 4 * d + f:4 * d + f + 1], w=[t])
            for f in range(4):
                t = act(Aa[:, f, :], pv2[:, 128 * f:128 * f + 128], ACT.Sigmoid, bias=VC["a0"][:, 4 * d + f:4 * d + f + 1])
            rel(b, t)
            rel(b2, t)
            c8 = lambda x: view(x[:, 0, 0:1], [64, 8], [1, 64])
            last = view(La[:, 0, 63:64], [64, 8], [0, 64])
            flat = lambda x: view(x[:, 0, 0:1], [1, 512])
            tl = scan(flat(La), rsw, flat(Sg), MUL, ADD, [t])
            if d == 1:
                vtt(c8(Ep), last, c8(La), SUB)
                tl = vtt(c8(La), c8(Ep), c8(Sg), ADD)
            te = act(flat(Ep), flat(La), ACT.Exp, scale=-KAP, w=[tl])
            te = act(flat(En), flat(La), ACT.Exp, scale=KAP)
            tl = vtt(flat(La), flat(La), flat(Sg), SUB, [te])
            te = act(flat(La), flat(La), ACT.Exp, scale=-KAP, w=[tl])
            ksl, kks = kT[:, :, a0_:a0_ + 128], kkT[:, :, a0_:a0_ + 128]
            t_kk = vtt(KKp, kks, La, MUL, [te])
            if lat:
                vtt(Rp, rT[:, :, a0_:a0_ + 128], Ep, MUL)
            vtt(Bn, kks, Aa, MUL)
            stt(Bn, Bn, -1.0, En, MUL, MUL)
            for f in range(4):
                vts(Aa[:, f, :], Aa[:, f, :], VC["ka"][:, f:f + 1], kam[:, f:f + 1], MUL, ADD)
            vtt(Kn, ksl, Aa, MUL)
            t_k = vtt(Kn, Kn, En, MUL)
            for src, dst in ((Bn, Bt), (Kn, Kt_)):
                b, pv, bw = bank()
                for f in range(4):
                    t = tr(pv[:, 128 * f:128 * f + 128], src[:, f, :], bw + [t_k] if f == 0 else (), f == 3)
                t_tok = scopy(dst, pv, [t])
                rel(b, t_tok)
            m0, n0 = (C["M0"], C["N0"]) if d == 0 else (C["N0"], C["M0"])
            strict, incl = (C["US"], C["UI"]) if d == 0 else (C["LS"], C["LI"])
            groups = []
            for g in range(2):
                hp = slice(64 * g, 64 * g + 64)

                def outer(l, r, w=()):
                    b, pv, bw = bank()
                    for i in range(4):
                        t = mm(pv[:, 128 * i:128 * i + 128], l[hp, i, :], r[hp, i, :], True, True,
                               bw + list(w) if i == 0 else (), i == 3)
                    return b, view(pv, [128, 4], [1, 128]), t
                vcopy(Tm[g], rep(C["ident"], 4))
                vcopy(TTm[g], rep(C["ident"], 4))
                b, pm, t = outer(KKp, Bn, [t_k])
                t1 = cpred(Tm[g], rep(m0, 4).bitcast(U32), pm, [t])
                rel(b, t1)
                b, pm, t = outer(Bn, KKp)
                t1 = cpred(TTm[g], rep(n0, 4).bitcast(U32), pm, [t])
                t2 = scopy(ATm[g], pm, [t1])
                rel(b, t2)
                groups.append((Tm[g], TTm[g], ATm[g], [t1, t2], Xm[g]))
                b, pm, t = outer(Kn, KKp)
                t1 = vtt(AkT[g], pm, rep(strict, 4), MUL, [t])
                rel(b, t1)
                if lat:
                    b, pm, t = outer(Bn, Rp)
                    t1 = vtt(BbT[g], pm, rep(incl, 4), MUL, [t])
                    rel(b, t1)
                    b, pm, t = outer(Kn, Rp)
                    t1 = vtt(BkT[g], pm, rep(incl, 4), MUL, [t])
                    rel(b, t1)
                t_mat = t1
            tinv = invert(groups, d == 0)
            w_inv = [x for ts_ in tinv for x in ts_] + [t_mat, t_tok]
            for p in ((0, 1) if d == 0 else (1, 0)):
                r_ = slice(64 * p, 64 * p + 64)
                edge = 64 * p + 63 if d == 0 else 64 * p
                S0, S1 = St[cur], St[1 - cur]
                b, pv, bw = bank()
                for i in range(4):
                    o = pv[r_, 128 * i:128 * i + 128]
                    mm(o, KKp[:, i, r_], S0[:, 128 * i:128 * i + 128], True, False,
                       bw + w_inv + [(V, V.n)] if i == 0 else ())
                    for g in range(2):
                        c_ = 128 * i + 64 * g
                        t = mm(pv[r_, c_:c_ + 64], AkT[g][r_, i, r_], vt[r_, ti, c_:c_ + 64], False, g == 1,
                               (), i == 3 and g == 1)
                t = vcopy(Xs[r_, :], pv[r_, :], [t])
                rel(b, t)
                b, pv, bw = bank()
                for i in range(4):
                    for g in range(2):
                        c_ = 128 * i + 64 * g
                        t = mm(pv[r_, c_:c_ + 64], TTm[g][r_, i, r_], Xs[r_, c_:c_ + 64], True, True,
                               bw + [t] if i + g == 0 else (), i == 3 and g == 1)
                tu = scopy(Us[r_, :], pv[r_, :], [t])
                rel(b, tu)
                b, pv, bw = bank()
                for i in range(4):
                    f_ = slice(128 * i, 128 * i + 128)
                    mm(pv[:, f_], Bt[r_, f_], Us[r_, f_], True, False, bw + [tu] if i == 0 else ())
                    t = mm(pv[:, f_], Kt_[r_, f_], vt[r_, ti, f_], False, True, (), i == 3)
                vtt(PCM, view(Ep[:, 0, edge:edge + 1], [128, 4], [0, 128]), rep(C["blk"], 4), MUL)
                vtt(S1, S0, pv, ADD, [t])
                ts_ = vtt(view(S1, [128, 4], [1, 128]), view(S1, [128, 4], [1, 128]), PCM, MUL)
                rel(b, ts_)
                if lat:
                    b, pv, bw = bank()
                    for i in range(4):
                        mm(pv[r_, 128 * i:128 * i + 128], Rp[:, i, r_], S0[:, 128 * i:128 * i + 128], True, False,
                           bw if i == 0 else ())
                        for g in range(2):
                            c_ = 128 * i + 64 * g
                            mm(pv[r_, c_:c_ + 64], BbT[g][r_, i, r_], Us[r_, c_:c_ + 64], False, False)
                            t = mm(pv[r_, c_:c_ + 64], BkT[g][r_, i, r_], vt[r_, ti, c_:c_ + 64], False, g == 1,
                                   (), i == 3 and g == 1)
                    y_ = Ya[r_, ti - 2, :]
                    t = vcopy(y_, pv[r_, :], [t]) if d == 0 else vtt(y_, y_, pv[r_, :], ADD, [t])
                    rel(b, t)
                cur = 1 - cur
    barrier()
    g2s, lw_, lb_ = KKp, Bt, Kt_
    lw_, lb_ = Bt, Kt_
    g2f = view(KKp[:, 0, 0:1], [1, 512])
    t_l = [load_small(g2f, I["rw_g2"][0]), load_small(lw_, row(I["rw_lnw"][0, :], 512)),
           load_small(lb_, row(I["rw_lnb"][0, :], 512))]
    bv = view(Rp[:, 0, 0:1], [1, 512])
    for i in range(4):
        y_ = Ya[:, i, :]
        group_norm(y_, 8, 64, 64e-5, small, Xs, True)
        vtt(y_, y_, lw_, MUL, t_l)
        vtt(y_, y_, lb_, ADD)
        vtt(view(bv, [64, 8], [1, 64]), view(vt[:, 2 + i, :], [64, 8], [1, 64]), view(bonus[:, i, :], [1, 8], [0, 64]), MUL)
        vtt(y_, y_, bv, ADD)
        b, pv, bw = bank()
        t = mm(pv, lo3[:, 2, 128 * i:128 * i + 128], g2f, True, True, bw + t_l, True)
        t = vtt(y_, y_, pv, MUL, [t])
        rel(b, t)
    to_fm([Ya[:, i, :] for i in range(4)], 4, lambda f: yaT[:, f, :], None, [t])
    ends = barrier()
    for n in range(NSLOT):
        slot_free[n] = tuple(ends)
    top[0] = mk

    x1 = view(al(4 * 1024), [1024, 4], [1, 1024])
    mk3 = top[0]
    mrow = al(1024)
    bcast_rows(mrow, 2)
    mg = view(al(4 * 1024), [1024, 4], [1, 1024])
    sg = view(al(4 * 512), [512, 4], [1, 512])
    tx = [load_small(x1[:, i, :], I["x"][0, 128 * i:128 * i + 128, :]) for i in range(4)]
    for br, (y_, pw) in enumerate(((yaT, "p_a"), (ybT, "p_b"), (ycT, "p_c"))):
        for hf in range(2):
            gemm_tm(I["w_in"], GO + 1024 * br + 512 * hf, 512, 8, hT, W512,
                    lambda c, i, pv, t, n: act(sg[:, i, :], pv, ACT.Sigmoid, w=[t, (V, V.n)]))

            def ev_m(c, i, pv, t, n, br=br, hf=hf):
                o = mg[:, i, 512 * hf:512 * hf + 512]
                if br == 0:
                    return vtt(o, sg[:, i, :], pv, MUL, [t, (S, S.n)])
                vtt(sg[:, i, :], sg[:, i, :], pv, MUL, [t, (S, S.n)])
                return vtt(o, o, sg[:, i, :], ADD)
            gemm_tm(I[pw], 512 * hf, 512, 4, y_, W512, ev_m)
    mT = hT[:, :, 0:512]
    t = to_fm([mg[:, i, :] for i in range(4)], 8, lambda f: hT[:, f, 0:512], None, [(V, V.n), (P, P.n)])

    def ev_o(c, i, pv, t, n):
        o = mg[:, i, c:c + 512]
        vtt(o, pv, mrow[:, c:c + 512], MUL, [t])
        return vtt(x1[:, i, c:c + 512], x1[:, i, c:c + 512], o, ADD, tx)
    gemm_tm(I["w_out"], 0, 1024, 8, hT, W512, ev_o, [t])
    barrier()
    xc = view(al(4 * 1024), [1024, 4], [1, 1024])
    scr = al(1024)
    t = vcopy(xc, x1)
    norm_mod_fm([xc[:, i, :] for i in range(4)], 0, sc2, mod[:, 24:32, :], 0, scr, [[t]] * 4)
    barrier()
    top[0] = mk3
    mrow = al(1024)
    bcast_rows(mrow, 5)
    hid = view(al(32 * 512), [512, 32], [1, 512])
    tmp = al(1024)
    tmp_i = [0]

    def ev_1(m, g, pv, t):
        o = tmp[:, 512 * (m % 2):512 * (m % 2) + 512]
        t1 = act(o, pv, ACT.Relu, w=[t, (V, V.n)])
        return vtt(hid[:, m, :], o, o, MUL, [t1])
    gemm_fm(I["w_mlp1"], 0, 4096, 8, hT, lambda m: [(0, 512)], ev_1)

    def ev_2(c, i, pv, t, n):
        o = tmp[:, 512 * (i % 2):512 * (i % 2) + 512]
        vtt(o, pv, mrow[:, c:c + 512], MUL, [t])
        return vtt(x1[:, i, c:c + 512], x1[:, i, c:c + 512], o, ADD)
    gemm_tm(I["w_mlp2"], 0, 1024, 32, hid, W512, ev_2, [(V, V.n)])
    barrier()
    top[0] = mk3
    gfr = al(1024)
    scr = al(1024)
    t_g = load_small(gfr, row(I["g_final"], 1024))
    for i in range(4):
        t = rms_scales(small[:, i:i + 1], x1[:, i, :], scr, [(V, V.n)])
        stt(x1[:, i, :], x1[:, i, :], small[:, i:i + 1], gfr, MUL, MUL, [t, t_g])
    barrier()

    top[0] = mk_hT
    barrier()
    hX = view(al(4 * 1024), [1024, 4], [1, 1024])
    vcopy(hX, x1)
    barrier()
    hh = view(al(8 * 512), [512, 8], [1, 512])
    small = al(256)
    cosT, sinT = al(512), al(512)
    base = top[0]
    ALPHA = 4.0 ** 0.25
    RP = slice(64, 96)

    pos_i = al(512).bitcast(I32)
    ang, kk_, wk = al(512), al(512), al(512)
    t = load_small(pos_i[RP, :], bass.AP(I["positions_2"].tensor, 0, [[0, 32], [1, 512]]))
    vcopy(ang[RP, :], pos_i[RP, :], [t])
    vts(ang[RP, :], ang[RP, :], C["rope"][RP, 0:1], None, MUL)
    MAGIC = 12582912.0
    C1 = 6.28125
    C2 = float(np.float32(2 * np.pi - C1))
    C3 = float(2 * np.pi - C1 - np.float64(np.float32(2 * np.pi - C1)))
    for dst, ph in ((sinT, 0.0), (cosT, 0.25)):
        k_, w_ = kk_[RP, :], wk[RP, :]
        vts(k_, ang[RP, :], 1.0 / (2 * np.pi), ph, MUL, ADD)
        vts(k_, k_, MAGIC, None, ADD)
        vts(k_, k_, MAGIC, None, SUB)
        stt(w_, k_, -C1, ang[RP, :], MUL, ADD, [(S, S.n)])
        stt(w_, k_, -C2, w_, MUL, ADD)
        stt(w_, k_, -C3, w_, MUL, ADD)
        if ph:
            vts(w_, w_, float(np.pi / 2), None, ADD)
        vts(w_, w_, 3.1415925, -3.1415925, MIN, MAX)
        act(dst[RP, :], w_, ACT.Sin, w=[(V, V.n)])
    vts(sinT[RP, :], sinT[RP, :], C["rope"][RP, 1:2], None, MUL, w=[(S, S.n)])
    barrier()
    top[0] = base

    def hT_from_x():
        t = to_fm([hX[:, i, :] for i in range(4)], 8, lambda f: hh[:, f, :], None, [(V, V.n), (P, P.n)])
        P.wait([t])
        return t

    def layer_norm_all(l, j):
        m_ = top[0]
        gr, br_ = al(1024), al(1024)
        e = barrier()
        tg = [load_small(gr, row(I["ln_g_2"][l, j, :], 1024)), load_small(br_, row(I["ln_b_2"][l, j, :], 1024))]
        for i in range(4):
            x_ = hX[:, i, :]
            layer_norm_tile(x_, x_, 1024, 1e-5, small)
            vtt(x_, x_, gr, MUL, tg)
            vtt(x_, x_, br_, ADD)
        t = hT_from_x()
        barrier()
        top[0] = m_
        return t

    def ffn(l, wi, wo, j):
        m_ = top[0]
        hid = view(al(22 * 512), [512, 22], [1, 512])
        tmp = al(1024)
        Wi, Wo = I[wi][l], I[wo][l]
        for ch in range(11):
            s, sl, tok = wload([
                (lambda x: view(x, [512, 8], [1, 256]), Wi[:, 256 * ch:256 * ch + 256].rearrange("(k p) c -> p k c", p=128)),
                (lambda x: view(x[:, 256:512], [512, 8], [1, 256]),
                 Wi[:, 2816 + 256 * ch:2816 + 256 * ch + 256].rearrange("(k p) c -> p k c", p=128))])
            wv = view(sl, [512, 8], [1, 512])
            for m in range(2):
                b, pv, bw = bank()
                b2, pv2, bw2 = bank()
                for k in range(8):
                    mm(pv, wv[:, k, 128 * m:128 * m + 128], hh[:, k, :], k == 0, k == 7, bw + [tok] if k == 0 else ())
                for k in range(8):
                    t = mm(pv2, wv[:, k, 256 + 128 * m:384 + 128 * m], hh[:, k, :], k == 0, k == 7,
                           bw2 if k == 0 else (), k == 7)
                slot_free[s] = (t,)
                o = tmp[:, 512 * m:512 * m + 512]
                t1 = act(o, pv, ACT.Silu, w=[t, (V, V.n)])
                rel(b, t1)
                t2 = vtt(hid[:, 2 * ch + m, :], o, pv2, MUL, [t1])
                rel(b2, t2)

        def ev(c, i, pv, t, n):
            o = tmp[:, 512 * (i % 2):512 * (i % 2) + 512]
            t1 = act(o, pv, ACT.Copy, scale=0.5, w=[t, (V, V.n)])
            x_ = hX[:, i, c:c + 512]
            V.wait([t1])
            stt(x_, x_, ALPHA, o, MUL, ADD)
            return t1
        gemm_tm(Wo, 0, 1024, 22, hid, W512, ev, [(V, V.n)])
        barrier()
        top[0] = m_
        layer_norm_all(l, j)

    def mixer(l):
        m0_ = top[0]
        Wm = I["mix_w_in_2"][l]
        catT = view(al(8 * 512), [512, 8], [1, 512])
        m1_ = top[0]
        qk = view(al(8 * 512), [512, 8], [1, 512])
        vtok = view(al(4 * 512), [512, 4], [1, 512])
        gz = view(al(4 * 512), [512, 4], [1, 512])
        gab = view(al(4 * 16), [16, 4], [1, 16])
        ktok = view(al(4 * 512), [512, 4], [1, 512])
        m2_ = top[0]
        ub = view(al(2 * 516), [516, 2], [1, 516])
        cv = view(al(2 * 512), [512, 2], [1, 512])
        sq_, rn = al(512), al(512)
        t0 = vset(ub, 0.0)
        ubf = [(t0,), (t0,)]
        cvf = [(), ()]
        cw = VC[f"gcw{l}"]

        def ev_c(m, g, pv, t):
            u = ub[:, m % 2, :]
            tc = scopy(u[:, 3:515], pv, [t] + list(ubf[m % 2]))
            o = cv[:, m % 2, :]
            vts(o, u[:, 0:512], cw[:, 4 * m:4 * m + 1], None, MUL, w=[tc] + list(cvf[m % 2]))
            for k in range(1, 4):
                tv = stt(o, u[:, k:k + 512], cw[:, 4 * m + k:4 * m + k + 1], o, MUL, ADD)
            ubf[m % 2] = (tv,)
            if m < 8:
                dst = qk[:, m, :]
                ta = act(dst, o, ACT.Silu, w=[tv])
                cvf[m % 2] = (ta,)
                tv = vtt(sq_, dst, dst, MUL, [ta])
                b, p1, bw = bank()
                tm = mm(p1, C["blk"], sq_, True, True, bw + [tv], True)
                ts_ = vts(rn, p1, 1e-6, None, ADD, w=[tm])
                rel(b, ts_)
                ta = act(rn, rn, ACT.Sqrt, w=[ts_])
                recip(rn, rn, [ta])
                if m < 4:
                    stt(dst, dst, 0.125, rn, MUL, MUL)
                else:
                    vtt(dst, dst, rn, MUL)
            else:
                ta = act(o, o, ACT.Silu, w=[tv])
                b, p1, bw = bank()
                for i in range(4):
                    tm = tr(p1[:, 128 * i:128 * i + 128], o[:, 128 * i:128 * i + 128], bw + [ta] if i == 0 else (), i == 3)
                ta = scopy(vtok[:, :, 128 * (m - 8):128 * (m - 8) + 128], view(p1, [128, 4], [1, 128]), [tm])
                rel(b, ta)
                cvf[m % 2] = (tm,)
            return tc
        gemm_fm(Wm, 0, 1536, 8, hh, lambda m: [(0, 512)], ev_c)
        gemm_tm(Wm, 1536, 512, 8, hh, W512, lambda c, i, pv, t, n: act(gz[:, i, :], pv, ACT.Silu, w=[t]))
        gemm_tm(Wm, 2048, 16, 8, hh, W512, lambda c, i, pv, t, n: vcopy(gab[:, i, :], pv[:, 0:16], [t]))
        barrier()
        top[0] = m2_
        al_, dtb = al(8), al(8)
        gg = view(al(32), [8, 4], [1, 8])
        ng = view(al(32), [8, 4], [1, 8])
        be = view(al(32), [8, 4], [1, 8])
        t8 = view(al(32), [8, 4], [1, 8])
        nbe = view(al(32), [8, 4], [1, 8])
        kde = view(al(32), [8, 4], [1, 8])
        egc = view(al(32), [8, 4], [1, 8])
        tl = [load_small(al_, row(I["gdn_a_log_2"][l, :], 8)), load_small(dtb, row(I["gdn_dt_bias_2"][l, :], 8))]
        ta = act(al_, al_, ACT.Exp, w=tl)
        vtt(gg, gab[:, :, 0:8], view(dtb, [0, 4], [1, 8]), ADD, tl)
        t = vcopy(t8, gg)
        act(t8, t8, ACT.Abs, w=[t])
        act(t8, t8, ACT.Exp, scale=-1.0)
        ta2 = act(t8, t8, ACT.Ln, bias=1.0)
        vts(gg, gg, 0.0, None, MAX)
        vtt(gg, gg, t8, ADD, [ta2])
        stt(gg, gg, -1.0, view(al_, [0, 4], [1, 8]), MUL, MUL, [ta])
        t = vts(ng, gg, -1.0, None, MUL)
        t = act(be, gab[:, :, 8:16], ACT.Sigmoid, w=[t])
        b, pv, bw = bank()
        mm(pv[:, 0:32], C["UI"], view(gg, [1, 32]), True, True, bw + [(V, V.n)])
        t = mm(pv[:, 32:64], C["blk"], view(gg, [1, 32]), True, True, (), True)
        act(view(egc, [1, 32]), pv[:, 0:32], ACT.Exp, w=[t])
        tg = scopy(view(t8, [1, 32]), pv[:, 0:32])
        tg = vtt(view(kde, [1, 32]), pv[:, 32:64], view(t8, [1, 32]), SUB, [tg])
        rel(b, tg)
        tg = act(kde, kde, ACT.Exp, w=[tg])
        stt(nbe, be, -1.0, egc, MUL, MUL, [tg])
        nb_ = view(al(32), [8, 4], [1, 8])
        vts(nb_, be, -1.0, None, MUL)
        egl = view(al(64), [8, 8], [1, 8])
        b, pv, bw = bank()
        for c_ in range(8):
            t = mm(pv[:, 8 * c_:8 * c_ + 8], C[f"half{c_ % 2}"], gg[:, c_ // 2, :], True, True,
                   bw + [(V, V.n)] if c_ == 0 else (), c_ == 7)
        t_egl = act(view(egl, [1, 64]), pv[:, 0:64], ACT.Exp, w=[t])
        rel(b, t_egl)
        for i in range(4):
            b, pv, bw = bank()
            for f in range(4):
                t = tr(pv[:, 128 * f:128 * f + 128], qk[:, 4 + f, 128 * i:128 * i + 128], bw if f == 0 else (), f == 3)
            tk_ = vtt(view(ktok[:, i, :], [64, 8], [1, 64]), view(pv, [64, 8], [1, 64]), view(kde[:, i, :], [1, 8], [0, 64]),
                      MUL, [t, tg])
            rel(b, tk_)
            vtt(view(vtok[:, i, :], [64, 8], [1, 64]), view(vtok[:, i, :], [64, 8], [1, 64]),
                view(be[:, i, :], [1, 8], [0, 64]), MUL)
        Og = view(al(4 * 512), [512, 4], [1, 512])
        Dm, QD, NA, TTm, Tm, ATm, Xm = [[view(al(512), [128, 4], [1, 128]) for _ in range(2)] for _ in range(7)]
        St = [al(512) for _ in range(2)]
        PCM = view(al(512), [64, 8], [1, 64])
        Xs, Us, t1s = al(512), al(512), al(512)
        vset(St[0], 0.0)
        cur = 0
        for ti in range(4):
            cs = slice(128 * ti, 128 * ti + 128)
            barrier()
            groups = []
            for g in range(2):
                hp = slice(64 * g, 64 * g + 64)
                b, pv, bw = bank()
                mm(pv, C["ident"], rep(C["negGD"], 4), True, False, bw + [(V, V.n)])
                for i in range(4):
                    h = 2 * i + g
                    o = pv[:, 128 * i:128 * i + 128]
                    mm(o, C["UI"], view(gg[:, ti, h:h + 1], [0, 128]), False, False)
                    t = mm(o, view(ng[:, ti, h:h + 1], [0, 128]), C["UI"], False, True, (), i == 3)
                td = act(Dm[g], view(pv, [128, 4], [1, 128]), ACT.Exp, w=[t])
                rel(b, td)
                b, pv, bw = bank()
                for i in range(4):
                    t = mm(pv[:, 128 * i:128 * i + 128], qk[hp, 4 + i, cs], qk[hp, 4 + i, cs], True, True,
                           bw if i == 0 else (), i == 3)
                t1 = vtt(NA[g], view(pv, [128, 4], [1, 128]), Dm[g], MUL, [t, td])
                rel(b, t1)
                t1 = vtt(NA[g], NA[g], view(nb_[:, ti, g:g + 1], [2, 4], [0, 128]), MUL)
                b, pv, bw = bank()
                for i in range(4):
                    t = mm(pv[:, 128 * i:128 * i + 128], qk[hp, i, cs], qk[hp, 4 + i, cs], True, True,
                           bw if i == 0 else (), i == 3)
                t2 = vtt(Dm[g], view(pv, [128, 4], [1, 128]), Dm[g], MUL, [t])
                rel(b, t2)
                for src, dst, tt in ((NA[g], ATm[g], t1), (Dm[g], QD[g], t2)):
                    b, pv, bw = bank()
                    for i in range(4):
                        t = tr(pv[:, 128 * i:128 * i + 128], src[:, i, :], bw + [tt] if i == 0 else (), i == 3)
                    tc = scopy(dst, view(pv, [128, 4], [1, 128]), [t])
                    if dst is ATm[g]:
                        t_at = tc
                    rel(b, tc)
                vcopy(Tm[g], rep(C["ident"], 4))
                vcopy(TTm[g], rep(C["ident"], 4))
                cpred(Tm[g], rep(C["M0"], 4).bitcast(U32), NA[g])
                t3 = cpred(TTm[g], rep(C["N0"], 4).bitcast(U32), ATm[g], [t_at])
                groups.append((Tm[g], TTm[g], ATm[g], [t3, tc], Xm[g]))
            tinv = invert(groups, True)
            w_inv = [x for y in tinv for x in y] + [tc]
            for p in (0, 1):
                r_ = slice(64 * p, 64 * p + 64)
                rt = slice(128 * ti + 64 * p, 128 * ti + 64 * p + 64)
                S0, S1 = St[cur], St[1 - cur]
                h8 = lambda x: view(x, [64, 8], [1, 64])
                col = lambda x: view(x[r_, ti, :], [1, 8], [0, 64])
                b, pv, bw = bank()
                for i in range(4):
                    t = mm(pv[r_, 128 * i:128 * i + 128], qk[:, 4 + i, rt], S0[:, 128 * i:128 * i + 128], True, True,
                           bw + w_inv + [(V, V.n)] if i == 0 else (), i == 3)
                vtt(h8(Xs[r_, :]), h8(pv[r_, :]), col(nbe), MUL, [t])
                t = vtt(Xs[r_, :], Xs[r_, :], vtok[r_, ti, :], ADD)
                rel(b, t)
                b, pv, bw = bank()
                for i in range(4):
                    for g in range(2):
                        c_ = 128 * i + 64 * g
                        t = mm(pv[r_, c_:c_ + 64], TTm[g][r_, i, r_], Xs[r_, c_:c_ + 64], True, True,
                               bw + [t] if i + g == 0 else (), i == 3 and g == 1)
                tu = scopy(Us[r_, :], pv[r_, :], [t])
                rel(b, tu)
                b, pv, bw = bank()
                for i in range(4):
                    f_ = slice(128 * i, 128 * i + 128)
                    t = mm(pv[:, f_], ktok[r_, ti, f_], Us[r_, f_], True, True, bw + [tu] if i == 0 else (), i == 3)
                ch = 2 * ti + p
                vtt(PCM, view(egl[:, ch, :], [1, 8], [0, 64]), h8(blkw), MUL, [t_egl])
                vtt(h8(S1), h8(S0), PCM, MUL)
                vtt(t1s, pv, blkw, MUL, [t])
                ts_ = vtt(S1, S1, t1s, ADD)
                rel(b, ts_)
                b, pv, bw = bank()
                b2, pv2, bw2 = bank()
                for i in range(4):
                    mm(pv[r_, 128 * i:128 * i + 128], qk[:, i, rt], S0[:, 128 * i:128 * i + 128], True, True,
                       bw if i == 0 else ())
                for i in range(4):
                    for g in range(2):
                        c_ = 128 * i + 64 * g
                        t = mm(pv2[r_, c_:c_ + 64], QD[g][r_, i, r_], Us[r_, c_:c_ + 64], True, True,
                               bw2 if i + g == 0 else (), i == 3 and g == 1)
                y_ = Og[r_, ti, :]
                vtt(h8(y_), h8(pv[r_, :]), col(egc), MUL, [t])
                t = vtt(y_, y_, pv2[r_, :], ADD)
                rel(b, t)
                rel(b2, t)
                cur = 1 - cur
        barrier()
        nr = al(64)
        tn = load_small(nr, row(I["gdn_norm_w_2"][l, :], 64))
        for i in range(4):
            y_ = Og[:, i, :]
            group_norm(y_, 8, 64, 1e-6, small, Xs, False)
            vtt(view(y_, [64, 8], [1, 64]), view(y_, [64, 8], [1, 64]), view(nr, [0, 8], [1, 64]), MUL, [tn])
            t = vtt(y_, y_, gz[:, i, :], MUL)
        to_fm([Og[:, i, :] for i in range(4)], 4, lambda f: catT[:, f, :], None, [t])
        barrier()
        top[0] = m1_

        sqk_ = view(al(4 * 512), [512, 4], [1, 512])
        sv = view(al(4 * 256), [256, 4], [1, 256])
        mq = view(al(4 * 256), [256, 4], [1, 256])
        ckv = view(al(4 * 128), [128, 4], [1, 128])
        krT = al(512)
        osb = view(al(4 * 256), [256, 4], [1, 256])
        gemm_fm(Wm, 2064, 512, 8, hh, lambda m: [(0, 512)],
                lambda m, g, pv, t: scopy(sqk_[:, m, :], pv, [t], scale=0.125 if m < 2 else 1.0))

        def ev_s(c, i, pv, t, n):
            scopy(sv[:, i, :], pv[:, 0:256], [t])
            return scopy(mq[:, i, :], pv[:, 256:512])
        gemm_tm(Wm, 2576, 512, 8, hh, W512, ev_s)
        gemm_tm(Wm, 3088, 128, 8, hh, W512, lambda c, i, pv, t, n: scopy(ckv[:, i, :], pv[:, 0:128], [t]))
        s, wv, tok = chunk(I["kr2"][l], 0, 8, 0, 64)
        b, pv, bw = bank()
        b2, pv2, bw2 = bank()
        for k in range(8):
            mm(pv[RP, :], wv[:, k, 0:32], hh[:, k, :], k == 0, k == 7, bw + [tok] if k == 0 else ())
        for k in range(8):
            t = mm(pv2[RP, :], wv[:, k, 32:64], hh[:, k, :], k == 0, k == 7, bw2 if k == 0 else (), k == 7)
        slot_free[s] = (t,)
        tmpr = al(512)

        def rope(dst, pa, pb, w):
            vtt(tmpr[RP, :], pa, cosT[RP, :], MUL, w)
            vtt(dst, pb, sinT[RP, :], MUL)
            return vtt(dst, dst, tmpr[RP, :], ADD)
        t_kr = rope(krT[RP, :], pv[RP, :], pv2[RP, :], [t])
        rel(b, t_kr)
        rel(b2, t_kr)
        m3_ = top[0]
        SP_ = [view(al(4 * 512), [512, 4], [1, 512]) for _ in range(2)]
        WT = [view(al(4 * 512), [512, 4], [1, 512]) for _ in range(2)]
        eb = [al(512), al(512)]
        wt_free = [(), ()]
        for h in range(4):
            hp = slice(64 * (h % 2), 64 * (h % 2) + 64)
            q_, k_ = sqk_[hp, h // 2, :], sqk_[hp, 2 + h // 2, :]
            SPh, W_ = SP_[h % 2], WT[h % 2]
            for s_ in range(4):
                lo = 128 * s_
                N = 512 - lo
                e_ = eb[s_ % 2]
                b, pv, bw = bank()
                t = mm(pv[:, 0:N], k_[:, lo:lo + 128], q_[:, lo:512], True, True, bw, True)
                act(e_[:, 0:N], pv[:, 0:N], ACT.Abs, w=[t, (V, V.n)])
                act(e_[:, 0:N], e_[:, 0:N], ACT.Exp, scale=-1.0)
                ta = act(e_[:, 0:N], e_[:, 0:N], ACT.Ln, bias=1.0)
                tv = stt(SPh[:, s_, lo:512], pv[:, 0:N], 0.0, e_[:, 0:N], MAX, ADD, [ta] + list(wt_free[h % 2]))
                rel(b, tv)
                tv = vtt(SPh[:, s_, lo:lo + 128], SPh[:, s_, lo:lo + 128], C["US128"], MUL)
            for s_ in range(4):
                lo = 128 * s_
                N = 512 - lo
                b, pv, bw = bank()
                mm(pv[:, 0:N], k_[:, lo:lo + 128], q_[:, lo:512], True, False, bw + [tv])
                mm(pv[:, 0:N], C["nLI128"], SPh[:, s_, lo:512], False, False)
                for j_ in range(s_ + 1, 4):
                    o_ = 128 * (j_ - s_)
                    mm(pv[:, o_:N], C["none"], SPh[:, j_, 128 * j_:512], False, False)
                t = mm(pv[:, 0:128], C["ident"], C["negGE"], False, True, (), True)
                ta = act(W_[:, s_, lo:512], pv[:, 0:N], ACT.Exp, w=[t] + list(wt_free[h % 2]))
                rel(b, ta)
            b, pv, bw = bank()
            for i in range(4):
                for s_ in range(i + 1):
                    t = mm(pv[:, 64 * i:64 * i + 64], W_[:, s_, 128 * i:128 * i + 128], sv[:, s_, 64 * h:64 * h + 64],
                           s_ == 0, s_ == i, bw + [ta] if i + s_ == 0 else (), i == 3 and s_ == 3)
            wt_free[h % 2] = (t,)
            tv = vcopy(osb[:, :, 64 * h:64 * h + 64], view(pv, [64, 4], [1, 64]), [t])
            rel(b, tv)
        to_fm([osb[:, i, :] for i in range(4)], 2, lambda f: catT[:, 4 + f, :], None, [tv])
        barrier()
        top[0] = m3_

        mqT = view(al(2 * 512), [512, 2], [1, 512])
        ckT = al(512)
        for i in range(4):
            group_norm(mq[:, i, :], 1, 256, 1e-6, small, tmpr, False)
            t = group_norm(ckv[:, i, :], 1, 128, 1e-6, small, tmpr, False)
        qn, kn = VC[f"qn{l}"], VC[f"kn{l}"]
        to_fm([mq[:, i, :] for i in range(4)], 2, lambda f: mqT[:, f, :],
              lambda f, o, i_, tt: act(o, i_, ACT.Copy, scale=qn[:, f:f + 1], w=[tt]), [t])
        t_cT = to_fm([ckv[:, i, :] for i in range(4)], 1, lambda f: ckT,
                     lambda f, o, i_, tt: act(o, i_, ACT.Copy, scale=kn[:, 0:1], w=[tt]), [t])
        uq = view(al(768), [384, 2], [1, 384])
        usw = view(al(256), [128, 2], [1, 128])
        ukv = al(512)
        tw = [load_small(uq, I["mla_w_uq_2"][l].rearrange("(k p) c -> p k c", p=128)),
              load_small(usw, I["uq_sw"][l].rearrange("(k p) c -> p k c", p=128)),
              load_small(ukv, I["mla_w_ukv_2"][l])]
        qh = view(al(4 * 512), [512, 4], [1, 512])
        kh = view(al(4 * 512), [512, 4], [1, 512])
        for h in range(4):
            b, pv, bw = bank()
            b2, pv2, bw2 = bank()
            b3, pv3, bw3 = bank()
            for k in range(2):
                mm(pv[0:96, :], uq[:, k, 96 * h:96 * h + 96], mqT[:, k, :], k == 0, k == 1, bw + tw + [t_cT] if k == 0 else ())
            for k in range(2):
                mm(pv2[RP, :], usw[:, k, 32 * h:32 * h + 32], mqT[:, k, :], k == 0, k == 1, bw2 if k == 0 else ())
            t = mm(pv3[0:64, :], ukv[:, 128 * h:128 * h + 64], ckT, True, True, bw3, True)
            ta = scopy(qh[0:64, h, :], pv[0:64, :], [t])
            ta = scopy(kh[0:64, h, :], pv3[0:64, :])
            rel(b3, ta)
            tv = rope(qh[RP, h, :], pv[RP, :], pv2[RP, :], [ta])
            vcopy(kh[RP, h, :], krT[RP, :])
            rel(b, tv, ta)
            rel(b2, tv)
        vm = view(al(4 * 256), [256, 4], [1, 256])
        for i in range(4):
            b, pv, bw = bank()
            t = mm(pv, ckT[:, 128 * i:128 * i + 128], ukv, True, True, bw, True)
            tv = vcopy(view(vm[:, i, :], [64, 4], [1, 64]), view(pv[:, 64:65], [128, 4], [1, 64]), [t])
            rel(b, tv)
        om = view(al(4 * 256), [256, 4], [1, 256])
        pr = [al(512), al(512)]
        pT = [view(al(512), [128, 4], [1, 128]) for _ in range(2)]
        pr_f, pT_f = [(), ()], [(), ()]
        SC = 96 ** -0.5
        n = 0
        st = al(8 * 16)
        for h in range(4):
            for i in range(4):
                N = 128 * (i + 1)
                z_ = n % 2
                sc_ = st[:, 8 * (n % 16):8 * (n % 16) + 8]
                b, pv, bw = bank()
                mm(pv[:, 0:N], qh[0:96, h, 128 * i:128 * i + 128], kh[0:96, h, 0:N], True, False, bw + [(V, V.n)] if n == 0 else bw)
                t = mm(pv[:, N - 128:N], C["ident"], C["negLT"], False, True, (), True)
                tm = vred(sc_[:, 0:1], pv[:, 0:N], MAX, [t])
                tm = vts(sc_[:, 1:2], sc_[:, 0:1], -SC, None, MUL)
                ta = act(pr[z_][:, 0:N], pv[:, 0:N], ACT.Exp, scale=SC, bias=sc_[:, 1:2], w=[tm] + list(pr_f[z_]),
                         acc=sc_[:, 2:3])
                rel(b, ta)
                tr_ = recip(sc_[:, 3:4], sc_[:, 2:3], [ta])
                b, pv, bw = bank()
                for s_ in range(i + 1):
                    t = tr(pv[:, 128 * s_:128 * s_ + 128], pr[z_][:, 128 * s_:128 * s_ + 128],
                           bw + [ta] if s_ == 0 else (), s_ == i)
                pr_f[z_] = (t,)
                ta = scopy(view(pT[z_], [1, N]), pv[:, 0:N], [t] + list(pT_f[z_]))
                rel(b, ta)
                b, pv, bw = bank()
                for s_ in range(i + 1):
                    t = mm(pv[:, 0:64], pT[z_][:, s_, :], vm[:, s_, 64 * h:64 * h + 64], s_ == 0, s_ == i,
                           bw + [ta] if s_ == 0 else (), s_ == i)
                pT_f[z_] = (t,)
                tv = vts(om[:, i, 64 * h:64 * h + 64], pv[:, 0:64], sc_[:, 3:4], None, MUL, w=[t])
                rel(b, tv)
                n += 1
        t = to_fm([om[:, i, :] for i in range(4)], 2, lambda f: catT[:, 6 + f, :], None, [tv])

        def ev(c, i, pv, t, n):
            x_ = hX[:, i, c:c + 512]
            return stt(x_, x_, ALPHA, pv, MUL, ADD, [t])
        gemm_tm(I["mix_w_o_2"][l], 0, 1024, 8, catT, W512, ev, [t])
        barrier()
        top[0] = m0_
        layer_norm_all(l, 1)

    blkw = al(512)
    vcopy(view(blkw, [128, 4], [1, 128]), rep(C["blk"], 4))
    hT_from_x()
    for l in range(2):
        ffn(l, "ffa_w_in_2", "ffa_w_out_2", 0)
        mixer(l)
        ffn(l, "ffb_w_in_2", "ffb_w_out_2", 2)
        m_ = top[0]
        pTl = view(al(1024), [512, 2], [1, 512])
        sg = view(al(4 * 512), [512, 4], [1, 512])
        t_p = load_small(pTl, I["pT"][l].rearrange("(k p) c -> p k c", p=128))
        for hf in range(2):
            gemm_tm(I["ple_w_gate_2"][l], 512 * hf, 512, 8, hh, W512,
                    lambda c, i, pv, t, n: act(sg[:, i, :], pv, ACT.Sigmoid, w=[t, (V, V.n)]))

            def ev_p(c, i, pv, t, n, hf=hf):
                t1 = vtt(sg[:, i, :], sg[:, i, :], pv, MUL, [t, (S, S.n)])
                x_ = hX[:, i, 512 * hf:512 * hf + 512]
                vtt(x_, x_, sg[:, i, :], ADD)
                return t1
            gemm_tm(I["ple_w_proj_2"][l], 512 * hf, 512, 2, pTl, W512, ev_p, [t_p])
        barrier()
        top[0] = m_
        if l == 0:
            hT_from_x()
    for i in range(4):
        load_small(out[0, 128 * i:128 * i + 128, :], hX[:, i, :], [(V, V.n)])


_WEIGHTS = ["x", "ctx", "b_ada", "w_ada", "w_in", "rw_w2", "rw_a2", "rw_g2", "rw_lnw", "rw_lnb", "ml_nw",
            "p_a", "p_b", "p_c", "w_out", "w_mlp1", "w_mlp2", "g_final", "positions_2", "ffa_w_in_2", "ffa_w_out_2",
            "mix_w_in_2", "gdn_a_log_2", "gdn_dt_bias_2", "gdn_norm_w_2", "mla_w_uq_2", "mla_w_ukv_2", "mix_w_o_2",
            "ffb_w_in_2", "ffb_w_out_2", "ln_g_2", "ln_b_2", "ple_w_gate_2", "ple_w_proj_2"]
_SQUEEZE = {"w_ada", "w_in", "p_a", "p_b", "p_c", "w_out", "w_mlp1", "w_mlp2"}


def _fm(v):
    v = np.asarray(v)
    return np.ascontiguousarray(v.reshape(-1, 128).T)


def arrays_of(inputs):
    a = {k: np.ascontiguousarray(inputs[k]) for k in _WEIGHTS}
    for k in _SQUEEZE:
        a[k] = a[k][0]
    g = {k: np.asarray(inputs[k]) for k in ("c", "c_ctx", "b_ada", "g_norm1", "g_norm2", "mu_prev", "mu_next", "rw_w0",
                                             "rw_a0", "rw_kk", "rw_ka", "rw_rk", "cv_dw", "cv_db", "cv_lnw", "cv_lnb",
                                             "gdn_conv_w_2", "mla_q_norm_w_2", "mla_kv_norm_w_2", "ml_ib", "ml_fb",
                                             "p_2", "mla_w_uq_2", "mix_w_in_2")}
    cdw = np.transpose(g["cv_dw"][0].reshape(31, 4, 128), (2, 1, 0)).reshape(128, 124)
    gcw = [np.transpose(g["gdn_conv_w_2"][l].reshape(4, 12, 128), (2, 1, 0)).reshape(128, 48) for l in range(2)]
    parts = [_fm(g["c"]), _fm(g["c_ctx"]), _fm(g["b_ada"]), _fm(g["g_norm1"]), _fm(g["g_norm2"]), _fm(g["mu_prev"]),
             _fm(g["mu_next"]), _fm(g["rw_w0"]), _fm(g["rw_a0"]), _fm(g["rw_kk"]), _fm(g["rw_ka"]), _fm(g["rw_rk"]),
             cdw, _fm(g["cv_db"]), _fm(g["cv_lnw"]), _fm(g["cv_lnb"]), gcw[0], gcw[1],
             _fm(g["mla_q_norm_w_2"][0]), _fm(g["mla_q_norm_w_2"][1]),
             _fm(g["mla_kv_norm_w_2"][0]), _fm(g["mla_kv_norm_w_2"][1])]
    a["vecs"] = np.ascontiguousarray(np.concatenate(parts, axis=1))
    a["mlgb"] = np.ascontiguousarray(np.stack([g["ml_ib"][0], g["ml_fb"][0]], axis=1).reshape(16))
    a["pT"] = np.ascontiguousarray(np.transpose(g["p_2"][:, 0], (0, 2, 1)))
    u = g["mla_w_uq_2"].reshape(2, 256, 4, 96)
    a["uq_sw"] = np.ascontiguousarray(np.concatenate([u[..., 80:96], u[..., 64:80]], axis=-1).reshape(2, 256, 128))
    r = g["mix_w_in_2"][:, :, 3216:3248]
    a["kr2"] = np.ascontiguousarray(np.concatenate([r, r[..., 16:32], r[..., 0:16]], axis=-1))
    a["consts"] = const_tables()[1]
    return a


def kernel(**inputs):
    import concourse.bacc as _bacc
    from concourse.bass_utils import run_bass_kernel_spmd as _run

    nc = _bacc.Bacc("TRN2", target_bir_lowering=False, num_devices=1)
    arrays = arrays_of(inputs)
    I = {k: nc.dram_tensor(f"in_{k}", v.shape, mybir.dt.from_np(v.dtype), kind="ExternalInput").ap()
         for k, v in arrays.items()}
    out = nc.dram_tensor("out", (1, 512, 1024), F32, kind="ExternalOutput").ap()
    build(nc, I, out)
    r = _run(nc, [{f"in_{k}": v for k, v in arrays.items()}], core_ids=[0])
    return r.results[0]["out"]
```

```python
from contextlib import ExitStack

import numpy as np

import concourse.bass as bass
from concourse import mybir

F32 = mybir.dt.float32
F32R = mybir.dt.float32r
U32 = mybir.dt.uint32
I32 = mybir.dt.int32
ALU = mybir.AluOpType
ACT = mybir.ActivationFunctionType
AX = mybir.AxisListType.X
ADD, SUB, MUL, MAX, MIN = ALU.add, ALU.subtract, ALU.mult, ALU.max, ALU.min
NEG = -1.0e30
KAP = float(np.exp(-0.5))
SLOT = 2048
NSLOT = 3
ARENA = 53200
RING = 3 * SLOT * NSLOT


def const_tables():
    i = np.arange(128)[:, None]
    j = np.arange(128)[None, :]
    same = i // 64 == j // 64
    t = {"ident": i == j, "ones": np.ones((128, 128)), "blk": same, "J": i + j == 127}
    for n in range(6):
        s = 1 << n
        m = (i // (2 * s) == j // (2 * s)) & (i // s % 2 == 1) & (j // s % 2 == 0)
        t[f"M{n}"] = m
        t[f"N{n}"] = m.T
    t["US"] = same & (i < j)
    t["UI"] = same & (i <= j)
    t["LS"] = same & (i > j)
    t["LI"] = same & (i >= j)
    t["US128"] = i < j
    t["LS128"] = i > j
    t["nUI128"] = -1.0 * (i <= j)
    t["nLI128"] = -1.0 * (i >= j)
    t["none"] = -np.ones((128, 128))
    t["negGT"] = NEG * (i > j)
    t["negLT"] = NEG * (i < j)
    t["negGE"] = NEG * (i >= j)
    t["negGD"] = NEG * (1 - (same & (i >= j)))
    t["b2"] = (i // 64 == j) * (j < 2)
    t["half0"] = (i < 64) + 0 * j
    t["half1"] = (i >= 64) + 0 * j
    t["rs64"] = 1.0 * (j % 64 != 0) + 0 * i
    t["rs128"] = 1.0 * (j != 0) + 0 * i
    for d in range(2):
        for h in range(4):
            t[f"sel{d}{h}"] = (i == 32 * d + h) + 0 * j
    inv = (1.0 / (np.float32(10000.0) ** (np.arange(0, 32, 2, dtype=np.float32) / np.float32(32)))).astype(np.float32)
    r = np.zeros((128, 128), np.float32)
    r[64:96, 0] = np.concatenate([inv, inv])
    r[64:96, 1] = np.concatenate([-np.ones(16), np.ones(16)])
    t["rope"] = r
    names = list(t)
    return names, np.concatenate([np.asarray(t[k], np.float32) for k in names], axis=1)


VECS = [("c", 8), ("cc", 8), ("bada", 48), ("g1", 8), ("g2", 8), ("mup", 15), ("mun", 15), ("w0", 8), ("a0", 8),
        ("kk", 4), ("ka", 4), ("rk", 4), ("cdw", 124), ("cdb", 4), ("clw", 4), ("clb", 4),
        ("gcw0", 48), ("gcw1", 48), ("qn0", 2), ("qn1", 2), ("kn0", 1), ("kn1", 1)]
VOFF, _o = {}, 0
for _n, _k in VECS:
    VOFF[_n] = (_o, _k)
    _o += _k
NVEC = _o


class Counter:

    def __init__(self, sem):
        self.sem, self.n = sem, 0


class Queue(Counter):

    def __init__(self, sem, chained):
        super().__init__(sem)
        self.todo, self.seen, self.chained = [], {}, chained

    def wait(self, tokens):
        for who, v in tokens:
            if self.seen.get(id(who), 0) < v:
                self.seen[id(who)] = v
                self.todo.append(("wait", who.sem, v))

    def op(self, fn, w=(), sig=True):
        self.wait(w)
        if self.chained:
            self.wait([(self, self.n)])
        if not sig:
            self.todo.append(("op", fn, None, 0))
            return None
        self.n += 1
        self.todo.append(("op", fn, self.sem, 1))
        return (self, self.n)

    def dma(self, fn, counter, w=()):
        self.wait(w)
        counter.n += 16
        self.todo.append(("op", fn, counter.sem, 16))
        return (counter, counter.n)

    def run(self, eng):
        for x in self.todo:
            if x[0] == "wait":
                eng.wait_ge(x[1], x[2])
            else:
                ins = x[1]()
                if x[2] is not None:
                    ins.then_inc(x[2], x[3])


def view(ap, *dims):
    return bass.AP(ap.tensor, ap.offset, [ap.ap[0]] + [list(d) for d in dims])


class Plan:

    def __init__(self):
        self.known, self.loads, self.fences, self.operands = False, [], set(), set()


def build(nc, I, out):
    with ExitStack() as ctx:
        sems = [ctx.enter_context(nc.semaphore(f"s{n}")) for n in range(40)]
        plan = Plan()
        psum = ctx.enter_context(nc.psum_tensor("psum", [128, 8, 512], F32))
        for last in (False, True):
            rmem = {}
            for n, (o, size) in enumerate(sorted(plan.operands)):
                with nc.sbuf_tensor(f"pad{n}", [128, o], F32):
                    with nc.sbuf_tensor(f"r{n}", [128, size], F32R) as rt:
                        rmem[o, size] = rt
            with ExitStack() as one:
                keep = ctx if last else one
                name = "" if last else "0"
                mem = [keep.enter_context(nc.sbuf_tensor(f"ring{name}", [128, RING], F32)),
                       keep.enter_context(nc.sbuf_tensor(f"arena{name}", [128, ARENA - RING], F32))]
                it = iter(sems)
                P, V, S, G, D = (Queue(next(it), c) for c in (False, True, True, True, False))
                slot_sem = [Counter(next(it)) for _ in range(NSLOT)]
                small_sem = [Counter(next(it)) for _ in range(24)]
                body(nc, I, out, mem, rmem, psum, P, V, S, G, D, slot_sem, small_sem, plan)
            plan.known = True
        block = ctx.enter_context(nc.Block())

        @block.sync
        def _(e):
            D.run(e)

        @block.tensor
        def _(e):
            P.run(e)

        @block.vector
        def _(e):
            V.run(e)

        @block.scalar
        def _(e):
            S.run(e)

        @block.gpsimd
        def _(e):
            G.run(e)
            for c in small_sem + slot_sem:
                if c.n:
                    e.wait_ge(c.sem, c.n)


def body(nc, I, out, mem, rmem, psum, P, V, S, G, D, slot_sem, small_sem, plan):
    top = [0]

    def al(n):
        o = top[0]
        top[0] += n
        assert top[0] <= ARENA, (top[0], n)
        if o < RING:
            assert top[0] <= RING
            return mem[0][:, o:o + n]
        return mem[1][:, o - RING:o - RING + n]

    free_banks = [(b, ()) for b in range(8)]

    def bank():
        b, w = free_banks.pop(0)
        return b, psum[:, b, :], list(w)

    def rel(b, *tokens):
        free_banks.append((b, tokens))

    def barrier():
        ends = [(q, q.n) for q in (P, V, S, G)]
        for q in (P, V, S, G):
            q.wait(ends)
        return ends

    def mm(o, l, r, start, stop, w=(), sig=False):
        return P.op(lambda: nc.tensor.matmul(o, l, r, start=start, stop=stop, skip_group_check=True), w, sig)

    def tr(o, i, w=(), sig=False):
        return P.op(lambda: nc.tensor.transpose(o, i, C["ident"]), w, sig)

    def act(o, i, f, scale=1.0, bias=0.0, w=(), acc=None):
        if acc is None:
            return S.op(lambda: nc.scalar.activation(o, i, f, scale=scale, bias=bias), w)
        return S.op(lambda: nc.scalar.activation(o, i, f, scale=scale, bias=bias, accum_out=acc), w)

    def scopy(o, i, w=(), scale=1.0):
        return act(o, i, ACT.Copy, scale=scale, w=w)

    def vcopy(o, i, w=()):
        return V.op(lambda: nc.vector.tensor_copy(o, i), w)

    def vtt(o, a, b, f, w=()):
        return V.op(lambda: nc.vector.tensor_tensor(o, a, b, f), w)

    def vts(o, a, s1, s2, f0, f1=None, w=()):
        if f1 is None:
            return V.op(lambda: nc.vector.tensor_scalar(o, a, s1, None, f0), w)
        return V.op(lambda: nc.vector.tensor_scalar(o, a, s1, s2, f0, f1), w)

    def stt(o, a, s, b, f0, f1, w=()):
        return V.op(lambda: nc.vector.scalar_tensor_tensor(out=o, in0=a, scalar=s, in1=b, op0=f0, op1=f1), w)

    def vred(o, i, f, w=()):
        return V.op(lambda: nc.vector.tensor_reduce(o, i, AX, f), w)

    def recip(o, i, w=()):
        return V.op(lambda: nc.vector.reciprocal(o, i), w)

    def scan(o, a, b, f0, f1, w=()):
        return V.op(lambda: nc.vector.tensor_tensor_scan(o, a, b, 0.0, f0, f1), w)

    def cpred(o, m, d, w=()):
        return V.op(lambda: nc.vector.copy_predicated(o, m, d), w)

    def vset(o, v, w=()):
        return V.op(lambda: nc.vector.memset(o, v), w)

    def gtt(o, a, b, f, w=()):
        return G.op(lambda: nc.gpsimd.tensor_tensor(o, a, b, f), w)

    n_small = [0]

    def load_small(dst, src, w=()):
        c = small_sem[n_small[0] % len(small_sem)]
        n_small[0] += 1

        def go():
            with nc.allow_non_contiguous_dma(reason="small"):
                return nc.gpsimd.dma_start(dst, src)
        return G.dma(go, c, list(w) + [(c, c.n)])


    ring = al(SLOT * NSLOT * 3)

    live = {(NSLOT * SLOT, 2 * NSLOT * SLOT)}
    plan.operands.add((NSLOT * SLOT, 2 * NSLOT * SLOT))

    def R(ap):
        if not plan.known:
            return ap
        o = ap.offset + (0 if ap.tensor.name == ring.tensor.name else RING)
        for (start, size), rt in rmem.items():
            if start <= o < start + size and (start, size) in live:
                base = rt[:, 0:1]
                return bass.AP(base.tensor, o - start, [base.ap[0]] + [list(d) for d in ap.ap[1:]])
        assert False

    raw = [ring[:, SLOT * n:SLOT * n + SLOT] for n in range(NSLOT)]
    his = [ring[:, SLOT * (NSLOT + n):SLOT * (NSLOT + n) + SLOT] for n in range(NSLOT)]
    los = [ring[:, SLOT * (2 * NSLOT + n):SLOT * (2 * NSLOT + n) + SLOT] for n in range(NSLOT)]
    raw_free = [() for _ in range(NSLOT)]
    use_free = [() for _ in range(NSLOT)]
    n_req, n_dma, n_split = [0], [0], [0]
    dma_tok, split_tok = {}, {}

    def ring_back(tokens):
        if not plan.known:
            plan.fences.add(n_req[0])
        for n in range(NSLOT):
            raw_free[n] = use_free[n] = tuple(tokens)

    def load_ahead(i):
        stop = min([f for f in plan.fences if f > i] + [len(plan.loads)])
        while n_dma[0] < min(i + NSLOT, stop) or n_split[0] < min(i + 2, stop):
            if n_split[0] < min(i + 2, stop) and n_split[0] < n_dma[0]:
                j = n_split[0]
                z, (pieces, size, split) = j % NSLOT, plan.loads[j]
                if split:
                    h_, l_, r_ = R(his[z][:, 0:size]), R(los[z][:, 0:size]), raw[z][:, 0:size]
                    t1 = act(h_, r_, ACT.Copy, w=[dma_tok[j]] + list(use_free[z]))
                    t2 = vtt(l_, r_, h_, SUB, [t1])
                    raw_free[z] = (t1, t2)
                    split_tok[j] = t2
                else:
                    split_tok[j] = dma_tok[j]
                n_split[0] += 1
            else:
                j = n_dma[0]
                z, (pieces, size, split) = j % NSLOT, plan.loads[j]
                for e, (fn, src) in enumerate(pieces):
                    dst = fn(raw[z])
                    dma_tok[j] = D.dma(lambda dst=dst, src=src: nc.sync.dma_start(dst, src), slot_sem[z],
                                       raw_free[z] if e == 0 else ())
                n_dma[0] += 1

    def wload(pieces, size, split=True):
        i = n_req[0]
        if not plan.known:
            plan.loads.append((pieces, size, split))
            n_req[0] += 1
            return i % NSLOT, raw[0], raw[0], (D, 0)
        load_ahead(i)
        n_req[0] += 1
        z = i % NSLOT
        return (z, R(his[z]), R(los[z]), split_tok[i]) if split else (z, raw[z], None, split_tok[i])

    def used(z, t, split=True):
        use_free[z] = (t,)
        if not split:
            raw_free[z] = (t,)

    def chunk(W, r0, kt, c0, nc_, split=True):
        src = W[r0:r0 + 128 * kt, c0:c0 + nc_].rearrange("(k p) c -> p k c", p=128)
        z, hi, lo, tok = wload([(lambda x: view(x, [nc_, kt], [1, nc_]), src)], nc_ * kt, split)
        return z, view(hi, [nc_, kt], [1, nc_]), lo and view(lo, [nc_, kt], [1, nc_]), tok

    def split_x(x, o, w=()):
        toks = []
        for k in range(x.shape[1]):
            t = act(R(o[:, 0, k, :]), x[:, k, :], ACT.Copy, w=w)
            toks.append(vtt(R(o[:, 1, k, :]), x[:, k, :], R(o[:, 0, k, :]), SUB, [t]))
        return toks

    def opnd(k, n):
        o = top[0]
        for key in [x for x in live if x[0] < o + 2 * k * n and o < x[0] + x[1]]:
            live.remove(key)
        live.add((o, 2 * k * n))
        plan.operands.add((o, 2 * k * n))
        return view(al(2 * k * n), [k * n, 2], [n, k], [1, n])

    def mm3(o, l, r, first, last, w=(), sig=False):
        (lh, ll), (rh, rl) = l, r
        mm(o, lh, rh, first, False, w)
        mm(o, lh, rl, False, False)
        return mm(o, ll, rh, False, last, (), sig)

    def gemm_fm(W, c0, ncols, kt, xs, segs, evac, w=(), r0=0, xt=None):
        for done in range(0, ncols, 256):
            n = min(256, ncols - done)
            z, wh, wl, tok = chunk(W, r0, kt, c0 + done, n)
            for m in range(0, n, 128):
                for g, (a, sz) in enumerate(segs((done + m) // 128)):
                    x = xs[g] if isinstance(xs, tuple) else xs
                    b, pv, bw = bank()
                    for k in range(kt):
                        t = mm3(pv[:, 0:sz], (wh[:, k, m:m + 128], wl[:, k, m:m + 128]),
                                (R(x[:, 0, k, a:a + sz]), R(x[:, 1, k, a:a + sz])), k == 0, k == kt - 1,
                                (bw + [tok] + list(w) if k == 0 else []) + ([xt[k]] if xt else []), k == kt - 1)
                    used(z, t)
                    rel(b, evac((done + m) // 128, g, pv, t))

    def gemm_tm(W, c0, ncols, kt, xs, tiles, evac, w=(), step=512, r0=0, xt=None):
        for done in range(0, ncols, step):
            n = min(step, ncols - done)
            kmax = min(8, 2048 // n) if n > 64 else 8
            banks = [bank() for _ in tiles]
            for k0 in range(0, kt, kmax):
                kn = min(kmax, kt - k0)
                z, wh, wl, tok = chunk(W, r0 + 128 * k0, kn, c0 + done, n)
                for i, a in enumerate(tiles):
                    b, pv, bw = banks[i]
                    x, a = a if isinstance(a, tuple) else (xs, a)
                    for k in range(kn):
                        q_ = k0 + k
                        t = mm3(pv[:, 0:n], (R(x[:, 0, q_, a:a + 128]), R(x[:, 1, q_, a:a + 128])),
                                (wh[:, k, :], wl[:, k, :]), q_ == 0, q_ == kt - 1,
                                (bw if q_ == 0 else []) + ([tok] + list(w) if k == 0 else []) + ([xt[q_]] if xt else []),
                                k == kn - 1)
                    used(z, t)
                    if k0 + kn == kt:
                        rel(b, evac(done, i, pv, t, n))

    def to_fm(srcs, nf, dst, evac=None, w=(), width=128):
        t2 = None
        for f in range(nf):
            for q in range(0, len(srcs), 4):
                part = srcs[q:q + 4]
                b, pv, bw = bank()
                for i, s_ in enumerate(part):
                    t = tr(pv[:, 128 * i:128 * i + 128], s_[:, 128 * f:128 * f + 128],
                           bw + list(w) if i == 0 else (), i == len(part) - 1)
                o = dst(f)[:, 128 * q:128 * q + 128 * len(part)]
                i_ = pv[:, 0:128 * len(part)]
                t2 = evac(f, o, i_, t) if evac else scopy(o, i_, [t])
                rel(b, t2)
        return t2

    tmp_op = al(1024)
    n_tmp = [0]
    tmp_free = [(), ()]

    def to_op(srcs, nf, dst, c0=0, scale=None, bias=None, w=()):
        toks = []
        for f in range(nf):
            b, pv, bw = bank()
            n = 128 * len(srcs)
            for i, s_ in enumerate(srcs):
                t = tr(pv[:, 128 * i:128 * i + 128], s_[:, 128 * f:128 * f + 128],
                       bw + list(w) if i == 0 else (), i == len(srcs) - 1)
            hi, lo = (R(dst[:, j, f, c0:c0 + n]) for j in (0, 1))
            if scale is None:
                t1 = act(hi, pv[:, 0:n], ACT.Copy, w=[t])
                t2 = vtt(lo, pv[:, 0:n], hi, SUB, [t1])
                rel(b, t2)
            else:
                z = n_tmp[0] % 2
                n_tmp[0] += 1
                x = tmp_op[:, 512 * z:512 * z + n]
                t1 = act(x, pv[:, 0:n], ACT.Identity, scale=scale(f), bias=bias(f) if bias else 0.0,
                         w=[t] + list(tmp_free[z]))
                rel(b, t1)
                t1 = act(hi, x, ACT.Copy)
                t2 = vtt(lo, x, hi, SUB, [t1])
                tmp_free[z] = (t2,)
            toks.append(t2)
        return toks

    def borrow():
        barrier()
        o = [0]

        def lend(n):
            o[0] += n
            assert o[0] <= 3 * NSLOT * SLOT, o[0]
            return ring[:, o[0] - n:o[0]]
        return lend

    names, _ = const_tables()
    cst = al(128 * len(names))
    C = {k: cst[:, 128 * i:128 * i + 128] for i, k in enumerate(names)}
    t_c = load_small(cst, I["consts"])
    vec = al(NVEC)
    t_v = load_small(vec, I["vecs"])
    VC = {k: vec[:, o:o + n] for k, (o, n) in VOFF.items()}
    for q in (P, V, S, G):
        q.wait([t_c, t_v])

    def rep(c, n, width=128):
        return view(c, [0, n], [1, width])

    def row(src_ap, n):
        return bass.AP(src_ap.tensor, src_ap.offset, [[0, 128], [1, n]])

    def rstd(o, ssq, n, eps, w=()):
        t = vts(o, ssq, 1.0 / n, eps, MUL, ADD, w=w)
        t = act(o, o, ACT.Sqrt, w=[t])
        return recip(o, o, [t])

    st6 = al(16)

    def layer_norm_tile(o, x, n, eps, scr, w=()):
        V.op(lambda: nc.vector.bn_stats(st6[:, 0:6], x[:, 0:512]), w)
        V.op(lambda: nc.vector.bn_stats(st6[:, 6:12], x[:, 512:1024]))
        t = V.op(lambda: nc.vector.bn_aggr(scr[:, 0:2], st6[:, 0:12]))
        rstd(scr[:, 2:3], scr[:, 1:2], 1.0, eps, w=[t])
        return vts(o, x, scr[:, 0:1], scr[:, 2:3], SUB, MUL)

    def group_norm(x, g, n, eps, scr, sq, mean, w=()):
        x3, q3 = view(x, [n, g], [1, n]), view(sq, [n, g], [1, n])
        if mean:
            vred(scr[:, 0:g], x3, ADD, w)
            vts(scr[:, 0:g], scr[:, 0:g], 1.0 / n, None, MUL)
            vtt(x3, x3, view(scr[:, 0:g], [1, g], [0, n]), SUB)
            w = ()
        vtt(q3, x3, x3, MUL, w)
        t = vred(scr[:, g:2 * g], q3, ADD)
        rstd(scr[:, 2 * g:3 * g], scr[:, g:2 * g], n, eps, [t])
        return vtt(x3, x3, view(scr[:, 2 * g:3 * g], [1, g], [0, n]), MUL)

    def invert(groups, low):
        toks = [g[3] for g in groups]
        for n in range(1, 6):
            m, mt = (C[f"M{n}"], C[f"N{n}"]) if low else (C[f"N{n}"], C[f"M{n}"])
            m, mt = rep(m, 4).bitcast(U32), rep(mt, 4).bitcast(U32)
            xs = []
            for gi, (T, TT, AT, _, X) in enumerate(groups):
                b, pv, bw = bank()
                for i in range(4):
                    t = mm(pv[:, 128 * i:128 * i + 128], AT[:, i, :], T[:, i, :], True, True,
                           bw + toks[gi] if i == 0 else (), i == 3)
                tx = scopy(view(X, [1, 512]), pv, [t])
                rel(b, tx)
                xs.append(tx)
            for gi, (T, TT, AT, _, X) in enumerate(groups):
                new = []
                jobs = [(1, TT, mt)] if n == 5 else [(0, T, m), (1, TT, mt)]
                for which, dst, mask in jobs:
                    b, pv, bw = bank()
                    for i in range(4):
                        l, r = (TT[:, i, :], X[:, i, :]) if which == 0 else (X[:, i, :], TT[:, i, :])
                        t = mm(pv[:, 128 * i:128 * i + 128], l, r, True, True,
                               bw + [xs[gi]] + toks[gi] if i == 0 else (), i == 3)
                    new.append((b, pv, t, dst, mask))
                last = new[-1][2]
                out_t = []
                for b, pv, t, dst, mask in new:
                    t2 = cpred(dst, mask, view(pv, [128, 4], [1, 128]), [last])
                    rel(b, t2)
                    out_t.append(t2)
                toks[gi] = out_t
        return toks

    SEGS = [(0, 512), (0, 256)]
    W512 = [0, 128, 256, 384]
    TW = 770
    TO = [514, 642, 0, 128, 256, 384]
    SEQ_ = ([0, 1, 2, 3, 4, 5], [1, 0, 5, 4, 3, 2])

    mk_hT = top[0]
    hL = opnd(8, 512)
    silc = al(16)
    silcv = view(silc, [2, 8], [1, 2])
    mod = view(al(96), [2, 48], [1, 2])
    small = al(256)
    sc1 = view(al(16), [2, 8], [1, 2])
    sc2 = view(al(16), [2, 8], [1, 2])
    mk_y = top[0]
    ycT = view(al(4 * 512), [512, 4], [1, 512])
    yaT = view(al(4 * 512), [512, 4], [1, 512])

    act(view(silc, [2, 8]), VC["c"], ACT.Silu)
    t_sil = act(view(silc[:, 1:2], [2, 8]), VC["cc"], ACT.Silu)
    need = [0, 1, 3, 4]
    for part in need:
        b, pv, bw = bank()
        for hf in range(4):
            s, wv, _, tok = chunk(I["w_ada"], 0, 8, part * 1024 + 256 * hf, 256, False)
            for m in range(2):
                for k in range(8):
                    t = mm(pv[:, 4 * hf + 2 * m:4 * hf + 2 * m + 2], wv[:, k, 128 * m:128 * m + 128], silcv[:, k, :],
                           k == 0, k == 7, bw + [tok, t_sil] if k == 0 and m == 0 else (), k == 7 and m == 1)
            used(s, t, False)
        o = mod[:, 8 * part:8 * part + 8, :]
        t = vtt(o, view(pv, [2, 8], [1, 2]), view(VC["bada"][:, 8 * part:8 * part + 8], [1, 8], [0, 2]), ADD, [t])
        rel(b, t)
    for sc, part, g in ((sc1, 1, "g1"), (sc2, 4, "g2")):
        vts(sc, mod[:, 8 * part:8 * part + 8, :], 1.0, None, ADD)
        t_sc = vtt(sc, sc, view(VC[g], [1, 8], [0, 2]), MUL)

    def bcast_rows(dst, part):
        m_ = top[0]
        lt = view(al(1024), [128, 8], [1, 128])
        bi = al(1024)
        t0 = load_small(bi, row(I["b_ada"][0, 1024 * part:1024 * part + 1024], 1024), barrier())
        t1 = vcopy(lt, view(silc, [2, 8], [0, 128]))
        for hf in range(2):
            b, pv, bw = bank()
            for k0 in (0, 4):
                s, wv, _, tok = chunk(I["w_ada"], 128 * k0, 4, part * 1024 + 512 * hf, 512, False)
                for k in range(4):
                    t = mm(pv, lt[:, k0 + k, :], wv[:, k, :], k + k0 == 0, k + k0 == 7,
                           (bw if k0 == 0 else []) + [tok, t1] if k == 0 else (), k == 3)
                used(s, t, False)
            t = vtt(dst[:, 512 * hf:512 * hf + 512], pv, bi[:, 512 * hf:512 * hf + 512], ADD, [t, t0])
            rel(b, t)
        barrier()
        top[0] = m_
        return t

    def rms_scales(o, x, scr, w=()):
        t = act(scr, x, ACT.Square, w=w, acc=o)
        return rstd(o, o, 1024, 1e-6, [t])

    def norm_mod_op(xs, cols, sc, sh, dst, scr, w=()):
        xn = []
        for i, x in enumerate(xs):
            r = small[:, i:i + 1]
            t = rms_scales(r, x, scr, w[i] if w else ())
            t = vts(x, x, r, None, MUL, w=[t])
            xn.append(x)

        V.wait([t_sc])
        S.wait([t_sc])
        return to_op(xn, 8, dst, 0, lambda f: sc[:, f, cols:cols + 1], lambda f: sh[:, f, cols:cols + 1], [t])

    mk_c = top[0]
    hC = opnd(8, 256)
    mk = top[0]
    xs_all = al(6 * 1024)
    scr = al(1024)
    tk = []
    for i in range(4):
        tk.append([load_small(xs_all[:, 1024 * i:1024 * i + 1024], I["x"][0, 128 * i:128 * i + 128, :])])
    for i in range(2):
        tk.append([load_small(xs_all[:, 1024 * (4 + i):1024 * (5 + i)], I["ctx"][0, 128 * i:128 * i + 128, :])])
    tiles = [xs_all[:, 1024 * i:1024 * i + 1024] for i in range(6)]
    norm_mod_op(tiles[0:4], 0, sc1, mod[:, 0:8, :], hL, scr, tk[0:4])
    norm_mod_op(tiles[4:6], 1, sc1, mod[:, 0:8, :], hC, scr, tk[4:6])
    barrier()
    top[0] = mk

    CVO, MLO, GO = 1920, 2944, 5008
    q = view(al(4 * 512), [512, 4], [1, 512])
    kx = view(al(4 * 768), [768, 4], [1, 768])
    v1 = view(al(6 * 4 * 129), [4 * 129, 6], [129, 4], [1, 129])
    og = view(al(4 * 512), [512, 4], [1, 512])
    gates = view(al(6 * 16), [16, 6], [1, 16])
    gb = al(16)
    t_gb = load_small(gb, row(I["mlgb"], 16))
    vset(v1, 1.0)
    KT = [512, 640, 0, 128, 256, 384]
    LC = [(hC, 0), (hC, 128)] + [(hL, a_) for a_ in W512]
    gemm_fm(I["w_in"], MLO, 512, 8, hL, lambda m: [(0, 512)], lambda m, g, pv, t: scopy(q[:, m, :], pv, [t]))
    gemm_fm(I["w_in"], MLO + 512, 512, 8, (hL, hC), lambda m: SEGS,
            lambda m, g, pv, t: scopy(kx[:, m, 512 * g:512 * g + SEGS[g][1]], pv[:, 0:SEGS[g][1]], [t],
                                      scale=128 ** -0.5))
    gemm_tm(I["w_in"], MLO + 1024, 512, 8, None, LC,
            lambda c, i, pv, t, n: vcopy(v1[:, i, :, 0:128], view(pv, [128, 4], [1, 128]), [t]))
    gemm_tm(I["w_in"], MLO + 1536, 512, 8, None, LC[2:],
            lambda c, i, pv, t, n: act(og[:, i, :], pv, ACT.Sigmoid, w=[t]))
    gemm_tm(I["w_in"], MLO + 2048, 16, 8, None, LC,
            lambda c, i, pv, t, n: vtt(gates[:, i, :], pv[:, 0:16], gb, ADD, [t, t_gb]))
    g4 = view(gates, [16, 6], [8, 2], [1, 8])
    IG = view(al(48), [8, 6], [4, 2], [1, 4])
    LF = view(al(48), [8, 6], [4, 2], [1, 4])
    tA = view(al(48), [8, 6], [4, 2], [1, 4])
    vcopy(IG, g4[:, :, :, 0:4])
    vcopy(LF, g4[:, :, :, 4:8])
    t = vcopy(tA, LF)
    act(tA, tA, ACT.Abs, w=[t])
    act(tA, tA, ACT.Exp, scale=-1.0)
    t = act(tA, tA, ACT.Ln, bias=1.0)
    vts(LF, LF, 0.0, None, MIN, w=[t])
    t_lf = vtt(LF, LF, tA, SUB)
    lend = borrow()
    lfr, igr, cumr, mr, rsm = (lend(768) for _ in range(5))
    for x in (lfr, igr):
        vset(x, 0.0)
    for d in range(2):
        for X, rw_ in ((LF, lfr), (IG, igr)):
            for half, n in ((0, 4), (4, 2)):
                b, pv, bw = bank()
                for i in range(n):
                    ti = SEQ_[d][half + i]
                    t = mm(pv[32 * d:32 * d + 4, 128 * i:128 * i + 128], X[:, ti, d, :], C["J" if d else "ident"],
                           True, True, bw + [t_lf] if i == 0 else (), i == n - 1)
                t = vcopy(rw_[32 * d:32 * d + 4, 128 * half:128 * (half + n)], pv[32 * d:32 * d + 4, 0:128 * n], [t])
                rel(b, t)
    vcopy(view(rsm, [128, 6], [1, 128]), rep(C["rs128"], 6))
    scan(mr[0:64], lfr[0:64], igr[0:64], ADD, MAX)
    scan(cumr[0:64], rsm[0:64], lfr[0:64], MUL, ADD)
    t_R = vtt(cumr[0:64], cumr[0:64], mr[0:64], SUB)
    Rn = lend(512)
    t = vset(Rn, 0.0)
    em = view(lend(4 * 8), [8, 4], [1, 8])
    id4 = C["ident"]
    cR = view(lend(4 * 8), [8, 4], [1, 8])
    vcopy(Rn[0:4, :], cumr[0:4, 256:768])
    b, pv, bw = bank()
    for i in range(4):
        t = mm(pv[:, 4 * i:4 * i + 4], mr[0:4, 256 + 128 * i:384 + 128 * i], id4[0:4, 0:4], True, True,
               bw + [t_R] if i == 0 else (), i == 3)
    t = vcopy(em[:, :, 0:4], view(pv, [4, 4], [1, 4]), [t])
    rel(b, t)
    b, pv, bw = bank()
    for i in range(4):
        ps = 3 - i
        for j, X in enumerate((cumr, mr)):
            t = mm(pv[:, 8 * i + 4 * j:8 * i + 4 * j + 4], X[32:36, 256 + 128 * ps:384 + 128 * ps], id4[32:36, 32:36],
                   True, True, bw + [t_R] if i + j == 0 else (), i == 3 and j == 1)
    t_cR = vcopy(cR, view(pv, [8, 4], [1, 8]), [t])
    rel(b, t_cR)
    b, pv, bw = bank()
    b2_, pv2, bw2 = bank()
    for i in range(4):
        mm(pv[:, 4 * i:4 * i + 4], C["J"], cR[:, i, 4:8], True, True, bw + [t_cR] if i == 0 else ())
        t = mm(pv2[32:36, 128 * i:128 * i + 128], cR[:, i, 0:4], C["J"], True, True, bw2 if i == 0 else (), i == 3)
    t1 = vcopy(em[:, :, 4:8], view(pv, [4, 4], [1, 4]), [t])
    rel(b, t1)
    t_Rn = vcopy(Rn[32:36, :], pv2[32:36, :], [t])
    rel(b2_, t_Rn)
    t_em = act(em, em, ACT.Exp, scale=-1.0, w=[t1])
    bias = view(lend(36 * 4), [4, 36], [1, 4])
    pair = {}
    b, pv, bw = bank()
    n_p = 0
    for d in range(2):
        for a in range(2, 6):
            for s_ in range(a + 1):
                T_, S_ = SEQ_[d][a], SEQ_[d][s_]
                pair[d, T_, S_] = n_p
                o = pv[:, 4 * n_p:4 * n_p + 4]
                if s_ == a:
                    terms = [(C["nUI128"] if d == 0 else C["nLI128"], S_)]
                else:
                    terms = [(C["LS128"] if d == 0 else C["US128"], S_)] + [(C["ones"], SEQ_[d][m_]) for m_ in range(s_ + 1, a)]
                for e, (mat, ti) in enumerate(terms):
                    t = mm(o, mat, LF[:, ti, d, :], e == 0, e == len(terms) - 1, bw + [t_lf] if n_p + e == 0 else (),
                           n_p == 35 and e == len(terms) - 1)
                n_p += 1
    for (d, T_, S_), n_ in pair.items():
        tb = vtt(bias[:, n_, :], pv[:, 4 * n_:4 * n_ + 4], IG[:, S_, d, :], ADD, [t])
    rel(b, tb)
    t_bias = tb
    Hm = view(lend(4 * 512), [512, 4], [1, 512])
    QK = view(lend(6 * 512), [512, 6], [1, 512])
    EE = view(lend(2 * 6 * 512), [6 * 512, 2], [512, 6], [1, 512])
    dn = al(16)
    ee_free = [(), ()]
    qk_free = ()
    for h in range(4):
        tq = None
        for s_ in range(6):
            kc = KT[s_]
            b, pv, bw = bank()
            t = mm(pv, kx[:, h, kc:kc + 128], q[:, h, :], True, True, bw, True)
            tq = scopy(QK[:, s_, :], pv, [t] + list(qk_free))
            rel(b, tq)
        for d in range(2):
            E_ = EE[:, d]
            b, pv, bw = bank()
            b2_, pv2, bw2 = bank()
            mm(pv, C[f"sel{d}{h}"][0:64], Rn[0:64], True, True, bw + [t_Rn])
            mm(pv2, C[f"sel{d}{h}"][0:64], Rn[0:64], True, False, bw2)
            t = mm(pv2, C["ident"], rep(C["negGT" if d == 0 else "negLT"], 4), False, True, (), True)
            for (dd, T_, S_), n_ in pair.items():
                if dd != d:
                    continue
                c0 = 128 * (T_ - 2)
                src = (pv2 if S_ == T_ else pv)[:, c0:c0 + 128]
                te = act(E_[:, S_, c0:c0 + 128], src, ACT.Exp, bias=bias[:, n_, h:h + 1],
                         w=[t, t_bias] + list(ee_free[d]))
            rel(b, te)
            rel(b2_, te)
            for S_ in range(6):
                if S_ < 2:
                    lo, hi = 0, 512
                elif d == 0:
                    lo, hi = 128 * (S_ - 2), 512
                else:
                    lo, hi = 0, 128 * (S_ - 1)
                te2 = vtt(E_[:, S_, lo:hi], E_[:, S_, lo:hi], QK[:, S_, lo:hi], MUL, [te, tq])
            qk_free = (te2,)
            for a in range(2, 6):
                T_ = SEQ_[d][a]
                c0 = 128 * (T_ - 2)
                b, pv, bw = bank()
                ks = SEQ_[d][0:a + 1]
                for e, S_ in enumerate(ks):
                    t = mm(pv[:, 0:129], E_[:, S_, c0:c0 + 128], v1[:, S_, h, :], e == 0, e == len(ks) - 1,
                           bw + [te2] if e == 0 else (), e == len(ks) - 1)
                vts(dn[:, 0:1], pv[:, 128:129], -1.0, em[:, T_ - 2, 4 * d + h:4 * d + h + 1], MUL, MAX, w=[t, t_em])
                vtt(dn[:, 0:1], dn[:, 0:1], pv[:, 128:129], MAX)
                recip(dn[:, 1:2], dn[:, 0:1])
                ho = Hm[:, T_ - 2, 128 * h:128 * h + 128]
                if d == 0:
                    tv = vts(ho, pv[:, 0:128], dn[:, 1:2], None, MUL)
                else:
                    tv = stt(ho, pv[:, 0:128], dn[:, 1:2], ho, MUL, ADD)
                rel(b, tv)
            ee_free[d] = (t,)
    barrier()
    nwr = lend(512)
    t_nw = load_small(nwr, row(I["ml_nw"][0, :], 512))
    sqs = EE[:, 0, 0, :]
    for i in range(4):
        x_ = Hm[:, i, :]
        group_norm(x_, 4, 128, 1e-5, small, sqs, True)
        vtt(x_, x_, nwr, MUL, [t_nw])
        t = vtt(x_, x_, og[:, i, :], MUL)
    to_fm([Hm[:, i, :] for i in range(4)], 4, lambda f: ycT[:, f, :], None, [t])
    ring_back(barrier())
    top[0] = mk

    rT = yaT
    kT = view(al(4 * TW), [TW, 4], [1, TW])
    lo3 = view(al(3 * TW), [TW, 3], [1, TW])
    vt = view(al(6 * 512), [512, 6], [1, 512])
    bonus = view(al(32), [8, 4], [1, 8])
    cm = al(15)
    kam = al(4)
    mk2 = top[0]
    ub = view(al(2 * 772), [772, 2], [1, 772])
    vv = tmp_op[:, 0:TW]
    t_ub = vset(ub, 0.0)
    vts(cm, VC["mup"], -1.0, 1.0, MUL, ADD)
    vtt(cm, cm, VC["mun"], SUB)
    t_km = vts(kam, VC["ka"], -1.0, 1.0, MUL, ADD)
    ub_free = [(t_ub,), (t_ub,)]
    vv_free = [()]

    def shift(m, o, n):
        u = ub[:, m % 2, :]
        vts(o, u[:, 1:1 + n], cm[:, m:m + 1], None, MUL)
        stt(o, u[:, 0:n], VC["mup"][:, m:m + 1], o, MUL, ADD)
        t = stt(o, u[:, 2:2 + n], VC["mun"][:, m:m + 1], o, MUL, ADD)
        ub_free[m % 2] = (t,)
        return t

    def ev_u(m, g, pv, t):
        n = 512 if g == 0 else 256
        o = ub[:, m % 2, 1:513] if g == 0 else ub[:, m % 2, 515:771]
        tc = scopy(o, pv[:, 0:n], [t] + list(ub_free[m % 2]))
        if m < 4:
            V.wait([tc])
            shift(m, rT[:, m, :], 512)
        elif g == 1:
            V.wait([tc])
            if m < 8:
                f = m - 4
                o = kT[:, f, :]
                shift(m, o, TW)
            elif m < 12:
                f = m - 8
                tv = V.op(lambda: nc.vector.memset(vv[:, 0:1], 0.0), vv_free[0])
                tv = shift(m, vv, TW)
                for q0, n in ((0, 4), (4, 2)):
                    b1, p1, w1 = bank()
                    for i in range(n):
                        a = TO[q0 + i]
                        tm = tr(p1[:, 128 * i:128 * i + 128], vv[:, a:a + 128], w1 + [tv] if i == 0 else (), i == n - 1)
                    ta = scopy(vt[:, q0:q0 + n, 128 * f:128 * f + 128], view(p1, [128, n], [1, 128]), [tm])
                    rel(b1, ta)
                vv_free[0] = (tm,)
            else:
                o = lo3[:, m - 12, :]
                ts_ = shift(m, o, TW)
                if m == 12:
                    act(o, o, ACT.Tanh, w=[ts_])
                if m == 14:
                    act(o, o, ACT.Sigmoid, w=[ts_])
        return tc
    gemm_fm(I["w_in"], 0, 1920, 8, (hL, hC), lambda m: SEGS[0:1] if m < 4 else SEGS, ev_u)
    b, pv, bw = bank()
    for f in range(4):
        rk = ub[:, f % 2, 0:512]
        vtt(rk, rT[:, f, :], kT[:, f, 0:512], MUL, ub_free[f % 2])
        tv = vts(rk, rk, VC["rk"][:, f:f + 1], None, MUL)
        for i in range(4):
            t = mm(pv[:, 8 * i + 2 * f:8 * i + 2 * f + 2], rk[:, 128 * i:128 * i + 128], C["b2"][:, 0:2], True, True,
                   bw + [tv] if i == 0 else (), i == 3)
        ub_free[f % 2] = (t,)
    t = vcopy(bonus, view(pv, [8, 4], [1, 8]), [t])
    rel(b, t)
    lend = borrow()
    top[0] = mk2
    top_, top[0] = top[0], mk_c
    kkT = view(al(4 * TW), [TW, 4], [1, TW])
    w2s, a2s = al(504 + 8), lend(512)
    assert top[0] <= mk
    top[0] = top_
    t_w2 = load_small(w2s, I["rw_w2"].rearrange("l d k c -> (l d k) c"))
    t_a2 = load_small(a2s, I["rw_a2"].rearrange("l d k c -> (l d k) c"))
    sqk = lend(TW)
    for f in range(4):
        o = kT[:, f, :]
        kr = kkT[:, f, :]
        vts(kr, o, VC["kk"][:, f:f + 1], None, MUL)
        tk_ = vtt(sqk, kr, kr, MUL)
        b1, p1, w1 = bank()
        b2, p2, w2 = bank()
        mm(p1, C["blk"], sqk[:, 0:512], True, True, w1 + [tk_])
        tm = mm(p2[:, 0:TW - 512], C["blk"], sqk[:, 512:TW], True, True, w2, True)
        act(sqk[:, 0:512], p1, ACT.Sqrt, w=[tm])
        ta = act(sqk[:, 512:TW], p2[:, 0:TW - 512], ACT.Sqrt)
        rel(b1, ta)
        rel(b2, ta)
        vts(sqk, sqk, 1e-12, None, MAX, w=[ta])
        recip(sqk, sqk)
        vtt(kr, kr, sqk, MUL)
    barrier()

    lend = borrow()
    lend(512)
    Ya = view(lend(4 * 512), [512, 4], [1, 512])
    rsw = lend(512)
    Sg, La, Ep, En, Aa = (view(lend(512), [128, 4], [1, 128]) for _ in range(5))
    KKp, Rp, Bn, Kn = (view(lend(512), [128, 4], [1, 128]) for _ in range(4))
    Bt, Kt_ = lend(512), lend(512)
    AkT, BbT, BkT, TTm, Tm, ATm, Xm = ([view(lend(512), [128, 4], [1, 128]) for _ in range(2)] for _ in range(7))
    St = [lend(512) for _ in range(2)]
    PCM = view(al(512), [128, 4], [1, 128])
    Xs, Us = lend(512), lend(512)
    vcopy(view(rsw, [128, 4], [1, 128]), rep(C["rs64"], 4))
    for d in range(2):
        vset(St[0], 0.0)
        cur = 0
        for pos in range(6):
            ti = SEQ_[d][pos]
            a0_ = TO[ti]
            lat = ti >= 2
            barrier()
            b, pv, bw = bank()
            b2, pv2, bw2 = bank()
            for f in range(4):
                mm(pv[:, 128 * f:128 * f + 128], w2s[64 * d:64 * d + 64, 128 * f:128 * f + 128],
                   lo3[64 * d:64 * d + 64, 0, a0_:a0_ + 128], True, True, bw + [t_w2] if f == 0 else ())
            for f in range(4):
                t = mm(pv2[:, 128 * f:128 * f + 128], a2s[64 * d:64 * d + 64, 128 * f:128 * f + 128],
                       lo3[64 * d:64 * d + 64, 1, a0_:a0_ + 128], True, True, bw2 + [t_a2] if f == 0 else (), f == 3)
            for f in range(4):
                act(Sg[:, f, :], pv[:, 128 * f:128 * f + 128], ACT.Sigmoid, bias=VC["w0"][:, 4 * d + f:4 * d + f + 1], w=[t])
            for f in range(4):
                t = act(Aa[:, f, :], pv2[:, 128 * f:128 * f + 128], ACT.Sigmoid, bias=VC["a0"][:, 4 * d + f:4 * d + f + 1])
            rel(b, t)
            rel(b2, t)
            c8 = lambda x: view(x[:, 0, 0:1], [64, 8], [1, 64])
            last = view(La[:, 0, 63:64], [64, 8], [0, 64])
            flat = lambda x: view(x[:, 0, 0:1], [1, 512])
            tl = scan(flat(La), rsw, flat(Sg), MUL, ADD, [t])
            if d == 1:
                vtt(c8(Ep), last, c8(La), SUB)
                tl = vtt(c8(La), c8(Ep), c8(Sg), ADD)
            te = act(flat(Ep), flat(La), ACT.Exp, scale=-KAP, w=[tl])
            te = act(flat(En), flat(La), ACT.Exp, scale=KAP)
            tl = vtt(flat(La), flat(La), flat(Sg), SUB, [te])
            te = act(flat(La), flat(La), ACT.Exp, scale=-KAP, w=[tl])
            ksl, kks = kT[:, :, a0_:a0_ + 128], kkT[:, :, a0_:a0_ + 128]
            t_kk = vtt(KKp, kks, La, MUL, [te])
            if lat:
                vtt(Rp, rT[:, :, a0_:a0_ + 128], Ep, MUL)
            vtt(Bn, kks, Aa, MUL)
            stt(Bn, Bn, -1.0, En, MUL, MUL)
            for f in range(4):
                vts(Aa[:, f, :], Aa[:, f, :], VC["ka"][:, f:f + 1], kam[:, f:f + 1], MUL, ADD)
            vtt(Kn, ksl, Aa, MUL)
            t_k = vtt(Kn, Kn, En, MUL)
            for src, dst in ((Bn, Bt), (Kn, Kt_)):
                b, pv, bw = bank()
                for f in range(4):
                    t = tr(pv[:, 128 * f:128 * f + 128], src[:, f, :], bw + [t_k] if f == 0 else (), f == 3)
                t_tok = scopy(dst, pv, [t])
                rel(b, t_tok)
            m0, n0 = (C["M0"], C["N0"]) if d == 0 else (C["N0"], C["M0"])
            strict, incl = (C["US"], C["UI"]) if d == 0 else (C["LS"], C["LI"])
            groups = []
            for g in range(2):
                hp = slice(64 * g, 64 * g + 64)

                def outer(l, r, w=()):
                    b, pv, bw = bank()
                    for i in range(4):
                        t = mm(pv[:, 128 * i:128 * i + 128], l[hp, i, :], r[hp, i, :], True, True,
                               bw + list(w) if i == 0 else (), i == 3)
                    return b, view(pv, [128, 4], [1, 128]), t
                vcopy(Tm[g], rep(C["ident"], 4))
                vcopy(TTm[g], rep(C["ident"], 4))
                b, pm, t = outer(KKp, Bn, [t_k])
                t1 = cpred(Tm[g], rep(m0, 4).bitcast(U32), pm, [t])
                rel(b, t1)
                b, pm, t = outer(Bn, KKp)
                t1 = cpred(TTm[g], rep(n0, 4).bitcast(U32), pm, [t])
                t2 = scopy(ATm[g], pm, [t1])
                rel(b, t2)
                groups.append((Tm[g], TTm[g], ATm[g], [t1, t2], Xm[g]))
                b, pm, t = outer(Kn, KKp)
                t1 = vtt(AkT[g], pm, rep(strict, 4), MUL, [t])
                rel(b, t1)
                if lat:
                    b, pm, t = outer(Bn, Rp)
                    t1 = vtt(BbT[g], pm, rep(incl, 4), MUL, [t])
                    rel(b, t1)
                    b, pm, t = outer(Kn, Rp)
                    t1 = vtt(BkT[g], pm, rep(incl, 4), MUL, [t])
                    rel(b, t1)
                t_mat = t1
            tinv = invert(groups, d == 0)
            w_inv = [x for ts_ in tinv for x in ts_] + [t_mat, t_tok]
            for p in ((0, 1) if d == 0 else (1, 0)):
                r_ = slice(64 * p, 64 * p + 64)
                edge = 64 * p + 63 if d == 0 else 64 * p
                S0, S1 = St[cur], St[1 - cur]
                b, pv, bw = bank()
                for i in range(4):
                    o = pv[r_, 128 * i:128 * i + 128]
                    mm(o, KKp[:, i, r_], S0[:, 128 * i:128 * i + 128], True, False,
                       bw + w_inv + [(V, V.n)] if i == 0 else ())
                    for g in range(2):
                        c_ = 128 * i + 64 * g
                        t = mm(pv[r_, c_:c_ + 64], AkT[g][r_, i, r_], vt[r_, ti, c_:c_ + 64], False, g == 1,
                               (), i == 3 and g == 1)
                t = vcopy(Xs[r_, :], pv[r_, :], [t])
                rel(b, t)
                b, pv, bw = bank()
                for i in range(4):
                    for g in range(2):
                        c_ = 128 * i + 64 * g
                        t = mm(pv[r_, c_:c_ + 64], TTm[g][r_, i, r_], Xs[r_, c_:c_ + 64], True, True,
                               bw + [t] if i + g == 0 else (), i == 3 and g == 1)
                tu = scopy(Us[r_, :], pv[r_, :], [t])
                rel(b, tu)
                b, pv, bw = bank()
                for i in range(4):
                    f_ = slice(128 * i, 128 * i + 128)
                    mm(pv[:, f_], Bt[r_, f_], Us[r_, f_], True, False, bw + [tu] if i == 0 else ())
                    t = mm(pv[:, f_], Kt_[r_, f_], vt[r_, ti, f_], False, True, (), i == 3)
                vtt(PCM, view(Ep[:, 0, edge:edge + 1], [128, 4], [0, 128]), rep(C["blk"], 4), MUL)
                vtt(S1, S0, pv, ADD, [t])
                ts_ = vtt(view(S1, [128, 4], [1, 128]), view(S1, [128, 4], [1, 128]), PCM, MUL)
                rel(b, ts_)
                if lat:
                    b, pv, bw = bank()
                    for i in range(4):
                        mm(pv[r_, 128 * i:128 * i + 128], Rp[:, i, r_], S0[:, 128 * i:128 * i + 128], True, False,
                           bw if i == 0 else ())
                        for g in range(2):
                            c_ = 128 * i + 64 * g
                            mm(pv[r_, c_:c_ + 64], BbT[g][r_, i, r_], Us[r_, c_:c_ + 64], False, False)
                            t = mm(pv[r_, c_:c_ + 64], BkT[g][r_, i, r_], vt[r_, ti, c_:c_ + 64], False, g == 1,
                                   (), i == 3 and g == 1)
                    y_ = Ya[r_, ti - 2, :]
                    t = vcopy(y_, pv[r_, :], [t]) if d == 0 else vtt(y_, y_, pv[r_, :], ADD, [t])
                    rel(b, t)
                cur = 1 - cur
    barrier()
    g2s, lw_, lb_ = KKp, Bt, Kt_
    lw_, lb_ = Bt, Kt_
    g2f = view(KKp[:, 0, 0:1], [1, 512])
    t_l = [load_small(g2f, I["rw_g2"][0]), load_small(lw_, row(I["rw_lnw"][0, :], 512)),
           load_small(lb_, row(I["rw_lnb"][0, :], 512))]
    bv = view(Rp[:, 0, 0:1], [1, 512])
    for i in range(4):
        y_ = Ya[:, i, :]
        group_norm(y_, 8, 64, 64e-5, small, Xs, True)
        vtt(y_, y_, lw_, MUL, t_l)
        vtt(y_, y_, lb_, ADD)
        vtt(view(bv, [64, 8], [1, 64]), view(vt[:, 2 + i, :], [64, 8], [1, 64]), view(bonus[:, i, :], [1, 8], [0, 64]), MUL)
        vtt(y_, y_, bv, ADD)
        b, pv, bw = bank()
        t = mm(pv, lo3[:, 2, 128 * i:128 * i + 128], g2f, True, True, bw + t_l, True)
        t = vtt(y_, y_, pv, MUL, [t])
        rel(b, t)
    to_fm([Ya[:, i, :] for i in range(4)], 4, lambda f: yaT[:, f, :], None, [t])
    ring_back(barrier())
    top[0] = mk_c

    ybT = view(al(4 * 512), [512, 4], [1, 512])
    mk = top[0]
    z = view(al(4 * 8 * 94), [8 * 94, 4], [94, 8], [1, 94])
    cga = view(al(4 * 512), [512, 4], [1, 512])
    t_z = vset(z, 0.0)

    def ev_a(m, g, pv, t):
        return scopy(cga[:, m, :], pv, [t])

    def ev_g(m, g, pv, t):
        t = act(sq4[:, m, :], pv, ACT.Sigmoid, w=[t])
        t1 = vtt(z[:, m, :, 15:79], view(cga[:, m, :], [64, 8], [1, 64]), view(sq4[:, m, :], [64, 8], [1, 64]), MUL, [t])
        return t1
    sq4 = view(al(4 * 512), [512, 4], [1, 512])
    gemm_fm(I["w_in"], CVO, 512, 8, hL, lambda m: [(0, 512)], ev_a)
    gemm_fm(I["w_in"], CVO + 512, 512, 8, hL, lambda m: [(0, 512)], ev_g)
    cacc = view(al(4 * 512), [512, 4], [1, 512])
    for f in range(4):
        o = view(cacc[:, f, :], [64, 8], [1, 64])
        cd = VC["cdw"][:, 31 * f:31 * f + 31]
        vts(o, z[:, f, :, 0:64], cd[:, 0:1], VC["cdb"][:, f:f + 1], MUL, ADD)
        for k in range(1, 31):
            t = stt(o, z[:, f, :, k:k + 64], cd[:, k:k + 1], o, MUL, ADD)
    b, pv, bw = bank()
    for f in range(4):
        t = mm(pv, C["ones"], cacc[:, f, :], f == 0, f == 3, bw + [t] if f == 0 else (), f == 3)
    mean = cga[:, 0, :]
    t = scopy(mean, pv, [t], scale=1.0 / 512)
    rel(b, t)
    t = vtt(cacc, cacc, rep(mean, 4, 512), SUB, [t])
    t = vtt(sq4, cacc, cacc, MUL)
    b, pv, bw = bank()
    for f in range(4):
        t = mm(pv, C["ones"], sq4[:, f, :], f == 0, f == 3, bw + [t] if f == 0 else (), f == 3)
    rs = cga[:, 1, :]
    t = vts(rs, pv, 1.0 / 512, 1e-5, MUL, ADD, w=[t])
    rel(b, t)
    t = act(rs, rs, ACT.Sqrt, w=[t])
    t = recip(rs, rs, [t])
    t = vtt(cacc, cacc, rep(rs, 4, 512), MUL)
    for f in range(4):
        act(ybT[:, f, :], cacc[:, f, :], ACT.Silu, scale=VC["clw"][:, f:f + 1], bias=VC["clb"][:, f:f + 1], w=[t])
    barrier()
    top[0] = mk

    mrow = al(1024)
    bcast_rows(mrow, 2)
    mg = view(al(4 * 1024), [1024, 4], [1, 1024])
    sg = view(al(4 * 512), [512, 4], [1, 512])
    mk4 = top[0]
    yop = opnd(4, 512)
    for br, (y_, pw) in enumerate(((yaT, "p_a"), (ybT, "p_b"), (ycT, "p_c"))):
        yt = None
        for hf in range(2):
            gemm_tm(I["w_in"], GO + 1024 * br + 512 * hf, 512, 8, hL, W512,
                    lambda c, i, pv, t, n: act(sg[:, i, :], pv, ACT.Sigmoid, w=[t, (V, V.n)]))
            if hf == 0:
                yt = split_x(y_, yop, [(P, P.n)])

            def ev_m(c, i, pv, t, n, br=br, hf=hf):
                o = mg[:, i, 512 * hf:512 * hf + 512]
                if br == 0:
                    return vtt(o, sg[:, i, :], pv, MUL, [t, (S, S.n)])
                t1 = vtt(sg[:, i, :], sg[:, i, :], pv, MUL, [t, (S, S.n)])
                vtt(o, o, sg[:, i, :], ADD)
                return t1
            gemm_tm(I[pw], 512 * hf, 512, 4, yop, W512, ev_m, yt)
    top[0] = mk4
    x1 = view(al(4 * 1024), [1024, 4], [1, 1024])
    tx = [load_small(x1[:, i, :], I["x"][0, 128 * i:128 * i + 128, :], [(P, P.n)]) for i in range(4)]
    t = to_op([mg[:, i, :] for i in range(4)], 8, hL, w=[(V, V.n)])

    def ev_o(c, i, pv, t, n):
        o = mg[:, i, c:c + 512]
        t1 = vtt(o, pv, mrow[:, c:c + 512], MUL, [t])
        vtt(x1[:, i, c:c + 512], x1[:, i, c:c + 512], o, ADD, tx)
        return t1
    gemm_tm(I["w_out"], 0, 1024, 8, hL, W512, ev_o, xt=t)
    barrier()
    top[0] = mk_y
    x1b = view(al(4 * 1024), [1024, 4], [1, 1024])
    xc = view(al(4 * 1024), [1024, 4], [1, 1024])
    mk3 = top[0]
    scr = al(1024)
    vcopy(x1b, x1)
    barrier()
    x1 = x1b
    t = vcopy(xc, x1)
    norm_mod_op([xc[:, i, :] for i in range(4)], 0, sc2, mod[:, 24:32, :], hL, scr, [[t]] * 4)
    barrier()
    top[0] = mk3 - 4096
    mrow = al(1024)
    bcast_rows(mrow, 5)
    hop = opnd(8, 512)
    tmp = al(2048)
    for part in range(4):
        ht = []

        def ev_1(m, g, pv, t):
            o = tmp[:, 512 * (m % 2):512 * (m % 2) + 512]
            o2 = tmp[:, 1024 + 512 * (m % 2):1536 + 512 * (m % 2)]
            t1 = act(o, pv, ACT.Relu, w=[t, (V, V.n)])
            t2 = vtt(o2, o, o, MUL, [t1])
            t3 = act(R(hop[:, 0, m, :]), o2, ACT.Copy, w=[t2, free_h])
            ht.append(vtt(R(hop[:, 1, m, :]), o2, R(hop[:, 0, m, :]), SUB, [t3]))
            return t1
        free_h = (P, P.n)
        gemm_fm(I["w_mlp1"], 1024 * part, 1024, 8, hL, lambda m: [(0, 512)], ev_1)

        def ev_2(c, i, pv, t, n):
            o = tmp[:, 512 * (i % 2):512 * (i % 2) + 512]
            t1 = vtt(o, pv, mrow[:, c:c + 512], MUL, [t])
            vtt(x1[:, i, c:c + 512], x1[:, i, c:c + 512], o, ADD)
            return t1
        gemm_tm(I["w_mlp2"], 0, 1024, 8, hop, W512, ev_2, r0=1024 * part, xt=ht)
    barrier()
    top[0] = mk3 - 4096
    gfr = al(1024)
    scr = al(1024)
    t_g = load_small(gfr, row(I["g_final"], 1024))
    for i in range(4):
        t = rms_scales(small[:, i:i + 1], x1[:, i, :], scr, [(V, V.n)])
        stt(x1[:, i, :], x1[:, i, :], small[:, i:i + 1], gfr, MUL, MUL, [t, t_g])
    barrier()

    hX = x1
    hh = hL
    top[0] = mk_y + 4096
    cosT, sinT = al(512), al(512)
    base = top[0]
    ALPHA = 4.0 ** 0.25
    RP = slice(64, 96)

    pos_i = al(512).bitcast(I32)
    ang, kk_, wk = al(512), al(512), al(512)
    t = load_small(pos_i[RP, :], bass.AP(I["positions_2"].tensor, 0, [[0, 32], [1, 512]]))
    vcopy(ang[RP, :], pos_i[RP, :], [t])
    vts(ang[RP, :], ang[RP, :], C["rope"][RP, 0:1], None, MUL)
    MAGIC = 12582912.0
    C1 = 6.28125
    C2 = float(np.float32(2 * np.pi - C1))
    C3 = float(2 * np.pi - C1 - np.float64(np.float32(2 * np.pi - C1)))
    for dst, ph in ((sinT, 0.0), (cosT, 0.25)):
        k_, w_ = kk_[RP, :], wk[RP, :]
        vts(k_, ang[RP, :], 1.0 / (2 * np.pi), ph, MUL, ADD)
        vts(k_, k_, MAGIC, None, ADD)
        vts(k_, k_, MAGIC, None, SUB)
        stt(w_, k_, -C1, ang[RP, :], MUL, ADD, [(S, S.n)])
        stt(w_, k_, -C2, w_, MUL, ADD)
        stt(w_, k_, -C3, w_, MUL, ADD)
        if ph:
            vts(w_, w_, float(np.pi / 2), None, ADD)
        vts(w_, w_, 3.1415925, -3.1415925, MIN, MAX)
        act(dst[RP, :], w_, ACT.Sin, w=[(V, V.n)])
    vts(sinT[RP, :], sinT[RP, :], C["rope"][RP, 1:2], None, MUL, w=[(S, S.n)])
    barrier()
    top[0] = base

    def hT_from_x():
        t = to_op([hX[:, i, :] for i in range(4)], 8, hh, w=[(V, V.n), (P, P.n)])
        P.wait(t)
        return t

    def layer_norm_all(l, j):
        m_ = top[0]
        gr, br_ = al(1024), al(1024)
        e = barrier()
        tg = [load_small(gr, row(I["ln_g_2"][l, j, :], 1024)), load_small(br_, row(I["ln_b_2"][l, j, :], 1024))]
        for i in range(4):
            x_ = hX[:, i, :]
            layer_norm_tile(x_, x_, 1024, 1e-5, small)
            vtt(x_, x_, gr, MUL, tg)
            vtt(x_, x_, br_, ADD)
        t = hT_from_x()
        barrier()
        top[0] = m_
        return t

    def ffn(l, wi, wo, j):
        m_ = top[0]
        hop = opnd(8, 512)
        tmp = al(2048)
        Wi, Wo = I[wi][l], I[wo][l]
        for part, nt in enumerate((8, 8, 6)):
            ht = []
            free_h = (P, P.n)
            for m in range(nt):
                c_ = 1024 * part + 128 * m
                z, wh, wl, tok = wload([
                    (lambda x: view(x, [256, 8], [1, 128]), Wi[:, c_:c_ + 128].rearrange("(k p) c -> p k c", p=128)),
                    (lambda x: view(x[:, 128:256], [256, 8], [1, 128]),
                     Wi[:, 2816 + c_:2816 + c_ + 128].rearrange("(k p) c -> p k c", p=128))], 2048)
                wh, wl = view(wh, [256, 8], [1, 256]), view(wl, [256, 8], [1, 256])
                b, pv, bw = bank()
                b2, pv2, bw2 = bank()
                for u_, (o_, w_) in enumerate(((pv, bw), (pv2, bw2))):
                    js = slice(128 * u_, 128 * u_ + 128)
                    for k in range(8):
                        t = mm3(o_, (wh[:, k, js], wl[:, k, js]), (R(hh[:, 0, k, :]), R(hh[:, 1, k, :])), k == 0, k == 7,
                                w_ + [tok] if k == 0 else (), k == 7)
                used(z, t)
                o = tmp[:, 512 * (m % 2):512 * (m % 2) + 512]
                o2 = tmp[:, 1024 + 512 * (m % 2):1536 + 512 * (m % 2)]
                t1 = act(o, pv, ACT.Silu, w=[t, (V, V.n)])
                rel(b, t1)
                t2 = vtt(o2, o, pv2, MUL, [t1])
                rel(b2, t2)
                t3 = act(R(hop[:, 0, m, :]), o2, ACT.Copy, w=[t2, free_h])
                ht.append(vtt(R(hop[:, 1, m, :]), o2, R(hop[:, 0, m, :]), SUB, [t3]))

            def ev(c, i, pv, t, n, part=part):
                o = tmp[:, 512 * (i % 2):512 * (i % 2) + 512]
                x_ = hX[:, i, c:c + 512]
                if part == 0:
                    t1 = act(o, pv, ACT.Copy, scale=0.5, w=[t, (V, V.n)])
                    stt(x_, x_, ALPHA, o, MUL, ADD, [t1])
                else:
                    t1 = stt(x_, pv, 0.5, x_, MUL, ADD, [t])
                return t1
            gemm_tm(Wo, 0, 1024, nt, hop, W512, ev, r0=1024 * part, xt=ht)
        barrier()
        top[0] = m_
        layer_norm_all(l, j)

    def mixer(l):
        m0_ = top[0]
        Wm = I["mix_w_in_2"][l]
        m1_ = top[0]
        qk = view(al(8 * 512), [512, 8], [1, 512])
        vtok = view(al(4 * 512), [512, 4], [1, 512])
        gz = view(al(4 * 512), [512, 4], [1, 512])
        gab = view(al(4 * 16), [16, 4], [1, 16])
        ktok = view(al(4 * 512), [512, 4], [1, 512])
        m2_ = top[0]
        ub = view(al(2 * 516), [516, 2], [1, 516])
        cv = view(al(2 * 512), [512, 2], [1, 512])
        sq_, rn = al(512), al(512)
        t0 = vset(ub, 0.0)
        ubf = [(t0,), (t0,)]
        cvf = [(), ()]
        cw = VC[f"gcw{l}"]

        def ev_c(m, g, pv, t):
            u = ub[:, m % 2, :]
            tc = scopy(u[:, 3:515], pv, [t] + list(ubf[m % 2]))
            o = cv[:, m % 2, :]
            vts(o, u[:, 0:512], cw[:, 4 * m:4 * m + 1], None, MUL, w=[tc] + list(cvf[m % 2]))
            for k in range(1, 4):
                tv = stt(o, u[:, k:k + 512], cw[:, 4 * m + k:4 * m + k + 1], o, MUL, ADD)
            ubf[m % 2] = (tv,)
            if m < 8:
                dst = qk[:, m, :]
                ta = act(dst, o, ACT.Silu, w=[tv])
                cvf[m % 2] = (ta,)
                tv = vtt(sq_, dst, dst, MUL, [ta])
                b, p1, bw = bank()
                tm = mm(p1, C["blk"], sq_, True, True, bw + [tv], True)
                ts_ = vts(rn, p1, 1e-6, None, ADD, w=[tm])
                rel(b, ts_)
                ta = act(rn, rn, ACT.Sqrt, w=[ts_])
                recip(rn, rn, [ta])
                if m < 4:
                    stt(dst, dst, 0.125, rn, MUL, MUL)
                else:
                    vtt(dst, dst, rn, MUL)
            else:
                ta = act(o, o, ACT.Silu, w=[tv])
                b, p1, bw = bank()
                for i in range(4):
                    tm = tr(p1[:, 128 * i:128 * i + 128], o[:, 128 * i:128 * i + 128], bw + [ta] if i == 0 else (), i == 3)
                ta = scopy(vtok[:, :, 128 * (m - 8):128 * (m - 8) + 128], view(p1, [128, 4], [1, 128]), [tm])
                rel(b, ta)
                cvf[m % 2] = (tm,)
            return tc
        gemm_fm(Wm, 0, 1536, 8, hh, lambda m: [(0, 512)], ev_c)
        gemm_tm(Wm, 1536, 512, 8, hh, W512, lambda c, i, pv, t, n: act(gz[:, i, :], pv, ACT.Silu, w=[t]))
        gemm_tm(Wm, 2048, 16, 8, hh, W512, lambda c, i, pv, t, n: vcopy(gab[:, i, :], pv[:, 0:16], [t]))
        barrier()
        top[0] = m2_
        al_, dtb = al(8), al(8)
        gg = view(al(32), [8, 4], [1, 8])
        ng = view(al(32), [8, 4], [1, 8])
        be = view(al(32), [8, 4], [1, 8])
        t8 = view(al(32), [8, 4], [1, 8])
        nbe = view(al(32), [8, 4], [1, 8])
        kde = view(al(32), [8, 4], [1, 8])
        egc = view(al(32), [8, 4], [1, 8])
        tl = [load_small(al_, row(I["gdn_a_log_2"][l, :], 8)), load_small(dtb, row(I["gdn_dt_bias_2"][l, :], 8))]
        ta = act(al_, al_, ACT.Exp, w=tl)
        vtt(gg, gab[:, :, 0:8], view(dtb, [0, 4], [1, 8]), ADD, tl)
        t = vcopy(t8, gg)
        act(t8, t8, ACT.Abs, w=[t])
        act(t8, t8, ACT.Exp, scale=-1.0)
        ta2 = act(t8, t8, ACT.Ln, bias=1.0)
        vts(gg, gg, 0.0, None, MAX)
        vtt(gg, gg, t8, ADD, [ta2])
        stt(gg, gg, -1.0, view(al_, [0, 4], [1, 8]), MUL, MUL, [ta])
        t = vts(ng, gg, -1.0, None, MUL)
        t = act(be, gab[:, :, 8:16], ACT.Sigmoid, w=[t])
        b, pv, bw = bank()
        mm(pv[:, 0:32], C["UI"], view(gg, [1, 32]), True, True, bw + [(V, V.n)])
        t = mm(pv[:, 32:64], C["blk"], view(gg, [1, 32]), True, True, (), True)
        act(view(egc, [1, 32]), pv[:, 0:32], ACT.Exp, w=[t])
        tg = scopy(view(t8, [1, 32]), pv[:, 0:32])
        tg = vtt(view(kde, [1, 32]), pv[:, 32:64], view(t8, [1, 32]), SUB, [tg])
        rel(b, tg)
        tg = act(kde, kde, ACT.Exp, w=[tg])
        stt(nbe, be, -1.0, egc, MUL, MUL, [tg])
        nb_ = view(al(32), [8, 4], [1, 8])
        vts(nb_, be, -1.0, None, MUL)
        egl = view(al(64), [8, 8], [1, 8])
        b, pv, bw = bank()
        for c_ in range(8):
            t = mm(pv[:, 8 * c_:8 * c_ + 8], C[f"half{c_ % 2}"], gg[:, c_ // 2, :], True, True,
                   bw + [(V, V.n)] if c_ == 0 else (), c_ == 7)
        t_egl = act(view(egl, [1, 64]), pv[:, 0:64], ACT.Exp, w=[t])
        rel(b, t_egl)
        for i in range(4):
            b, pv, bw = bank()
            for f in range(4):
                t = tr(pv[:, 128 * f:128 * f + 128], qk[:, 4 + f, 128 * i:128 * i + 128], bw if f == 0 else (), f == 3)
            tk_ = vtt(view(ktok[:, i, :], [64, 8], [1, 64]), view(pv, [64, 8], [1, 64]), view(kde[:, i, :], [1, 8], [0, 64]),
                      MUL, [t, tg])
            rel(b, tk_)
            vtt(view(vtok[:, i, :], [64, 8], [1, 64]), view(vtok[:, i, :], [64, 8], [1, 64]),
                view(be[:, i, :], [1, 8], [0, 64]), MUL)
        lend = borrow()
        Og = view(lend(4 * 512), [512, 4], [1, 512])
        Dm, QD, NA, TTm, Tm, ATm, Xm = [[view(lend(512), [128, 4], [1, 128]) for _ in range(2)] for _ in range(7)]
        St = [lend(512) for _ in range(2)]
        PCM = view(lend(512), [64, 8], [1, 64])
        Xs, Us, t1s = lend(512), lend(512), lend(512)
        vset(St[0], 0.0)
        cur = 0
        for ti in range(4):
            cs = slice(128 * ti, 128 * ti + 128)
            barrier()
            groups = []
            for g in range(2):
                hp = slice(64 * g, 64 * g + 64)
                b, pv, bw = bank()
                mm(pv, C["ident"], rep(C["negGD"], 4), True, False, bw + [(V, V.n)])
                for i in range(4):
                    h = 2 * i + g
                    o = pv[:, 128 * i:128 * i + 128]
                    mm(o, C["UI"], view(gg[:, ti, h:h + 1], [0, 128]), False, False)
                    t = mm(o, view(ng[:, ti, h:h + 1], [0, 128]), C["UI"], False, True, (), i == 3)
                td = act(Dm[g], view(pv, [128, 4], [1, 128]), ACT.Exp, w=[t])
                rel(b, td)
                b, pv, bw = bank()
                for i in range(4):
                    t = mm(pv[:, 128 * i:128 * i + 128], qk[hp, 4 + i, cs], qk[hp, 4 + i, cs], True, True,
                           bw if i == 0 else (), i == 3)
                t1 = vtt(NA[g], view(pv, [128, 4], [1, 128]), Dm[g], MUL, [t, td])
                rel(b, t1)
                t1 = vtt(NA[g], NA[g], view(nb_[:, ti, g:g + 1], [2, 4], [0, 128]), MUL)
                b, pv, bw = bank()
                for i in range(4):
                    t = mm(pv[:, 128 * i:128 * i + 128], qk[hp, i, cs], qk[hp, 4 + i, cs], True, True,
                           bw if i == 0 else (), i == 3)
                t2 = vtt(Dm[g], view(pv, [128, 4], [1, 128]), Dm[g], MUL, [t])
                rel(b, t2)
                for src, dst, tt in ((NA[g], ATm[g], t1), (Dm[g], QD[g], t2)):
                    b, pv, bw = bank()
                    for i in range(4):
                        t = tr(pv[:, 128 * i:128 * i + 128], src[:, i, :], bw + [tt] if i == 0 else (), i == 3)
                    tc = scopy(dst, view(pv, [128, 4], [1, 128]), [t])
                    if dst is ATm[g]:
                        t_at = tc
                    rel(b, tc)
                vcopy(Tm[g], rep(C["ident"], 4))
                vcopy(TTm[g], rep(C["ident"], 4))
                cpred(Tm[g], rep(C["M0"], 4).bitcast(U32), NA[g])
                t3 = cpred(TTm[g], rep(C["N0"], 4).bitcast(U32), ATm[g], [t_at])
                groups.append((Tm[g], TTm[g], ATm[g], [t3, tc], Xm[g]))
            tinv = invert(groups, True)
            w_inv = [x for y in tinv for x in y] + [tc]
            for p in (0, 1):
                r_ = slice(64 * p, 64 * p + 64)
                rt = slice(128 * ti + 64 * p, 128 * ti + 64 * p + 64)
                S0, S1 = St[cur], St[1 - cur]
                h8 = lambda x: view(x, [64, 8], [1, 64])
                col = lambda x: view(x[r_, ti, :], [1, 8], [0, 64])
                b, pv, bw = bank()
                for i in range(4):
                    t = mm(pv[r_, 128 * i:128 * i + 128], qk[:, 4 + i, rt], S0[:, 128 * i:128 * i + 128], True, True,
                           bw + w_inv + [(V, V.n)] if i == 0 else (), i == 3)
                vtt(h8(Xs[r_, :]), h8(pv[r_, :]), col(nbe), MUL, [t])
                t = vtt(Xs[r_, :], Xs[r_, :], vtok[r_, ti, :], ADD)
                rel(b, t)
                b, pv, bw = bank()
                for i in range(4):
                    for g in range(2):
                        c_ = 128 * i + 64 * g
                        t = mm(pv[r_, c_:c_ + 64], TTm[g][r_, i, r_], Xs[r_, c_:c_ + 64], True, True,
                               bw + [t] if i + g == 0 else (), i == 3 and g == 1)
                tu = scopy(Us[r_, :], pv[r_, :], [t])
                rel(b, tu)
                b, pv, bw = bank()
                for i in range(4):
                    f_ = slice(128 * i, 128 * i + 128)
                    t = mm(pv[:, f_], ktok[r_, ti, f_], Us[r_, f_], True, True, bw + [tu] if i == 0 else (), i == 3)
                ch = 2 * ti + p
                vtt(PCM, view(egl[:, ch, :], [1, 8], [0, 64]), h8(blkw), MUL, [t_egl])
                vtt(h8(S1), h8(S0), PCM, MUL)
                vtt(t1s, pv, blkw, MUL, [t])
                ts_ = vtt(S1, S1, t1s, ADD)
                rel(b, ts_)
                b, pv, bw = bank()
                b2, pv2, bw2 = bank()
                for i in range(4):
                    mm(pv[r_, 128 * i:128 * i + 128], qk[:, i, rt], S0[:, 128 * i:128 * i + 128], True, True,
                       bw if i == 0 else ())
                for i in range(4):
                    for g in range(2):
                        c_ = 128 * i + 64 * g
                        t = mm(pv2[r_, c_:c_ + 64], QD[g][r_, i, r_], Us[r_, c_:c_ + 64], True, True,
                               bw2 if i + g == 0 else (), i == 3 and g == 1)
                y_ = Og[r_, ti, :]
                vtt(h8(y_), h8(pv[r_, :]), col(egc), MUL, [t])
                t = vtt(y_, y_, pv2[r_, :], ADD)
                rel(b, t)
                rel(b2, t)
                cur = 1 - cur
        barrier()
        top[0] = m1_
        catT = view(al(8 * 512), [512, 8], [1, 512])
        m1_ = top[0]
        nr = lend(64)
        tn = load_small(nr, row(I["gdn_norm_w_2"][l, :], 64))
        for i in range(4):
            y_ = Og[:, i, :]
            group_norm(y_, 8, 64, 1e-6, small, Xs, False)
            vtt(view(y_, [64, 8], [1, 64]), view(y_, [64, 8], [1, 64]), view(nr, [0, 8], [1, 64]), MUL, [tn])
            t = vtt(y_, y_, gz[:, i, :], MUL)
        to_fm([Og[:, i, :] for i in range(4)], 4, lambda f: catT[:, f, :], None, [t])
        ring_back(barrier())
        top[0] = m1_

        sqk_ = view(al(4 * 512), [512, 4], [1, 512])
        sv = view(al(4 * 256), [256, 4], [1, 256])
        mq = view(al(4 * 256), [256, 4], [1, 256])
        ckv = view(al(4 * 128), [128, 4], [1, 128])
        krT = al(512)
        osb = view(al(4 * 256), [256, 4], [1, 256])
        gemm_fm(Wm, 2064, 512, 8, hh, lambda m: [(0, 512)],
                lambda m, g, pv, t: scopy(sqk_[:, m, :], pv, [t], scale=0.125 if m < 2 else 1.0))

        def ev_s(c, i, pv, t, n):
            scopy(sv[:, i, :], pv[:, 0:256], [t])
            return scopy(mq[:, i, :], pv[:, 256:512])
        gemm_tm(Wm, 2576, 512, 8, hh, W512, ev_s)
        gemm_tm(Wm, 3088, 128, 8, hh, W512, lambda c, i, pv, t, n: scopy(ckv[:, i, :], pv[:, 0:128], [t]))
        s, wv, wl, tok = chunk(I["kr2"][l], 0, 8, 0, 192)
        b, pv, bw = bank()
        b2, pv2, bw2 = bank()
        for k in range(8):
            mm3(pv[0:96, :], (wv[:, k, 0:96], wl[:, k, 0:96]), (R(hh[:, 0, k, :]), R(hh[:, 1, k, :])), k == 0, k == 7,
                bw + [tok] if k == 0 else ())
        for k in range(8):
            t = mm3(pv2[0:96, :], (wv[:, k, 96:192], wl[:, k, 96:192]), (R(hh[:, 0, k, :]), R(hh[:, 1, k, :])),
                    k == 0, k == 7, bw2 if k == 0 else (), k == 7)
        used(s, t)
        tmpr = al(512)

        def rope(dst, pa, pb, w):
            vtt(tmpr[RP, :], pa, cosT[RP, :], MUL, w)
            vtt(dst, pb, sinT[RP, :], MUL)
            return vtt(dst, dst, tmpr[RP, :], ADD)
        t_kr = rope(krT[RP, :], pv[RP, :], pv2[RP, :], [t])
        rel(b, t_kr)
        rel(b2, t_kr)
        lend = borrow()
        SP_ = [view(lend(4 * 512), [512, 4], [1, 512]) for _ in range(2)]
        WT = [view(lend(4 * 512), [512, 4], [1, 512]) for _ in range(2)]
        eb = [lend(512), lend(512)]
        wt_free = [(), ()]
        for h in range(4):
            hp = slice(64 * (h % 2), 64 * (h % 2) + 64)
            q_, k_ = sqk_[hp, h // 2, :], sqk_[hp, 2 + h // 2, :]
            SPh, W_ = SP_[h % 2], WT[h % 2]
            for s_ in range(4):
                lo = 128 * s_
                N = 512 - lo
                e_ = eb[s_ % 2]
                b, pv, bw = bank()
                t = mm(pv[:, 0:N], k_[:, lo:lo + 128], q_[:, lo:512], True, True, bw, True)
                act(e_[:, 0:N], pv[:, 0:N], ACT.Abs, w=[t, (V, V.n)])
                act(e_[:, 0:N], e_[:, 0:N], ACT.Exp, scale=-1.0)
                ta = act(e_[:, 0:N], e_[:, 0:N], ACT.Ln, bias=1.0)
                tv = stt(SPh[:, s_, lo:512], pv[:, 0:N], 0.0, e_[:, 0:N], MAX, ADD, [ta] + list(wt_free[h % 2]))
                rel(b, tv)
                tv = vtt(SPh[:, s_, lo:lo + 128], SPh[:, s_, lo:lo + 128], C["US128"], MUL)
            for s_ in range(4):
                lo = 128 * s_
                N = 512 - lo
                b, pv, bw = bank()
                mm(pv[:, 0:N], k_[:, lo:lo + 128], q_[:, lo:512], True, False, bw + [tv])
                mm(pv[:, 0:N], C["nLI128"], SPh[:, s_, lo:512], False, False)
                for j_ in range(s_ + 1, 4):
                    o_ = 128 * (j_ - s_)
                    mm(pv[:, o_:N], C["none"], SPh[:, j_, 128 * j_:512], False, False)
                t = mm(pv[:, 0:128], C["ident"], C["negGE"], False, True, (), True)
                ta = act(W_[:, s_, lo:512], pv[:, 0:N], ACT.Exp, w=[t] + list(wt_free[h % 2]))
                rel(b, ta)
            b, pv, bw = bank()
            for i in range(4):
                for s_ in range(i + 1):
                    t = mm(pv[:, 64 * i:64 * i + 64], W_[:, s_, 128 * i:128 * i + 128], sv[:, s_, 64 * h:64 * h + 64],
                           s_ == 0, s_ == i, bw + [ta] if i + s_ == 0 else (), i == 3 and s_ == 3)
            wt_free[h % 2] = (t,)
            tv = vcopy(osb[:, :, 64 * h:64 * h + 64], view(pv, [64, 4], [1, 64]), [t])
            rel(b, tv)
        to_fm([osb[:, i, :] for i in range(4)], 2, lambda f: catT[:, 4 + f, :], None, [tv])
        barrier()
        lend = borrow()

        mqT = view(lend(2 * 512), [512, 2], [1, 512])
        ckT = lend(512)
        for i in range(4):
            group_norm(mq[:, i, :], 1, 256, 1e-6, small, tmpr, False)
            t = group_norm(ckv[:, i, :], 1, 128, 1e-6, small, tmpr, False)
        qn, kn = VC[f"qn{l}"], VC[f"kn{l}"]
        to_fm([mq[:, i, :] for i in range(4)], 2, lambda f: mqT[:, f, :],
              lambda f, o, i_, tt: act(o, i_, ACT.Copy, scale=qn[:, f:f + 1], w=[tt]), [t])
        t_cT = to_fm([ckv[:, i, :] for i in range(4)], 1, lambda f: ckT,
                     lambda f, o, i_, tt: act(o, i_, ACT.Copy, scale=kn[:, 0:1], w=[tt]), [t])
        uq = view(lend(768), [384, 2], [1, 384])
        usw = view(lend(256), [128, 2], [1, 128])
        ukv = lend(512)
        tw = [load_small(uq, I["mla_w_uq_2"][l].rearrange("(k p) c -> p k c", p=128)),
              load_small(usw, I["uq_sw"][l].rearrange("(k p) c -> p k c", p=128)),
              load_small(ukv, I["mla_w_ukv_2"][l])]
        qh = view(lend(4 * 512), [512, 4], [1, 512])
        kh = view(lend(4 * 512), [512, 4], [1, 512])
        for h in range(4):
            b, pv, bw = bank()
            b2, pv2, bw2 = bank()
            b3, pv3, bw3 = bank()
            for k in range(2):
                mm(pv[0:96, :], uq[:, k, 96 * h:96 * h + 96], mqT[:, k, :], k == 0, k == 1, bw + tw + [t_cT] if k == 0 else ())
            for k in range(2):
                mm(pv2[RP, :], usw[:, k, 32 * h:32 * h + 32], mqT[:, k, :], k == 0, k == 1, bw2 if k == 0 else ())
            t = mm(pv3[0:64, :], ukv[:, 128 * h:128 * h + 64], ckT, True, True, bw3, True)
            ta = scopy(qh[0:64, h, :], pv[0:64, :], [t])
            ta = scopy(kh[0:64, h, :], pv3[0:64, :])
            rel(b3, ta)
            tv = rope(qh[RP, h, :], pv[RP, :], pv2[RP, :], [ta])
            vcopy(kh[RP, h, :], krT[RP, :])
            rel(b, tv, ta)
            rel(b2, tv)
        vm = view(lend(4 * 256), [256, 4], [1, 256])
        for i in range(4):
            b, pv, bw = bank()
            t = mm(pv, ckT[:, 128 * i:128 * i + 128], ukv, True, True, bw, True)
            tv = vcopy(view(vm[:, i, :], [64, 4], [1, 64]), view(pv[:, 64:65], [128, 4], [1, 64]), [t])
            rel(b, tv)
        om = view(lend(4 * 256), [256, 4], [1, 256])
        pr = [lend(512), lend(512)]
        pT = [view(lend(512), [128, 4], [1, 128]) for _ in range(2)]
        pr_f, pT_f = [(), ()], [(), ()]
        SC = 96 ** -0.5
        n = 0
        st = lend(8 * 16)
        for h in range(4):
            for i in range(4):
                N = 128 * (i + 1)
                z_ = n % 2
                sc_ = st[:, 8 * (n % 16):8 * (n % 16) + 8]
                b, pv, bw = bank()
                mm(pv[:, 0:N], qh[0:96, h, 128 * i:128 * i + 128], kh[0:96, h, 0:N], True, False, bw + [(V, V.n)] if n == 0 else bw)
                t = mm(pv[:, N - 128:N], C["ident"], C["negLT"], False, True, (), True)
                tm = vred(sc_[:, 0:1], pv[:, 0:N], MAX, [t])
                tm = vts(sc_[:, 1:2], sc_[:, 0:1], -SC, None, MUL)
                ta = act(pr[z_][:, 0:N], pv[:, 0:N], ACT.Exp, scale=SC, bias=sc_[:, 1:2], w=[tm] + list(pr_f[z_]),
                         acc=sc_[:, 2:3])
                rel(b, ta)
                tr_ = recip(sc_[:, 3:4], sc_[:, 2:3], [ta])
                b, pv, bw = bank()
                for s_ in range(i + 1):
                    t = tr(pv[:, 128 * s_:128 * s_ + 128], pr[z_][:, 128 * s_:128 * s_ + 128],
                           bw + [ta] if s_ == 0 else (), s_ == i)
                pr_f[z_] = (t,)
                ta = scopy(view(pT[z_], [1, N]), pv[:, 0:N], [t] + list(pT_f[z_]))
                rel(b, ta)
                b, pv, bw = bank()
                for s_ in range(i + 1):
                    t = mm(pv[:, 0:64], pT[z_][:, s_, :], vm[:, s_, 64 * h:64 * h + 64], s_ == 0, s_ == i,
                           bw + [ta] if s_ == 0 else (), s_ == i)
                pT_f[z_] = (t,)
                tv = vts(om[:, i, 64 * h:64 * h + 64], pv[:, 0:64], sc_[:, 3:4], None, MUL, w=[t])
                rel(b, tv)
                n += 1
        t = to_fm([om[:, i, :] for i in range(4)], 2, lambda f: catT[:, 6 + f, :], None, [tv])
        ring_back(barrier())
        ct = split_x(catT, hh)

        def ev(c, i, pv, t, n):
            x_ = hX[:, i, c:c + 512]
            return stt(x_, x_, ALPHA, pv, MUL, ADD, [t])
        gemm_tm(I["mix_w_o_2"][l], 0, 1024, 8, hh, W512, ev, xt=ct)
        barrier()
        top[0] = m0_
        layer_norm_all(l, 1)

    blkw = al(512)
    vcopy(view(blkw, [128, 4], [1, 128]), rep(C["blk"], 4))
    hT_from_x()
    for l in range(2):
        ffn(l, "ffa_w_in_2", "ffa_w_out_2", 0)
        mixer(l)
        ffn(l, "ffb_w_in_2", "ffb_w_out_2", 2)
        m_ = top[0]
        pTl = view(al(1024), [512, 2], [1, 512])
        pop = opnd(2, 512)
        sg = view(al(4 * 512), [512, 4], [1, 512])
        t_p = load_small(pTl, I["pT"][l].rearrange("(k p) c -> p k c", p=128))
        pt = split_x(pTl, pop, [t_p])
        for hf in range(2):
            gemm_tm(I["ple_w_gate_2"][l], 512 * hf, 512, 8, hh, W512,
                    lambda c, i, pv, t, n: act(sg[:, i, :], pv, ACT.Sigmoid, w=[t, (V, V.n)]))

            def ev_p(c, i, pv, t, n, hf=hf):
                t1 = vtt(sg[:, i, :], sg[:, i, :], pv, MUL, [t, (S, S.n)])
                x_ = hX[:, i, 512 * hf:512 * hf + 512]
                vtt(x_, x_, sg[:, i, :], ADD)
                return t1
            gemm_tm(I["ple_w_proj_2"][l], 512 * hf, 512, 2, pop, W512, ev_p, pt)
        barrier()
        top[0] = m_
        if l == 0:
            hT_from_x()
    for i in range(4):
        load_small(out[0, 128 * i:128 * i + 128, :], hX[:, i, :], [(V, V.n)])


_WEIGHTS = ["x", "ctx", "b_ada", "w_ada", "w_in", "rw_w2", "rw_a2", "rw_g2", "rw_lnw", "rw_lnb", "ml_nw",
            "p_a", "p_b", "p_c", "w_out", "w_mlp1", "w_mlp2", "g_final", "positions_2", "ffa_w_in_2", "ffa_w_out_2",
            "mix_w_in_2", "gdn_a_log_2", "gdn_dt_bias_2", "gdn_norm_w_2", "mla_w_uq_2", "mla_w_ukv_2", "mix_w_o_2",
            "ffb_w_in_2", "ffb_w_out_2", "ln_g_2", "ln_b_2", "ple_w_gate_2", "ple_w_proj_2"]
_SQUEEZE = {"w_ada", "w_in", "p_a", "p_b", "p_c", "w_out", "w_mlp1", "w_mlp2"}


def _fm(v):
    v = np.asarray(v)
    return np.ascontiguousarray(v.reshape(-1, 128).T)


def arrays_of(inputs):
    a = {k: np.ascontiguousarray(inputs[k]) for k in _WEIGHTS}
    for k in _SQUEEZE:
        a[k] = a[k][0]
    g = {k: np.asarray(inputs[k]) for k in ("c", "c_ctx", "b_ada", "g_norm1", "g_norm2", "mu_prev", "mu_next", "rw_w0",
                                             "rw_a0", "rw_kk", "rw_ka", "rw_rk", "cv_dw", "cv_db", "cv_lnw", "cv_lnb",
                                             "gdn_conv_w_2", "mla_q_norm_w_2", "mla_kv_norm_w_2", "ml_ib", "ml_fb",
                                             "p_2", "mla_w_uq_2", "mix_w_in_2")}
    cdw = np.transpose(g["cv_dw"][0].reshape(31, 4, 128), (2, 1, 0)).reshape(128, 124)
    gcw = [np.transpose(g["gdn_conv_w_2"][l].reshape(4, 12, 128), (2, 1, 0)).reshape(128, 48) for l in range(2)]
    parts = [_fm(g["c"]), _fm(g["c_ctx"]), _fm(g["b_ada"]), _fm(g["g_norm1"]), _fm(g["g_norm2"]), _fm(g["mu_prev"]),
             _fm(g["mu_next"]), _fm(g["rw_w0"]), _fm(g["rw_a0"]), _fm(g["rw_kk"]), _fm(g["rw_ka"]), _fm(g["rw_rk"]),
             cdw, _fm(g["cv_db"]), _fm(g["cv_lnw"]), _fm(g["cv_lnb"]), gcw[0], gcw[1],
             _fm(g["mla_q_norm_w_2"][0]), _fm(g["mla_q_norm_w_2"][1]),
             _fm(g["mla_kv_norm_w_2"][0]), _fm(g["mla_kv_norm_w_2"][1])]
    a["vecs"] = np.ascontiguousarray(np.concatenate(parts, axis=1))
    a["mlgb"] = np.ascontiguousarray(np.stack([g["ml_ib"][0], g["ml_fb"][0]], axis=1).reshape(16))
    a["pT"] = np.ascontiguousarray(np.transpose(g["p_2"][:, 0], (0, 2, 1)))
    u = g["mla_w_uq_2"].reshape(2, 256, 4, 96)
    a["uq_sw"] = np.ascontiguousarray(np.concatenate([u[..., 80:96], u[..., 64:80]], axis=-1).reshape(2, 256, 128))
    r = g["mix_w_in_2"][:, :, 3216:3248]
    z64 = np.zeros(r.shape[:2] + (64,), r.dtype)
    a["kr2"] = np.ascontiguousarray(np.concatenate([z64, r, z64, r[..., 16:32], r[..., 0:16]], axis=-1))
    a["consts"] = const_tables()[1]
    return a


def kernel(**inputs):
    import concourse.bacc as _bacc
    from concourse.bass_utils import run_bass_kernel_spmd as _run

    nc = _bacc.Bacc("TRN2", target_bir_lowering=False, num_devices=1)
    arrays = arrays_of(inputs)
    I = {k: nc.dram_tensor(f"in_{k}", v.shape, mybir.dt.from_np(v.dtype), kind="ExternalInput").ap()
         for k, v in arrays.items()}
    out = nc.dram_tensor("out", (1, 512, 1024), F32, kind="ExternalOutput").ap()
    build(nc, I, out)
    r = _run(nc, [{f"in_{k}": v for k, v in arrays.items()}], core_ids=[0])
    return r.results[0]["out"]
```

```python
from contextlib import ExitStack

import numpy as np

import concourse.bass as bass
from concourse import mybir

F32 = mybir.dt.float32
F32R = mybir.dt.float32r
U32 = mybir.dt.uint32
I32 = mybir.dt.int32
ALU = mybir.AluOpType
ACT = mybir.ActivationFunctionType
AX = mybir.AxisListType.X
ADD, SUB, MUL, MAX, MIN = ALU.add, ALU.subtract, ALU.mult, ALU.max, ALU.min
NEG = -1.0e30
KAP = float(np.exp(-0.5))
SLOT = 2048
NSLOT = 3
ARENA = 53200
RING = 3 * SLOT * NSLOT


def const_tables():
    i = np.arange(128)[:, None]
    j = np.arange(128)[None, :]
    same = i // 64 == j // 64
    t = {"ident": i == j, "ones": np.ones((128, 128)), "blk": same, "J": i + j == 127}
    t["UI"] = same & (i <= j)

    def stack(m):
        return np.concatenate([m[0:64, 0:64], m[64:128, 64:128]], axis=0)

    def pair(a, b):
        return np.concatenate([stack(1.0 * a), stack(1.0 * b)], axis=1)
    for n in range(6):
        s = 1 << n
        m = (i // (2 * s) == j // (2 * s)) & (i // s % 2 == 1) & (j // s % 2 == 0)
        t[f"M{n}"] = m
        t[f"N{n}"] = m.T
    t["SU"] = pair(same & (i < j), same & (i <= j))
    t["SL"] = pair(same & (i > j), same & (i >= j))
    t["SI"] = pair(i == j, NEG * (1 - (same & (i >= j))))
    t["US128"] = i < j
    t["LS128"] = i > j
    t["nUI128"] = -1.0 * (i <= j)
    t["nLI128"] = -1.0 * (i >= j)
    t["none"] = -np.ones((128, 128))
    t["negGT"] = NEG * (i > j)
    t["negLT"] = NEG * (i < j)
    t["negGE"] = NEG * (i >= j)
    t["hs"] = np.concatenate([(np.arange(16)[None, :] == 2 * m + i // 64) for m in range(8)], axis=1)
    t["b2"] = (i // 64 == j) * (j < 2)
    t["half0"] = (i < 64) + 0 * j
    t["half1"] = (i >= 64) + 0 * j
    t["rs64"] = 1.0 * (j % 64 != 0) + 0 * i
    t["rs128"] = 1.0 * (j != 0) + 0 * i
    for d in range(2):
        for h in range(4):
            t[f"sel{d}{h}"] = (i == 32 * d + h) + 0 * j
    inv = (1.0 / (np.float32(10000.0) ** (np.arange(0, 32, 2, dtype=np.float32) / np.float32(32)))).astype(np.float32)
    r = np.zeros((128, 128), np.float32)
    r[64:96, 0] = np.concatenate([inv, inv])
    r[64:96, 1] = np.concatenate([-np.ones(16), np.ones(16)])
    t["rope"] = r
    names = list(t)
    return names, np.concatenate([np.asarray(t[k], np.float32) for k in names], axis=1)


VECS = [("c", 8), ("cc", 8), ("bada", 48), ("g1", 8), ("g2", 8), ("mup", 15), ("mun", 15), ("w0", 8), ("a0", 8),
        ("kk", 4), ("ka", 4), ("rk", 4), ("cdw", 124), ("cdb", 4), ("clw", 4), ("clb", 4),
        ("gcw0", 48), ("gcw1", 48), ("qn0", 2), ("qn1", 2), ("kn0", 1), ("kn1", 1)]
VOFF, _o = {}, 0
for _n, _k in VECS:
    VOFF[_n] = (_o, _k)
    _o += _k
NVEC = _o


class Counter:

    def __init__(self, sem):
        self.sem, self.n = sem, 0


class Queue(Counter):

    def __init__(self, sem, chained):
        super().__init__(sem)
        self.todo, self.seen, self.chained = [], {}, chained

    def wait(self, tokens):
        for who, v in tokens:
            if self.seen.get(id(who), 0) < v:
                self.seen[id(who)] = v
                self.todo.append(("wait", who.sem, v))

    def op(self, fn, w=(), sig=True):
        self.wait(w)
        if self.chained:
            self.wait([(self, self.n)])
        if not sig:
            self.todo.append(("op", fn, None, 0))
            return None
        self.n += 1
        self.todo.append(("op", fn, self.sem, 1))
        return (self, self.n)

    def dma(self, fn, counter, w=()):
        self.wait(w)
        counter.n += 16
        self.todo.append(("op", fn, counter.sem, 16))
        return (counter, counter.n)

    def run(self, eng):
        for x in self.todo:
            if x[0] == "wait":
                eng.wait_ge(x[1], x[2])
            else:
                ins = x[1]()
                if x[2] is not None:
                    ins.then_inc(x[2], x[3])


def view(ap, *dims):
    return bass.AP(ap.tensor, ap.offset, [ap.ap[0]] + [list(d) for d in dims])


class Plan:

    def __init__(self):
        self.known, self.loads, self.fences, self.operands = False, [], set(), set()


def build(nc, I, out):
    with ExitStack() as ctx:
        sems = [ctx.enter_context(nc.semaphore(f"s{n}")) for n in range(40)]
        plan = Plan()
        psum = ctx.enter_context(nc.psum_tensor("psum", [128, 8, 512], F32))
        for last in (False, True):
            rmem = {}
            for n, (o, size) in enumerate(sorted(plan.operands)):
                with nc.sbuf_tensor(f"pad{n}", [128, o], F32):
                    with nc.sbuf_tensor(f"r{n}", [128, size], F32R) as rt:
                        rmem[o, size] = rt
            with ExitStack() as one:
                keep = ctx if last else one
                name = "" if last else "0"
                mem = [keep.enter_context(nc.sbuf_tensor(f"ring{name}", [128, RING], F32)),
                       keep.enter_context(nc.sbuf_tensor(f"arena{name}", [128, ARENA - RING], F32))]
                it = iter(sems)
                P, V, S, G, D = (Queue(next(it), c) for c in (False, True, True, True, False))
                slot_sem = [Counter(next(it)) for _ in range(NSLOT)]
                small_sem = [Counter(next(it)) for _ in range(24)]
                body(nc, I, out, mem, rmem, psum, P, V, S, G, D, slot_sem, small_sem, plan)
            plan.known = True
        block = ctx.enter_context(nc.Block())

        @block.sync
        def _(e):
            D.run(e)

        @block.tensor
        def _(e):
            P.run(e)

        @block.vector
        def _(e):
            V.run(e)

        @block.scalar
        def _(e):
            S.run(e)

        @block.gpsimd
        def _(e):
            G.run(e)
            for c in small_sem + slot_sem:
                if c.n:
                    e.wait_ge(c.sem, c.n)


def body(nc, I, out, mem, rmem, psum, P, V, S, G, D, slot_sem, small_sem, plan):
    top = [0]

    def al(n):
        o = top[0]
        top[0] += n
        assert top[0] <= ARENA, (top[0], n)
        if o < RING:
            assert top[0] <= RING
            return mem[0][:, o:o + n]
        return mem[1][:, o - RING:o - RING + n]

    def al_at(o, n):
        return mem[1][:, o - RING:o - RING + n]

    free_banks = [(b, ()) for b in range(8)]

    def bank():
        b, w = free_banks.pop(0)
        return b, psum[:, b, :], list(w)

    def rel(b, *tokens):
        free_banks.append((b, tokens))

    def barrier():
        ends = [(q, q.n) for q in (P, V, S, G)]
        for q in (P, V, S, G):
            q.wait(ends)
        return ends

    def mm(o, l, r, start, stop, w=(), sig=False):
        return P.op(lambda: nc.tensor.matmul(o, l, r, start=start, stop=stop, skip_group_check=True), w, sig)

    def tr(o, i, w=(), sig=False):
        return P.op(lambda: nc.tensor.transpose(o, i, C["ident"]), w, sig)

    def act(o, i, f, scale=1.0, bias=0.0, w=(), acc=None):
        if acc is None:
            return S.op(lambda: nc.scalar.activation(o, i, f, scale=scale, bias=bias), w)
        return S.op(lambda: nc.scalar.activation(o, i, f, scale=scale, bias=bias, accum_out=acc), w)

    def scopy(o, i, w=(), scale=1.0):
        return act(o, i, ACT.Copy, scale=scale, w=w)

    def vcopy(o, i, w=()):
        return V.op(lambda: nc.vector.tensor_copy(o, i), w)

    def vtt(o, a, b, f, w=()):
        return V.op(lambda: nc.vector.tensor_tensor(o, a, b, f), w)

    def vts(o, a, s1, s2, f0, f1=None, w=()):
        if f1 is None:
            return V.op(lambda: nc.vector.tensor_scalar(o, a, s1, None, f0), w)
        return V.op(lambda: nc.vector.tensor_scalar(o, a, s1, s2, f0, f1), w)

    def stt(o, a, s, b, f0, f1, w=()):
        return V.op(lambda: nc.vector.scalar_tensor_tensor(out=o, in0=a, scalar=s, in1=b, op0=f0, op1=f1), w)

    def vred(o, i, f, w=()):
        return V.op(lambda: nc.vector.tensor_reduce(o, i, AX, f), w)

    def recip(o, i, w=()):
        return V.op(lambda: nc.vector.reciprocal(o, i), w)

    def scan(o, a, b, f0, f1, w=()):
        return V.op(lambda: nc.vector.tensor_tensor_scan(o, a, b, 0.0, f0, f1), w)

    def cpred(o, m, d, w=()):
        return V.op(lambda: nc.vector.copy_predicated(o, m, d), w)

    def vset(o, v, w=()):
        return V.op(lambda: nc.vector.memset(o, v), w)

    def gtt(o, a, b, f, w=()):
        return G.op(lambda: nc.gpsimd.tensor_tensor(o, a, b, f), w)

    n_small = [0]

    def load_small(dst, src, w=()):
        c = small_sem[n_small[0] % len(small_sem)]
        n_small[0] += 1

        def go():
            with nc.allow_non_contiguous_dma(reason="small"):
                return nc.gpsimd.dma_start(dst, src)
        return G.dma(go, c, list(w) + [(c, c.n)])


    ring = al(SLOT * NSLOT * 3)

    live = {(NSLOT * SLOT, 2 * NSLOT * SLOT)}
    plan.operands.add((NSLOT * SLOT, 2 * NSLOT * SLOT))

    def R(ap):
        if not plan.known:
            return ap
        o = ap.offset + (0 if ap.tensor.name == ring.tensor.name else RING)
        for (start, size), rt in rmem.items():
            if start <= o < start + size and (start, size) in live:
                base = rt[:, 0:1]
                return bass.AP(base.tensor, o - start, [base.ap[0]] + [list(d) for d in ap.ap[1:]])
        assert False

    raw = [ring[:, SLOT * n:SLOT * n + SLOT] for n in range(NSLOT)]
    his = [ring[:, SLOT * (NSLOT + n):SLOT * (NSLOT + n) + SLOT] for n in range(NSLOT)]
    los = [ring[:, SLOT * (2 * NSLOT + n):SLOT * (2 * NSLOT + n) + SLOT] for n in range(NSLOT)]
    raw_free = [() for _ in range(NSLOT)]
    use_free = [() for _ in range(NSLOT)]
    n_req, n_dma, n_split = [0], [0], [0]
    dma_tok, split_tok = {}, {}

    def ring_back(tokens):
        if not plan.known:
            plan.fences.add(n_req[0])
        for n in range(NSLOT):
            raw_free[n] = use_free[n] = tuple(tokens)

    def load_ahead(i):
        stop = min([f for f in plan.fences if f > i] + [len(plan.loads)])
        while n_dma[0] < min(i + NSLOT, stop) or n_split[0] < min(i + 2, stop):
            if n_split[0] < min(i + 2, stop) and n_split[0] < n_dma[0]:
                j = n_split[0]
                z, (pieces, size, split) = j % NSLOT, plan.loads[j]
                if split:
                    h_, l_, r_ = R(his[z][:, 0:size]), R(los[z][:, 0:size]), raw[z][:, 0:size]
                    t1 = act(h_, r_, ACT.Copy, w=[dma_tok[j]] + list(use_free[z]))
                    t2 = vtt(l_, r_, h_, SUB, [t1])
                    raw_free[z] = (t1, t2)
                    split_tok[j] = t2
                else:
                    split_tok[j] = dma_tok[j]
                n_split[0] += 1
            else:
                j = n_dma[0]
                z, (pieces, size, split) = j % NSLOT, plan.loads[j]
                for e, (fn, src) in enumerate(pieces):
                    dst = fn(raw[z])
                    dma_tok[j] = D.dma(lambda dst=dst, src=src: nc.sync.dma_start(dst, src), slot_sem[z],
                                       raw_free[z] if e == 0 else ())
                n_dma[0] += 1

    def wload(pieces, size, split=True):
        i = n_req[0]
        if not plan.known:
            plan.loads.append((pieces, size, split))
            n_req[0] += 1
            return i % NSLOT, raw[0], raw[0], (D, 0)
        load_ahead(i)
        n_req[0] += 1
        z = i % NSLOT
        return (z, R(his[z]), R(los[z]), split_tok[i]) if split else (z, raw[z], None, split_tok[i])

    def used(z, t, split=True):
        use_free[z] = (t,)
        if not split:
            raw_free[z] = (t,)

    def chunk(W, r0, kt, c0, nc_, split=True):
        src = W[r0:r0 + 128 * kt, c0:c0 + nc_].rearrange("(k p) c -> p k c", p=128)
        z, hi, lo, tok = wload([(lambda x: view(x, [nc_, kt], [1, nc_]), src)], nc_ * kt, split)
        return z, view(hi, [nc_, kt], [1, nc_]), lo and view(lo, [nc_, kt], [1, nc_]), tok

    def split_x(x, o, w=()):
        toks = []
        for k in range(x.shape[1]):
            t = act(R(o[:, 0, k, :]), x[:, k, :], ACT.Copy, w=w)
            toks.append(vtt(R(o[:, 1, k, :]), x[:, k, :], R(o[:, 0, k, :]), SUB, [t]))
        return toks

    def opnd(k, n):
        o = top[0]
        for key in [x for x in live if x[0] < o + 2 * k * n and o < x[0] + x[1]]:
            live.remove(key)
        live.add((o, 2 * k * n))
        plan.operands.add((o, 2 * k * n))
        return view(al(2 * k * n), [k * n, 2], [n, k], [1, n])

    def mm3(o, l, r, first, last, w=(), sig=False):
        (lh, ll), (rh, rl) = l, r
        mm(o, lh, rh, first, False, w)
        mm(o, lh, rl, False, False)
        return mm(o, ll, rh, False, last, (), sig)

    def gemm_fm(W, c0, ncols, kt, xs, segs, evac, w=(), r0=0, xt=None):
        for done in range(0, ncols, 256):
            n = min(256, ncols - done)
            z, wh, wl, tok = chunk(W, r0, kt, c0 + done, n)
            for m in range(0, n, 128):
                for g, (a, sz) in enumerate(segs((done + m) // 128)):
                    x = xs[g] if isinstance(xs, tuple) else xs
                    b, pv, bw = bank()
                    for k in range(kt):
                        t = mm3(pv[:, 0:sz], (wh[:, k, m:m + 128], wl[:, k, m:m + 128]),
                                (R(x[:, 0, k, a:a + sz]), R(x[:, 1, k, a:a + sz])), k == 0, k == kt - 1,
                                (bw + [tok] + list(w) if k == 0 else []) + ([xt[k]] if xt else []), k == kt - 1)
                    used(z, t)
                    rel(b, evac((done + m) // 128, g, pv, t))

    def gemm_tm(W, c0, ncols, kt, xs, tiles, evac, w=(), step=512, r0=0, xt=None):
        for done in range(0, ncols, step):
            n = min(step, ncols - done)
            kmax = min(8, 2048 // n) if n > 64 else 8
            banks = [bank() for _ in tiles]
            for k0 in range(0, kt, kmax):
                kn = min(kmax, kt - k0)
                z, wh, wl, tok = chunk(W, r0 + 128 * k0, kn, c0 + done, n)
                for i, a in enumerate(tiles):
                    b, pv, bw = banks[i]
                    x, a = a if isinstance(a, tuple) else (xs, a)
                    for k in range(kn):
                        q_ = k0 + k
                        t = mm3(pv[:, 0:n], (R(x[:, 0, q_, a:a + 128]), R(x[:, 1, q_, a:a + 128])),
                                (wh[:, k, :], wl[:, k, :]), q_ == 0, q_ == kt - 1,
                                (bw if q_ == 0 else []) + ([tok] + list(w) if k == 0 else []) + ([xt[q_]] if xt else []),
                                k == kn - 1)
                    used(z, t)
                    if k0 + kn == kt:
                        rel(b, evac(done, i, pv, t, n))

    def to_fm(srcs, nf, dst, evac=None, w=(), width=128):
        t2 = None
        for f in range(nf):
            for q in range(0, len(srcs), 4):
                part = srcs[q:q + 4]
                b, pv, bw = bank()
                for i, s_ in enumerate(part):
                    t = tr(pv[:, 128 * i:128 * i + 128], s_[:, 128 * f:128 * f + 128],
                           bw + list(w) if i == 0 else (), i == len(part) - 1)
                o = dst(f)[:, 128 * q:128 * q + 128 * len(part)]
                i_ = pv[:, 0:128 * len(part)]
                t2 = evac(f, o, i_, t) if evac else scopy(o, i_, [t])
                rel(b, t2)
        return t2

    tmp_op = al(1024)
    n_tmp = [0]
    tmp_free = [(), ()]

    def to_op(srcs, nf, dst, c0=0, scale=None, bias=None, w=()):
        toks = []
        for f in range(nf):
            b, pv, bw = bank()
            n = 128 * len(srcs)
            for i, s_ in enumerate(srcs):
                t = tr(pv[:, 128 * i:128 * i + 128], s_[:, 128 * f:128 * f + 128],
                       bw + list(w) if i == 0 else (), i == len(srcs) - 1)
            hi, lo = (R(dst[:, j, f, c0:c0 + n]) for j in (0, 1))
            if scale is None:
                t1 = act(hi, pv[:, 0:n], ACT.Copy, w=[t])
                t2 = vtt(lo, pv[:, 0:n], hi, SUB, [t1])
                rel(b, t2)
            else:
                z = n_tmp[0] % 2
                n_tmp[0] += 1
                x = tmp_op[:, 512 * z:512 * z + n]
                t1 = act(x, pv[:, 0:n], ACT.Identity, scale=scale(f), bias=bias(f) if bias else 0.0,
                         w=[t] + list(tmp_free[z]))
                rel(b, t1)
                t1 = act(hi, x, ACT.Copy)
                t2 = vtt(lo, x, hi, SUB, [t1])
                tmp_free[z] = (t2,)
            toks.append(t2)
        return toks

    def borrow():
        barrier()
        o = [0]

        def lend(n):
            o[0] += n
            assert o[0] <= 3 * NSLOT * SLOT, o[0]
            return ring[:, o[0] - n:o[0]]
        return lend

    names, _ = const_tables()
    cst = al(128 * len(names))
    C = {k: cst[:, 128 * i:128 * i + 128] for i, k in enumerate(names)}
    t_c = load_small(cst, I["consts"])
    vec = al(NVEC)
    t_v = load_small(vec, I["vecs"])
    VC = {k: vec[:, o:o + n] for k, (o, n) in VOFF.items()}
    for q in (P, V, S, G):
        q.wait([t_c, t_v])

    def rep(c, n, width=128):
        return view(c, [0, n], [1, width])

    def row(src_ap, n):
        return bass.AP(src_ap.tensor, src_ap.offset, [[0, 128], [1, n]])

    def rstd(o, ssq, n, eps, w=()):
        t = vts(o, ssq, 1.0 / n, eps, MUL, ADD, w=w)
        t = act(o, o, ACT.Sqrt, w=[t])
        return recip(o, o, [t])

    st6 = al(16)

    def layer_norm_tile(o, x, n, eps, scr, w=()):
        V.op(lambda: nc.vector.bn_stats(st6[:, 0:6], x[:, 0:512]), w)
        V.op(lambda: nc.vector.bn_stats(st6[:, 6:12], x[:, 512:1024]))
        t = V.op(lambda: nc.vector.bn_aggr(scr[:, 0:2], st6[:, 0:12]))
        rstd(scr[:, 2:3], scr[:, 1:2], 1.0, eps, w=[t])
        return vts(o, x, scr[:, 0:1], scr[:, 2:3], SUB, MUL)

    def group_norm(x, g, n, eps, scr, sq, mean, w=()):
        x3, q3 = view(x, [n, g], [1, n]), view(sq, [n, g], [1, n])
        if mean:
            vred(scr[:, 0:g], x3, ADD, w)
            vts(scr[:, 0:g], scr[:, 0:g], 1.0 / n, None, MUL)
            vtt(x3, x3, view(scr[:, 0:g], [1, g], [0, n]), SUB)
            w = ()
        vtt(q3, x3, x3, MUL, w)
        t = vred(scr[:, g:2 * g], q3, ADD)
        rstd(scr[:, 2 * g:3 * g], scr[:, g:2 * g], n, eps, [t])
        return vtt(x3, x3, view(scr[:, 2 * g:3 * g], [1, g], [0, n]), MUL)

    HALF = (slice(0, 64), slice(64, 128))

    def diag(x, p):
        return view(x[HALF[p], 64 * p:64 * p + 64], [128, 8], [1, 64])

    def h8(x):
        return view(x, [64, 8], [1, 64])

    def mask8(name, k, n=8):
        return rep(C[name][:, 64 * k:64 * k + 64], n, 64)

    def invert(T, TT, AT, X, low, w):
        blk_ = lambda x, h: x[:, 128 * h:128 * h + 128]
        for n in range(1, 6):
            m, mt = (rep(C[k + str(n)], 4).bitcast(U32) for k in ("MN" if low else "NM"))
            tx = []
            for q_ in (0, 1):
                b, pv, bw = bank()
                for i in range(4):
                    h = 4 * q_ + i
                    t = mm(blk_(pv, i), blk_(AT, h), blk_(T, h), True, True, bw + list(w) if i == 0 else (), i == 3)
                tx.append(scopy(X[:, 512 * q_:512 * q_ + 512], pv, [t]))
                rel(b, tx[-1])
            yield None
            new = []
            for q_ in (0, 1):
                jobs = [(X, TT, TT, mt)]
                if n < 5:
                    jobs.append((TT, X, T, m))
                todo = []
                for l, r, dst, msk in jobs:
                    b, pv, bw = bank()
                    for i in range(4):
                        h = 4 * q_ + i
                        t = mm(blk_(pv, i), blk_(l, h), blk_(r, h), True, True, bw + [tx[q_]] if i == 0 else (), i == 3)
                    todo.append((b, pv, dst, msk))
                for b, pv, dst, msk in todo:
                    new.append(cpred(view(dst[:, 512 * q_:512 * q_ + 512], [128, 4], [1, 128]), msk,
                                     view(pv, [128, 4], [1, 128]), [t]))
                    rel(b, new[-1])
            w = new
            yield w

    def interleave(*streams, lag=0):
        streams = list(streams)
        for _ in range(lag):
            next(streams[0])
        while streams:
            for s_ in list(streams):
                try:
                    next(s_)
                except StopIteration:
                    streams.remove(s_)

    def gcopy(o, i, w=()):
        return G.op(lambda: nc.gpsimd.tensor_copy(o, i), w)
    SEGS = [(0, 512), (0, 256)]
    W512 = [0, 128, 256, 384]
    TW = 770
    TO = [514, 642, 0, 128, 256, 384]
    SEQ_ = ([0, 1, 2, 3, 4, 5], [1, 0, 5, 4, 3, 2])

    mk_hT = top[0]
    hL = opnd(8, 512)
    silc = al(16)
    silcv = view(silc, [2, 8], [1, 2])
    mod = view(al(96), [2, 48], [1, 2])
    small = al(256)
    sc1 = view(al(16), [2, 8], [1, 2])
    sc2 = view(al(16), [2, 8], [1, 2])
    mk_y = top[0]
    ycT = view(al(4 * 512), [512, 4], [1, 512])
    yaT = view(al(4 * 512), [512, 4], [1, 512])

    act(view(silc, [2, 8]), VC["c"], ACT.Silu)
    t_sil = act(view(silc[:, 1:2], [2, 8]), VC["cc"], ACT.Silu)
    def modulate(part):
        b, pv, bw = bank()
        for hf in range(4):
            s, wv, _, tok = chunk(I["w_ada"], 0, 8, part * 1024 + 256 * hf, 256, False)
            for m in range(2):
                for k in range(8):
                    t = mm(pv[:, 4 * hf + 2 * m:4 * hf + 2 * m + 2], wv[:, k, 128 * m:128 * m + 128], silcv[:, k, :],
                           k == 0, k == 7, bw + [tok, t_sil] if k == 0 and m == 0 else (), k == 7 and m == 1)
            used(s, t, False)
        o = mod[:, 8 * part:8 * part + 8, :]
        t = vtt(o, view(pv, [2, 8], [1, 2]), view(VC["bada"][:, 8 * part:8 * part + 8], [1, 8], [0, 2]), ADD, [t])
        rel(b, t)
    def norm_scale(sc, part, g):
        vts(sc, mod[:, 8 * part:8 * part + 8, :], 1.0, None, ADD)
        return vtt(sc, sc, view(VC[g], [1, 8], [0, 2]), MUL)
    modulate(0)
    modulate(1)
    t_sc = norm_scale(sc1, 1, "g1")

    def bcast_rows(dst, part):
        m_ = top[0]
        lt = view(al(1024), [128, 8], [1, 128])
        bi = al(1024)
        t0 = load_small(bi, row(I["b_ada"][0, 1024 * part:1024 * part + 1024], 1024), barrier())
        t1 = vcopy(lt, view(silc, [2, 8], [0, 128]))
        for hf in range(2):
            b, pv, bw = bank()
            for k0 in (0, 4):
                s, wv, _, tok = chunk(I["w_ada"], 128 * k0, 4, part * 1024 + 512 * hf, 512, False)
                for k in range(4):
                    t = mm(pv, lt[:, k0 + k, :], wv[:, k, :], k + k0 == 0, k + k0 == 7,
                           (bw if k0 == 0 else []) + [tok, t1] if k == 0 else (), k == 3)
                used(s, t, False)
            t = vtt(dst[:, 512 * hf:512 * hf + 512], pv, bi[:, 512 * hf:512 * hf + 512], ADD, [t, t0])
            rel(b, t)
        barrier()
        top[0] = m_
        return t

    def rms_scales(o, x, scr, w=()):
        t = act(scr, x, ACT.Square, w=w, acc=o)
        return rstd(o, o, 1024, 1e-6, [t])

    def norm_mod_op(xs, cols, sc, sh, dst, scr, t_sc, w=()):
        xn = []
        for i, x in enumerate(xs):
            r = small[:, i:i + 1]
            t = rms_scales(r, x, scr, w[i] if w else ())
            t = vts(x, x, r, None, MUL, w=[t])
            xn.append(x)

        V.wait([t_sc])
        S.wait([t_sc])
        return to_op(xn, 8, dst, 0, lambda f: sc[:, f, cols:cols + 1], lambda f: sh[:, f, cols:cols + 1], [t])

    mk_c = top[0]
    hC = opnd(8, 256)
    mk = top[0]
    xs_all = al(6 * 1024)
    scr = al(1024)
    tk = []
    for i in range(4):
        tk.append([load_small(xs_all[:, 1024 * i:1024 * i + 1024], I["x"][0, 128 * i:128 * i + 128, :])])
    for i in range(2):
        tk.append([load_small(xs_all[:, 1024 * (4 + i):1024 * (5 + i)], I["ctx"][0, 128 * i:128 * i + 128, :])])
    tiles = [xs_all[:, 1024 * i:1024 * i + 1024] for i in range(6)]
    norm_mod_op(tiles[0:4], 0, sc1, mod[:, 0:8, :], hL, scr, t_sc, tk[0:4])
    norm_mod_op(tiles[4:6], 1, sc1, mod[:, 0:8, :], hC, scr, t_sc, tk[4:6])
    barrier()
    top[0] = mk

    CVO, MLO, GO = 1920, 2944, 5008
    q = view(al(4 * 512), [512, 4], [1, 512])
    kx = view(al(4 * 768), [768, 4], [1, 768])
    v1 = view(al(6 * 4 * 129), [4 * 129, 6], [129, 4], [1, 129])
    og = view(al(4 * 512), [512, 4], [1, 512])
    gates = view(al(6 * 16), [16, 6], [1, 16])
    gb = al(16)
    t_gb = load_small(gb, row(I["mlgb"], 16))
    vset(v1, 1.0)
    KT = [512, 640, 0, 128, 256, 384]
    LC = [(hC, 0), (hC, 128)] + [(hL, a_) for a_ in W512]
    gemm_fm(I["w_in"], MLO, 512, 8, hL, lambda m: [(0, 512)], lambda m, g, pv, t: scopy(q[:, m, :], pv, [t]))
    gemm_fm(I["w_in"], MLO + 512, 512, 8, (hL, hC), lambda m: SEGS,
            lambda m, g, pv, t: scopy(kx[:, m, 512 * g:512 * g + SEGS[g][1]], pv[:, 0:SEGS[g][1]], [t],
                                      scale=128 ** -0.5))
    gemm_tm(I["w_in"], MLO + 1024, 512, 8, None, LC,
            lambda c, i, pv, t, n: vcopy(v1[:, i, :, 0:128], view(pv, [128, 4], [1, 128]), [t]))
    gemm_tm(I["w_in"], MLO + 1536, 512, 8, None, LC[2:],
            lambda c, i, pv, t, n: act(og[:, i, :], pv, ACT.Sigmoid, w=[t]))
    gemm_tm(I["w_in"], MLO + 2048, 16, 8, None, LC,
            lambda c, i, pv, t, n: vtt(gates[:, i, :], pv[:, 0:16], gb, ADD, [t, t_gb]))
    g4 = view(gates, [16, 6], [8, 2], [1, 8])
    IG = view(al(48), [8, 6], [4, 2], [1, 4])
    LF = view(al(48), [8, 6], [4, 2], [1, 4])
    tA = view(al(48), [8, 6], [4, 2], [1, 4])
    vcopy(IG, g4[:, :, :, 0:4])
    vcopy(LF, g4[:, :, :, 4:8])
    t = vcopy(tA, LF)
    act(tA, tA, ACT.Abs, w=[t])
    act(tA, tA, ACT.Exp, scale=-1.0)
    t = act(tA, tA, ACT.Ln, bias=1.0)
    vts(LF, LF, 0.0, None, MIN, w=[t])
    t_lf = vtt(LF, LF, tA, SUB)
    lend = borrow()
    lfr, igr, cumr, mr, rsm = (lend(768) for _ in range(5))
    for x in (lfr, igr):
        vset(x, 0.0)
    for d in range(2):
        for X, rw_ in ((LF, lfr), (IG, igr)):
            for half, n in ((0, 4), (4, 2)):
                b, pv, bw = bank()
                for i in range(n):
                    ti = SEQ_[d][half + i]
                    t = mm(pv[32 * d:32 * d + 4, 128 * i:128 * i + 128], X[:, ti, d, :], C["J" if d else "ident"],
                           True, True, bw + [t_lf] if i == 0 else (), i == n - 1)
                t = vcopy(rw_[32 * d:32 * d + 4, 128 * half:128 * (half + n)], pv[32 * d:32 * d + 4, 0:128 * n], [t])
                rel(b, t)
    vcopy(view(rsm, [128, 6], [1, 128]), rep(C["rs128"], 6))
    scan(mr[0:64], lfr[0:64], igr[0:64], ADD, MAX)
    scan(cumr[0:64], rsm[0:64], lfr[0:64], MUL, ADD)
    t_R = vtt(cumr[0:64], cumr[0:64], mr[0:64], SUB)
    Rn = lend(512)
    t = vset(Rn, 0.0)
    em = view(lend(4 * 8), [8, 4], [1, 8])
    id4 = C["ident"]
    cR = view(lend(4 * 8), [8, 4], [1, 8])
    vcopy(Rn[0:4, :], cumr[0:4, 256:768])
    b, pv, bw = bank()
    for i in range(4):
        t = mm(pv[:, 4 * i:4 * i + 4], mr[0:4, 256 + 128 * i:384 + 128 * i], id4[0:4, 0:4], True, True,
               bw + [t_R] if i == 0 else (), i == 3)
    t = vcopy(em[:, :, 0:4], view(pv, [4, 4], [1, 4]), [t])
    rel(b, t)
    b, pv, bw = bank()
    for i in range(4):
        ps = 3 - i
        for j, X in enumerate((cumr, mr)):
            t = mm(pv[:, 8 * i + 4 * j:8 * i + 4 * j + 4], X[32:36, 256 + 128 * ps:384 + 128 * ps], id4[32:36, 32:36],
                   True, True, bw + [t_R] if i + j == 0 else (), i == 3 and j == 1)
    t_cR = vcopy(cR, view(pv, [8, 4], [1, 8]), [t])
    rel(b, t_cR)
    b, pv, bw = bank()
    b2_, pv2, bw2 = bank()
    for i in range(4):
        mm(pv[:, 4 * i:4 * i + 4], C["J"], cR[:, i, 4:8], True, True, bw + [t_cR] if i == 0 else ())
        t = mm(pv2[32:36, 128 * i:128 * i + 128], cR[:, i, 0:4], C["J"], True, True, bw2 if i == 0 else (), i == 3)
    t1 = vcopy(em[:, :, 4:8], view(pv, [4, 4], [1, 4]), [t])
    rel(b, t1)
    t_Rn = vcopy(Rn[32:36, :], pv2[32:36, :], [t])
    rel(b2_, t_Rn)
    t_em = act(em, em, ACT.Exp, scale=-1.0, w=[t1])
    bias = view(lend(36 * 4), [4, 36], [1, 4])
    pair = {}
    b, pv, bw = bank()
    n_p = 0
    for d in range(2):
        for a in range(2, 6):
            for s_ in range(a + 1):
                T_, S_ = SEQ_[d][a], SEQ_[d][s_]
                pair[d, T_, S_] = n_p
                o = pv[:, 4 * n_p:4 * n_p + 4]
                if s_ == a:
                    terms = [(C["nUI128"] if d == 0 else C["nLI128"], S_)]
                else:
                    terms = [(C["LS128"] if d == 0 else C["US128"], S_)] + [(C["ones"], SEQ_[d][m_]) for m_ in range(s_ + 1, a)]
                for e, (mat, ti) in enumerate(terms):
                    t = mm(o, mat, LF[:, ti, d, :], e == 0, e == len(terms) - 1, bw + [t_lf] if n_p + e == 0 else (),
                           n_p == 35 and e == len(terms) - 1)
                n_p += 1
    for (d, T_, S_), n_ in pair.items():
        tb = vtt(bias[:, n_, :], pv[:, 4 * n_:4 * n_ + 4], IG[:, S_, d, :], ADD, [t])
    rel(b, tb)
    t_bias = tb
    Hm = view(lend(4 * 512), [512, 4], [1, 512])
    QK = view(lend(6 * 512), [512, 6], [1, 512])
    EE = view(lend(2 * 6 * 512), [6 * 512, 2], [512, 6], [1, 512])
    dn = al(16)
    ee_free = [(), ()]
    def weights(h, d):
        if d == 0:
            for s_ in range(6):
                kc = KT[s_]
                b, pv, bw = bank()
                t = mm(pv, kx[:, h, kc:kc + 128], q[:, h, :], True, True, bw, True)
                tqk[0] = scopy(QK[:, s_, :], pv, [t] + list(qk_free[0]))
                rel(b, tqk[0])
        E_ = EE[:, d]
        b, pv, bw = bank()
        b2_, pv2, bw2 = bank()
        mm(pv, C[f"sel{d}{h}"][0:64], Rn[0:64], True, True, bw + [t_Rn])
        mm(pv2, C[f"sel{d}{h}"][0:64], Rn[0:64], True, False, bw2)
        t = mm(pv2, C["ident"], rep(C["negGT" if d == 0 else "negLT"], 4), False, True, (), True)
        for (dd, T_, S_), n_ in pair.items():
            if dd != d:
                continue
            c0 = 128 * (T_ - 2)
            src = (pv2 if S_ == T_ else pv)[:, c0:c0 + 128]
            te = act(E_[:, S_, c0:c0 + 128], src, ACT.Exp, bias=bias[:, n_, h:h + 1],
                     w=[t, t_bias] + list(ee_free[d]))
        rel(b, te)
        rel(b2_, te)
        for S_ in range(6):
            if S_ < 2:
                lo, hi = 0, 512
            elif d == 0:
                lo, hi = 128 * (S_ - 2), 512
            else:
                lo, hi = 0, 128 * (S_ - 1)
            te2 = vtt(E_[:, S_, lo:hi], E_[:, S_, lo:hi], QK[:, S_, lo:hi], MUL, [te, tqk[0]])
        qk_free[0] = (te2,)
        return te2

    def outputs(h, d, te2):
        E_ = EE[:, d]
        for a in range(2, 6):
            T_ = SEQ_[d][a]
            c0 = 128 * (T_ - 2)
            b, pv, bw = bank()
            ks = SEQ_[d][0:a + 1]
            for e, S_ in enumerate(ks):
                t = mm(pv[:, 0:129], E_[:, S_, c0:c0 + 128], v1[:, S_, h, :], e == 0, e == len(ks) - 1,
                       bw + [te2] if e == 0 else (), e == len(ks) - 1)
            vts(dn[:, 0:1], pv[:, 128:129], -1.0, em[:, T_ - 2, 4 * d + h:4 * d + h + 1], MUL, MAX, w=[t, t_em])
            vtt(dn[:, 0:1], dn[:, 0:1], pv[:, 128:129], MAX)
            recip(dn[:, 1:2], dn[:, 0:1])
            ho = Hm[:, T_ - 2, 128 * h:128 * h + 128]
            if d == 0:
                tv = vts(ho, pv[:, 0:128], dn[:, 1:2], None, MUL)
            else:
                tv = stt(ho, pv[:, 0:128], dn[:, 1:2], ho, MUL, ADD)
            rel(b, tv)
        ee_free[d] = (t,)

    tqk, qk_free, before = [None], [()], None
    for h in range(4):
        for d in range(2):
            te2 = weights(h, d)
            if before:
                outputs(*before)
            before = (h, d, te2)
    outputs(*before)
    barrier()
    nwr = lend(512)
    t_nw = load_small(nwr, row(I["ml_nw"][0, :], 512))
    sqs = EE[:, 0, 0, :]
    for i in range(4):
        x_ = Hm[:, i, :]
        group_norm(x_, 4, 128, 1e-5, small, sqs, True)
        vtt(x_, x_, nwr, MUL, [t_nw])
        t = vtt(x_, x_, og[:, i, :], MUL)
    to_fm([Hm[:, i, :] for i in range(4)], 4, lambda f: ycT[:, f, :], None, [t])
    ring_back(barrier())
    top[0] = mk

    rT = yaT
    kT = view(al(4 * TW), [TW, 4], [1, TW])
    lo3 = view(al(3 * TW), [TW, 3], [1, TW])
    vt = view(al(6 * 512), [512, 6], [1, 512])
    bonus = view(al(32), [8, 4], [1, 8])
    cm = al(15)
    kam = al(4)
    nwa = al(16)
    mk2 = top[0]
    ub = view(al(2 * 772), [772, 2], [1, 772])
    vv = tmp_op[:, 0:TW]
    t_ub = vset(ub, 0.0)
    vts(cm, VC["mup"], -1.0, 1.0, MUL, ADD)
    vtt(cm, cm, VC["mun"], SUB)
    vts(nwa[:, 0:8], VC["w0"], 0.5, None, MUL)
    vts(nwa[:, 8:16], VC["a0"], 0.5, None, MUL)
    t_km = vts(kam, VC["ka"], -1.0, 1.0, MUL, ADD)
    ub_free = [(t_ub,), (t_ub,)]
    vv_free = [()]

    def shift(m, o, n):
        u = ub[:, m % 2, :]
        vts(o, u[:, 1:1 + n], cm[:, m:m + 1], None, MUL)
        stt(o, u[:, 0:n], VC["mup"][:, m:m + 1], o, MUL, ADD)
        t = stt(o, u[:, 2:2 + n], VC["mun"][:, m:m + 1], o, MUL, ADD)
        ub_free[m % 2] = (t,)
        return t

    later = []

    def ev_u(m, g, pv, t):
        while later and g == 0:
            later.pop(0)()
        n = 512 if g == 0 else 256
        o = ub[:, m % 2, 1:513] if g == 0 else ub[:, m % 2, 515:771]
        tc = scopy(o, pv[:, 0:n], [t] + list(ub_free[m % 2]))
        if m < 4:
            V.wait([tc])
            shift(m, rT[:, m, :], 512)
        elif g == 1:
            V.wait([tc])
            if m < 8:
                f = m - 4
                o = kT[:, f, :]
                shift(m, o, TW)
            elif m < 12:
                f = m - 8
                tv = V.op(lambda: nc.vector.memset(vv[:, 0:1], 0.0), vv_free[0])
                tv = shift(m, vv, TW)

                def to_tokens(f=f, tv=tv):
                    for q0, n in ((0, 4), (4, 2)):
                        b1, p1, w1 = bank()
                        for i in range(n):
                            a = TO[q0 + i]
                            tm = tr(p1[:, 128 * i:128 * i + 128], vv[:, a:a + 128], w1 + [tv] if i == 0 else (), i == n - 1)
                        ta = scopy(vt[:, q0:q0 + n, 128 * f:128 * f + 128], view(p1, [128, n], [1, 128]), [tm])
                        rel(b1, ta)
                    vv_free[0] = (tm,)
                later.append(to_tokens)
            else:
                o = lo3[:, m - 12, :]
                ts_ = shift(m, o, TW)
                if m == 12:
                    act(o, o, ACT.Tanh, w=[ts_])
                if m == 14:
                    act(o, o, ACT.Sigmoid, w=[ts_])
        return tc
    gemm_fm(I["w_in"], 0, 1920, 8, (hL, hC), lambda m: SEGS[0:1] if m < 4 else SEGS, ev_u)
    b, pv, bw = bank()
    for f in range(4):
        rk = ub[:, f % 2, 0:512]
        vtt(rk, rT[:, f, :], kT[:, f, 0:512], MUL, ub_free[f % 2])
        tv = vts(rk, rk, VC["rk"][:, f:f + 1], None, MUL)
        for i in range(4):
            t = mm(pv[:, 8 * i + 2 * f:8 * i + 2 * f + 2], rk[:, 128 * i:128 * i + 128], C["b2"][:, 0:2], True, True,
                   bw + [tv] if i == 0 else (), i == 3)
        ub_free[f % 2] = (t,)
    t = vcopy(bonus, view(pv, [8, 4], [1, 8]), [t])
    rel(b, t)
    lend = borrow()
    top[0] = mk2
    top_, top[0] = top[0], mk_c
    kkT = view(al(4 * TW), [TW, 4], [1, TW])
    w2s, a2s = al(504 + 8), lend(512)
    assert top[0] <= mk
    top[0] = top_
    t_w2 = load_small(w2s, I["rw_w2"].rearrange("l d k c -> (l d k) c"))
    t_a2 = load_small(a2s, I["rw_a2"].rearrange("l d k c -> (l d k) c"))
    sqk = lend(TW)
    for f in range(4):
        o = kT[:, f, :]
        kr = kkT[:, f, :]
        vts(kr, o, VC["kk"][:, f:f + 1], None, MUL)
        tk_ = vtt(sqk, kr, kr, MUL)
        b1, p1, w1 = bank()
        b2, p2, w2 = bank()
        mm(p1, C["blk"], sqk[:, 0:512], True, True, w1 + [tk_])
        tm = mm(p2[:, 0:TW - 512], C["blk"], sqk[:, 512:TW], True, True, w2, True)
        act(sqk[:, 0:512], p1, ACT.Sqrt, w=[tm])
        ta = act(sqk[:, 512:TW], p2[:, 0:TW - 512], ACT.Sqrt)
        rel(b1, ta)
        rel(b2, ta)
        vts(sqk, sqk, 1e-12, None, MAX, w=[ta])
        recip(sqk, sqk)
        vtt(kr, kr, sqk, MUL)
    barrier()

    lend = borrow()
    lend(512)
    hx = view(lend(8 * 512), [512, 8], [1, 512])
    t = vtt(hx, R(hL[:, 0]), R(hL[:, 1]), ADD)
    t_spill = load_small(I["spill"], hx, [t])
    lend = borrow()
    lend(512)
    for q in (P, V, S, G):
        q.wait([t_spill])
    o_hl = [0]
    hflat = al_at(mk_hT, 8192)

    def room(n):
        if o_hl[0] + n <= 8192:
            o_hl[0] += n
            return hflat[:, o_hl[0] - n:o_hl[0]]
        if top[0] + n <= ARENA:
            return al(n)
        return lend(n)
    Ya = view(room(4 * 512), [512, 4], [1, 512])
    rsw = room(512)
    vcopy(view(rsw, [128, 4], [1, 128]), rep(C["rs64"], 4))
    written = set()

    def f4(x):
        return view(x, [128, 4], [1, 128])

    def rwkv_stream(d, SA, La, Ep, En, KKp, Rp, BK, TK, MB, AK, TT, AT, X, St, UV, PCM):
        Sg, Aa = SA[:, 0:512], SA[:, 512:1024]
        T, Xs = SA, En
        vset(St, 0.0)
        ends = [(V, V.n)]
        S.wait(ends)
        cur = 0
        uv = 0
        uv_free = [(), ()]
        BN = view(BK, [256, 4], [128, 2], [1, 64])
        KN = view(BK[:, 64:128], [256, 4], [128, 2], [1, 64])
        c4 = lambda x: view(x, [128, 4], [64, 2], [1, 64])
        c8 = lambda x: view(x, [64, 8], [1, 64])
        strict, incl = (("SU", 0), ("SU", 1)) if d == 0 else (("SL", 0), ("SL", 1))
        for pos in range(6):
            ti = SEQ_[d][pos]
            a0_ = TO[ti]
            lat = ti >= 2
            for q in (V, S, G):
                q.wait(ends)
            b, pv, bw = bank()
            b2, pv2, bw2 = bank()
            for f in range(4):
                mm(pv[:, 128 * f:128 * f + 128], w2s[64 * d:64 * d + 64, 128 * f:128 * f + 128],
                   lo3[64 * d:64 * d + 64, 0, a0_:a0_ + 128], True, True, bw + [t_w2] if f == 0 else ())
            for f in range(4):
                t = mm(pv2[:, 128 * f:128 * f + 128], a2s[64 * d:64 * d + 64, 128 * f:128 * f + 128],
                       lo3[64 * d:64 * d + 64, 1, a0_:a0_ + 128], True, True, bw2 + [t_a2] if f == 0 else (), f == 3)
            for f in range(4):
                t1 = act(Sg[:, 128 * f:128 * f + 128], pv[:, 128 * f:128 * f + 128], ACT.Tanh, scale=0.5,
                         bias=nwa[:, 4 * d + f:4 * d + f + 1], w=[t])
            rel(b, t1)
            for f in range(4):
                t = act(Aa[:, 128 * f:128 * f + 128], pv2[:, 128 * f:128 * f + 128], ACT.Tanh, scale=0.5,
                        bias=nwa[:, 8 + 4 * d + f:9 + 4 * d + f])
            rel(b2, t)
            yield
            t1 = t = vts(SA, SA, 0.5, 0.5, MUL, ADD, w=[t])
            last = view(La[:, 63:64], [64, 8], [0, 64])
            tl = scan(La, rsw, Sg, MUL, ADD, [t1])
            if d == 1:
                vtt(c8(Ep), last, c8(La), SUB)
                tl = vtt(La, Ep, Sg, ADD)
            yield
            act(Ep, La, ACT.Exp, scale=-KAP, w=[tl])
            te = act(En, La, ACT.Exp, scale=KAP)
            yield
            tl = vtt(La, La, Sg, SUB, [te])
            te = act(La, La, ACT.Exp, scale=-KAP, w=[tl])
            kks, ksl = kkT[:, :, a0_:a0_ + 128], kT[:, :, a0_:a0_ + 128]
            kks2 = view(kkT[:, 0, a0_:a0_ + 1], [TW, 4], [64, 2], [1, 64])
            ksl2 = view(kT[:, 0, a0_:a0_ + 1], [TW, 4], [64, 2], [1, 64])
            yield
            vtt(BN, kks2, c4(Aa), MUL, [t])
            t_b = stt(BN, BN, -1.0, c4(En), MUL, MUL)
            yield
            for f in range(4):
                vts(Aa[:, 128 * f:128 * f + 128], Aa[:, 128 * f:128 * f + 128], VC["ka"][:, f:f + 1], kam[:, f:f + 1],
                    MUL, ADD)
            yield
            vtt(KN, ksl2, c4(Aa), MUL)
            t_k = vtt(KN, KN, c4(En), MUL)
            yield
            if lat:
                vtt(f4(Rp), rT[:, :, a0_:a0_ + 128], f4(Ep), MUL)
            t_kk = vtt(f4(KKp), kks, f4(La), MUL, [te])
            yield
            for x in (T, TT):
                vcopy(view(x, [128, 8], [1, 128]), rep(C["ident"], 8))
            for p in (0, 1):
                b, pv, bw = bank()
                for f in range(4):
                    t = tr(pv[:, 128 * f:128 * f + 128], BK[:, 256 * f + 128 * p:256 * f + 128 * p + 128],
                           bw + [t_k] if f == 0 else (), f == 3)
                t_tok = scopy(TK[:, 512 * p:512 * p + 512], pv, [t])
                rel(b, t_tok)
            q4 = lambda x: view(x, [64, 4], [1, 64])
            for g in range(2):
                hp = HALF[g]
                b, pv, bw = bank()
                b2, pv2, bw2 = bank()
                kk_ = lambda i: KKp[hp, 128 * i:128 * i + 128]
                bb_ = lambda i: view(BK[hp, 256 * i:256 * i + 64], [128, 2], [1, 64])
                for i in range(4):
                    t0 = mm(pv[:, 128 * i:128 * i + 128], kk_(i), bb_(i), True, True, bw + [t_kk] if i == 0 else (), i == 3)
                for p in (0, 1):
                    for i in range(4):
                        t = mm(pv2[HALF[p], 128 * i:128 * i + 128], BK[hp, 256 * i + 128 * p:256 * i + 128 * p + 64],
                               kk_(i), True, True, bw2 if i + p == 0 else (), i == 3 and p == 1)
                m0, n0 = (rep(C[k], 4).bitcast(U32) for k in (("M0", "N0") if d == 0 else ("N0", "M0")))
                hv = lambda x: view(x[:, 128 * g:128 * g + 128], [256, 4], [1, 128])
                t0 = cpred(hv(T), m0, view(pv, [128, 4], [1, 128]), [t0])
                rel(b, t0)
                t1 = cpred(hv(TT), n0, view(pv2, [128, 4], [1, 128]), [t])
                t = scopy(hv(AT), view(pv2, [128, 4], [1, 128]), [t1])
                rel(b2, t)
                yield
            w = [t1, t]
            yield
            for g in range(2):
                hp = HALF[g]
                o3 = lambda x, r: view(x[r, 64 * g:64 * g + 64], [512, 2], [128, 4], [1, 64])
                b, pv, bw = bank()
                for p in (0, 1):
                    for i in range(4):
                        t = mm(pv[64:128, 256 * p + 64 * i:256 * p + 64 * i + 64],
                               BK[hp, 256 * i + 128 * p + 64:256 * i + 128 * p + 128],
                               KKp[hp, 128 * i + 64 * p:128 * i + 64 * p + 64], True, True,
                               bw if i + p == 0 else (), i == 3 and p == 1)
                msk = lambda k, r: view(C[k[0]][r, 64 * k[1]:64 * k[1] + 64], [0, 2], [0, 4], [1, 64])
                t_mat = vtt(o3(AK, HALF[1]), view(pv[64:128], [256, 2], [64, 4], [1, 64]), msk(strict, HALF[1]), MUL, [t])
                rel(b, t_mat)
                if lat:
                    b, pv, bw = bank()
                    for p in (0, 1):
                        for i in range(4):
                            t = mm(pv[:, 256 * p + 64 * i:256 * p + 64 * i + 64],
                                   BK[hp, 256 * i + 128 * p:256 * i + 128 * p + 128],
                                   Rp[hp, 128 * i + 64 * p:128 * i + 64 * p + 64], True, True,
                                   bw if i + p == 0 else (), i == 3 and p == 1)
                    t_mat = vtt(o3(MB, slice(0, 128)), view(pv, [256, 2], [64, 4], [1, 64]), msk(incl, slice(0, 128)),
                                MUL, [t])
                    rel(b, t_mat)
                yield
            for x in invert(T, TT, AT, X, d == 0, w):
                if x:
                    w_inv = x
                yield
            w_inv = w_inv + [t_mat, t_tok]
            for p in ((0, 1) if d == 0 else (1, 0)):
                r_ = HALF[p]
                edge = 64 * p + 63 if d == 0 else 64 * p
                S0, S1 = St[:, 512 * cur:512 * cur + 512], St[:, 512 * (1 - cur):512 * (1 - cur) + 512]
                uv_ = UV[:, 512 * uv:512 * uv + 512]
                tg = gcopy(uv_[64:128], vt[r_, ti, :], uv_free[uv])
                tp = G.op(lambda ep=view(Ep[:, edge:edge + 1], [128, 4], [0, 128]):
                          nc.gpsimd.tensor_tensor(f4(PCM), ep, rep(C["blk"], 4), MUL), [(V, V.n)])
                b, pv, bw = bank()
                for i in range(4):
                    mm(pv[r_, 128 * i:128 * i + 128], KKp[:, 128 * i + 64 * p:128 * i + 64 * p + 64],
                       S0[:, 128 * i:128 * i + 128], True, False, bw + w_inv + [(V, V.n), tg] if i == 0 else ())
                    for g in range(2):
                        c_ = 128 * i + 64 * g
                        t = mm(pv[r_, c_:c_ + 64], AK[64:128, 512 * p + c_:512 * p + c_ + 64], uv_[64:128, c_:c_ + 64],
                               False, g == 1, (), i == 3 and g == 1)
                t = vcopy(Xs[r_, :], pv[r_, :], [t])
                rel(b, t)
                yield
                b, pv, bw = bank()
                for h in range(8):
                    c_ = 64 * h
                    t = mm(pv[0:64, c_:c_ + 64], TT[r_, 2 * c_ + 64 * p:2 * c_ + 64 * p + 64], Xs[r_, c_:c_ + 64], True, True,
                           bw + [t] if h == 0 else (), h == 7)
                tu = scopy(uv_[0:64, :], pv[0:64, :], [t])
                rel(b, tu)
                yield
                b, pv, bw = bank()
                for i in range(4):
                    f_ = slice(128 * i, 128 * i + 128)
                    t = mm(pv[:, f_], TK[:, 512 * p + 128 * i:512 * p + 128 * i + 128], uv_[:, f_], True, True,
                           bw + [tu] if i == 0 else (), i == 3)
                vtt(S1, S0, pv, ADD, [t])
                ts_ = vtt(S1, S1, PCM, MUL, [tp])
                rel(b, ts_)
                if lat:
                    b, pv, bw = bank()
                    for i in range(4):
                        mm(pv[r_, 128 * i:128 * i + 128], Rp[:, 128 * i + 64 * p:128 * i + 64 * p + 64],
                           S0[:, 128 * i:128 * i + 128], True, False, bw if i == 0 else ())
                        for g in range(2):
                            c_ = 128 * i + 64 * g
                            t = mm(pv[r_, c_:c_ + 64], MB[:, 512 * p + c_:512 * p + c_ + 64], uv_[:, c_:c_ + 64],
                                   False, g == 1, (), i == 3 and g == 1)
                    y_ = Ya[r_, ti - 2, :]
                    if (ti, p) in written:
                        t1 = vtt(y_, y_, pv[r_, :], ADD, [t])
                    else:
                        written.add((ti, p))
                        t1 = vcopy(y_, pv[r_, :], [t])
                    rel(b, t1)
                uv_free[uv] = (t,)
                uv = 1 - uv
                cur = 1 - cur
                yield
            ends = [(P, P.n), (V, V.n), (S, S.n), (G, G.n)]

    sizes = (1024,) + (512,) * 5 + (1024,) * 9
    interleave(*[rwkv_stream(d, *[room(n) for n in sizes], tmp_op[:, 512 * d:512 * d + 512]) for d in range(2)], lag=20)
    barrier()
    lend = borrow()
    lend(512)
    Xs, g2f, lw_, lb_, bv = (lend(512) for _ in range(5))
    hx = view(lend(8 * 512), [512, 8], [1, 512])
    Yb = view(lend(4 * 512), [512, 4], [1, 512])
    vcopy(Yb, Ya)
    Ya = Yb
    t_hx = load_small(hx, I["spill"])
    t_l = [load_small(g2f, I["rw_g2"][0]), load_small(lw_, row(I["rw_lnw"][0, :], 512)),
           load_small(lb_, row(I["rw_lnb"][0, :], 512))]
    for i in range(4):
        y_ = Ya[:, i, :]
        group_norm(y_, 8, 64, 64e-5, small, Xs, True)
        vtt(y_, y_, lw_, MUL, t_l)
        vtt(y_, y_, lb_, ADD)
        vtt(view(bv, [64, 8], [1, 64]), view(vt[:, 2 + i, :], [64, 8], [1, 64]), view(bonus[:, i, :], [1, 8], [0, 64]), MUL)
        vtt(y_, y_, bv, ADD)
        b, pv, bw = bank()
        t = mm(pv, lo3[:, 2, 128 * i:128 * i + 128], g2f, True, True, bw + t_l, True)
        t = vtt(y_, y_, pv, MUL, [t])
        rel(b, t)
    to_fm([Ya[:, i, :] for i in range(4)], 4, lambda f: yaT[:, f, :], None, [t])
    split_x(hx, hL, [t_hx, t])
    ring_back(barrier())
    top[0] = mk_c

    modulate(3)
    modulate(4)
    t_sc = norm_scale(sc2, 4, "g2")
    mk = top[0]
    z = view(al(4 * 8 * 94), [8 * 94, 4], [94, 8], [1, 94])
    cacc = view(al(4 * 512), [512, 4], [1, 512])
    ybT = cacc
    mk5 = top[0]
    cga = view(al(4 * 512), [512, 4], [1, 512])
    t_z = vset(z, 0.0)

    def ev_a(m, g, pv, t):
        return scopy(cga[:, m, :], pv, [t])

    def ev_g(m, g, pv, t):
        t = act(sq4[:, m, :], pv, ACT.Sigmoid, w=[t])
        t1 = vtt(z[:, m, :, 15:79], view(cga[:, m, :], [64, 8], [1, 64]), view(sq4[:, m, :], [64, 8], [1, 64]), MUL, [t])
        return t1
    sq4 = view(al(4 * 512), [512, 4], [1, 512])
    gemm_fm(I["w_in"], CVO, 512, 8, hL, lambda m: [(0, 512)], ev_a)
    gemm_fm(I["w_in"], CVO + 512, 512, 8, hL, lambda m: [(0, 512)], ev_g)
    barrier()
    top[0] = mk5

    def conv_steps():
        for f in range(4):
            o = view(cacc[:, f, :], [64, 8], [1, 64])
            cd = VC["cdw"][:, 31 * f:31 * f + 31]
            vts(o, z[:, f, :, 0:64], cd[:, 0:1], VC["cdb"][:, f:f + 1], MUL, ADD)
            for k in range(1, 31):
                stt(o, z[:, f, :, k:k + 64], cd[:, k:k + 1], o, MUL, ADD)
                if k % 4 == 0:
                    yield
    conv = conv_steps()

    mg = view(al(4 * 1024), [1024, 4], [1, 1024])
    mrow = al(1024)
    sg = [tmp_op[:, 0:512], tmp_op[:, 512:1024], mrow[:, 0:512], mrow[:, 512:1024]]
    mk4 = top[0]
    yop = opnd(4, 512)

    def conv_norm():
        for _ in conv:
            pass
        yflat = view(yop, [1, 4096])
        sq4 = view(yflat[:, 0:2048], [512, 4], [1, 512])
        t = (V, V.n)
        V.wait([(P, P.n)])
        S.wait([(P, P.n)])
        b, pv, bw = bank()
        for f in range(4):
            t = mm(pv, C["ones"], cacc[:, f, :], f == 0, f == 3, bw + [t] if f == 0 else (), f == 3)
        mean = yflat[:, 2048:2560]
        t = scopy(mean, pv, [t], scale=1.0 / 512)
        rel(b, t)
        t = vtt(cacc, cacc, rep(mean, 4, 512), SUB, [t])
        t = vtt(sq4, cacc, cacc, MUL)
        b, pv, bw = bank()
        for f in range(4):
            t = mm(pv, C["ones"], sq4[:, f, :], f == 0, f == 3, bw + [t] if f == 0 else (), f == 3)
        rs = yflat[:, 2560:3072]
        t = vts(rs, pv, 1.0 / 512, 1e-5, MUL, ADD, w=[t])
        rel(b, t)
        t = act(rs, rs, ACT.Sqrt, w=[t])
        t = recip(rs, rs, [t])
        t = vtt(cacc, cacc, rep(rs, 4, 512), MUL)
        for f in range(4):
            act(ybT[:, f, :], cacc[:, f, :], ACT.Silu, scale=VC["clw"][:, f:f + 1], bias=VC["clb"][:, f:f + 1], w=[t])

    for br, y_, pw in ((0, yaT, "p_a"), (2, ycT, "p_c"), (1, ybT, "p_b")):
        yt = None
        if br == 1:
            conv_norm()
            V.wait([(S, S.n), (P, P.n)])
            S.wait([(P, P.n)])
        for hf in range(2):
            gemm_tm(I["w_in"], GO + 1024 * br + 512 * hf, 512, 8, hL, W512,
                    lambda c, i, pv, t, n: act(sg[i], pv, ACT.Sigmoid, w=[t, (V, V.n)]))
            if hf == 0:
                yt = split_x(y_, yop, [(P, P.n)])

            def ev_m(c, i, pv, t, n, br=br, hf=hf):
                o = mg[:, i, 512 * hf:512 * hf + 512]
                if br == 0:
                    t1 = vtt(o, sg[i], pv, MUL, [t, (S, S.n)])
                else:
                    t1 = vtt(sg[i], sg[i], pv, MUL, [t, (S, S.n)])
                    vtt(o, o, sg[i], ADD)
                if br != 1:
                    next(conv, None)
                    next(conv, None)
                return t1
            gemm_tm(I[pw], 512 * hf, 512, 4, yop, W512, ev_m, yt)
    top[0] = mk4
    bcast_rows(mrow, 2)
    x1 = view(al(4 * 1024), [1024, 4], [1, 1024])
    tx = [load_small(x1[:, i, :], I["x"][0, 128 * i:128 * i + 128, :], [(P, P.n)]) for i in range(4)]
    t = to_op([mg[:, i, :] for i in range(4)], 8, hL, w=[(V, V.n)])

    def ev_o(c, i, pv, t, n):
        o = mg[:, i, c:c + 512]
        t1 = vtt(o, pv, mrow[:, c:c + 512], MUL, [t])
        vtt(x1[:, i, c:c + 512], x1[:, i, c:c + 512], o, ADD, tx)
        return t1
    gemm_tm(I["w_out"], 0, 1024, 8, hL, W512, ev_o, xt=t)
    barrier()
    top[0] = mk_y
    x1b = view(al(4 * 1024), [1024, 4], [1, 1024])
    xc = view(al(4 * 1024), [1024, 4], [1, 1024])
    mk3 = top[0]
    scr = al(1024)
    vcopy(x1b, x1)
    barrier()
    x1 = x1b
    t = vcopy(xc, x1)
    norm_mod_op([xc[:, i, :] for i in range(4)], 0, sc2, mod[:, 24:32, :], hL, scr, t_sc, [[t]] * 4)
    barrier()
    top[0] = mk3 - 4096
    mrow = al(1024)
    bcast_rows(mrow, 5)
    hop = opnd(8, 512)
    tmp = al(2048)
    for part in range(4):
        ht = []

        def ev_1(m, g, pv, t):
            o = tmp[:, 512 * (m % 2):512 * (m % 2) + 512]
            o2 = tmp[:, 1024 + 512 * (m % 2):1536 + 512 * (m % 2)]
            t1 = act(o, pv, ACT.Relu, w=[t, (V, V.n)])
            t2 = vtt(o2, o, o, MUL, [t1])
            t3 = act(R(hop[:, 0, m, :]), o2, ACT.Copy, w=[t2, free_h])
            ht.append(vtt(R(hop[:, 1, m, :]), o2, R(hop[:, 0, m, :]), SUB, [t3]))
            return t1
        free_h = (P, P.n)
        gemm_fm(I["w_mlp1"], 1024 * part, 1024, 8, hL, lambda m: [(0, 512)], ev_1)

        def ev_2(c, i, pv, t, n):
            o = tmp[:, 512 * (i % 2):512 * (i % 2) + 512]
            t1 = vtt(o, pv, mrow[:, c:c + 512], MUL, [t])
            vtt(x1[:, i, c:c + 512], x1[:, i, c:c + 512], o, ADD)
            return t1
        gemm_tm(I["w_mlp2"], 0, 1024, 8, hop, W512, ev_2, r0=1024 * part, xt=ht)
    barrier()
    top[0] = mk3 - 4096
    gfr = al(1024)
    scr = al(1024)
    t_g = load_small(gfr, row(I["g_final"], 1024))
    for i in range(4):
        t = rms_scales(small[:, i:i + 1], x1[:, i, :], scr, [(V, V.n)])
        stt(x1[:, i, :], x1[:, i, :], small[:, i:i + 1], gfr, MUL, MUL, [t, t_g])
    barrier()

    hX = x1
    hh = hL
    top[0] = mk_y + 4096
    cosT, sinT = al(512), al(512)
    base = top[0]
    ALPHA = 4.0 ** 0.25
    RP = slice(64, 96)

    pos_i = al(512).bitcast(I32)
    ang, kk_, wk = al(512), al(512), al(512)
    t = load_small(pos_i[RP, :], bass.AP(I["positions_2"].tensor, 0, [[0, 32], [1, 512]]))
    vcopy(ang[RP, :], pos_i[RP, :], [t])
    vts(ang[RP, :], ang[RP, :], C["rope"][RP, 0:1], None, MUL)
    MAGIC = 12582912.0
    C1 = 6.28125
    C2 = float(np.float32(2 * np.pi - C1))
    C3 = float(2 * np.pi - C1 - np.float64(np.float32(2 * np.pi - C1)))
    for dst, ph in ((sinT, 0.0), (cosT, 0.25)):
        k_, w_ = kk_[RP, :], wk[RP, :]
        vts(k_, ang[RP, :], 1.0 / (2 * np.pi), ph, MUL, ADD)
        vts(k_, k_, MAGIC, None, ADD)
        vts(k_, k_, MAGIC, None, SUB)
        stt(w_, k_, -C1, ang[RP, :], MUL, ADD, [(S, S.n)])
        stt(w_, k_, -C2, w_, MUL, ADD)
        stt(w_, k_, -C3, w_, MUL, ADD)
        if ph:
            vts(w_, w_, float(np.pi / 2), None, ADD)
        vts(w_, w_, 3.1415925, -3.1415925, MIN, MAX)
        act(dst[RP, :], w_, ACT.Sin, w=[(V, V.n)])
    vts(sinT[RP, :], sinT[RP, :], C["rope"][RP, 1:2], None, MUL, w=[(S, S.n)])
    barrier()
    top[0] = base

    def hT_from_x():
        t = to_op([hX[:, i, :] for i in range(4)], 8, hh, w=[(V, V.n), (P, P.n)])
        P.wait(t)
        return t

    def layer_norm_all(l, j):
        m_ = top[0]
        gr, br_ = al(1024), al(1024)
        e = barrier()
        tg = [load_small(gr, row(I["ln_g_2"][l, j, :], 1024)), load_small(br_, row(I["ln_b_2"][l, j, :], 1024))]
        for i in range(4):
            x_ = hX[:, i, :]
            layer_norm_tile(x_, x_, 1024, 1e-5, small)
            vtt(x_, x_, gr, MUL, tg)
            vtt(x_, x_, br_, ADD)
        t = hT_from_x()
        barrier()
        top[0] = m_
        return t

    def ffn(l, wi, wo, j):
        m_ = top[0]
        hop = opnd(8, 512)
        tmp = al(2048)
        Wi, Wo = I[wi][l], I[wo][l]
        for part, nt in enumerate((8, 8, 6)):
            ht = []
            free_h = (P, P.n)
            for m in range(nt):
                c_ = 1024 * part + 128 * m
                z, wh, wl, tok = wload([
                    (lambda x: view(x, [256, 8], [1, 128]), Wi[:, c_:c_ + 128].rearrange("(k p) c -> p k c", p=128)),
                    (lambda x: view(x[:, 128:256], [256, 8], [1, 128]),
                     Wi[:, 2816 + c_:2816 + c_ + 128].rearrange("(k p) c -> p k c", p=128))], 2048)
                wh, wl = view(wh, [256, 8], [1, 256]), view(wl, [256, 8], [1, 256])
                b, pv, bw = bank()
                b2, pv2, bw2 = bank()
                for u_, (o_, w_) in enumerate(((pv, bw), (pv2, bw2))):
                    js = slice(128 * u_, 128 * u_ + 128)
                    for k in range(8):
                        t = mm3(o_, (wh[:, k, js], wl[:, k, js]), (R(hh[:, 0, k, :]), R(hh[:, 1, k, :])), k == 0, k == 7,
                                w_ + [tok] if k == 0 else (), k == 7)
                used(z, t)
                o = tmp[:, 512 * (m % 2):512 * (m % 2) + 512]
                o2 = tmp[:, 1024 + 512 * (m % 2):1536 + 512 * (m % 2)]
                t1 = act(o, pv, ACT.Silu, w=[t, (V, V.n)])
                rel(b, t1)
                t2 = vtt(o2, o, pv2, MUL, [t1])
                rel(b2, t2)
                t3 = act(R(hop[:, 0, m, :]), o2, ACT.Copy, w=[t2, free_h])
                ht.append(vtt(R(hop[:, 1, m, :]), o2, R(hop[:, 0, m, :]), SUB, [t3]))

            def ev(c, i, pv, t, n, part=part):
                o = tmp[:, 512 * (i % 2):512 * (i % 2) + 512]
                x_ = hX[:, i, c:c + 512]
                if part == 0:
                    t1 = act(o, pv, ACT.Copy, scale=0.5, w=[t, (V, V.n)])
                    stt(x_, x_, ALPHA, o, MUL, ADD, [t1])
                else:
                    t1 = stt(x_, pv, 0.5, x_, MUL, ADD, [t])
                return t1
            gemm_tm(Wo, 0, 1024, nt, hop, W512, ev, r0=1024 * part, xt=ht)
        barrier()
        top[0] = m_
        layer_norm_all(l, j)

    def mixer(l):
        m0_ = top[0]
        Wm = I["mix_w_in_2"][l]
        m1_ = top[0]
        qk = view(al(8 * 512), [512, 8], [1, 512])
        vtok = view(al(4 * 512), [512, 4], [1, 512])
        gz = view(al(4 * 512), [512, 4], [1, 512])
        gab = view(al(4 * 16), [16, 4], [1, 16])
        ktok = view(al(4 * 512), [512, 4], [1, 512])
        m2_ = top[0]
        ub = view(al(2 * 516), [516, 2], [1, 516])
        cv = view(al(2 * 512), [512, 2], [1, 512])
        sq_, rn = tmp_op, al(512)
        hb = view(ktok, [1, 1024])
        for q_ in (0, 1):
            b, pv, bw = bank()
            for i in range(4):
                m = 4 * q_ + i
                t = tr(pv[0:16, 128 * i:128 * i + 128], C["hs"][:, 16 * m:16 * m + 16], bw if i == 0 else (), i == 3)
            t_hb = scopy(hb[0:16, 512 * q_:512 * q_ + 512], pv[0:16, :], [t])
            rel(b, t_hb)
        b_s, pv_s, bw_s = bank()
        sq_free = [(), ()]
        t0 = vset(ub, 0.0)
        ubf = [(t0,), (t0,)]
        cvf = [(), ()]
        cw = VC[f"gcw{l}"]

        later = []

        def ev_c(m, g, pv, t):
            while later:
                later.pop(0)()
            u = ub[:, m % 2, :]
            tc = scopy(u[:, 3:515], pv, [t] + list(ubf[m % 2]))
            o = cv[:, m % 2, :]
            vts(o, u[:, 0:512], cw[:, 4 * m:4 * m + 1], None, MUL, w=[tc] + list(cvf[m % 2]))
            for k in range(1, 4):
                tv = stt(o, u[:, k:k + 512], cw[:, 4 * m + k:4 * m + k + 1], o, MUL, ADD)
            ubf[m % 2] = (tv,)
            if m < 8:
                dst = qk[:, m, :]
                ta = act(dst, o, ACT.Silu, w=[tv])
                cvf[m % 2] = (ta,)
                x = sq_[:, 512 * (m % 2):512 * (m % 2) + 512]
                tv = vtt(x, dst, dst, MUL, [ta] + list(sq_free[m % 2]))

                def head_sums(m=m, x=x, tv=tv):
                    tm = mm(pv_s[0:16, :], C["hs"][:, 16 * m:16 * m + 16], x, m == 0, m == 7,
                            (bw_s if m == 0 else []) + [tv], True)
                    sq_free[m % 2] = (tm,)
                later.append(head_sums)
            else:
                ta = act(o, o, ACT.Silu, w=[tv])

                def to_tokens(m=m, o=o, ta=ta):
                    b, p1, bw = bank()
                    for i in range(4):
                        tm = tr(p1[:, 128 * i:128 * i + 128], o[:, 128 * i:128 * i + 128], bw + [ta] if i == 0 else (), i == 3)
                    ta = scopy(vtok[:, :, 128 * (m - 8):128 * (m - 8) + 128], view(p1, [128, 4], [1, 128]), [tm])
                    rel(b, ta)
                    cvf[m % 2] = (tm,)
                later.append(to_tokens)
            return tc
        gemm_fm(Wm, 0, 1536, 8, hh, lambda m: [(0, 512)], ev_c)
        while later:
            later.pop(0)()
        ts_ = vts(rn[0:16], pv_s[0:16, :], 1e-6, None, ADD, w=[(P, P.n)])
        rel(b_s, ts_)
        ta = act(rn[0:16], rn[0:16], ACT.Sqrt, w=[ts_])
        t_rn = recip(rn[0:16], rn[0:16], [ta])
        for m in range(8):
            b, pv, bw = bank()
            t = mm(pv, hb[0:16, 128 * m:128 * m + 128], rn[0:16], True, True, bw + [t_rn, t_hb], True)
            dst = qk[:, m, :]
            if m < 4:
                t = stt(dst, dst, 0.125, pv, MUL, MUL, [t])
            else:
                t = vtt(dst, dst, pv, MUL, [t])
            rel(b, t)
        gemm_tm(Wm, 1536, 512, 8, hh, W512, lambda c, i, pv, t, n: act(gz[:, i, :], pv, ACT.Silu, w=[t]))
        gemm_tm(Wm, 2048, 16, 8, hh, W512, lambda c, i, pv, t, n: vcopy(gab[:, i, :], pv[:, 0:16], [t]))
        barrier()
        top[0] = m2_
        al_, dtb = al(8), al(8)
        gg = view(al(32), [8, 4], [1, 8])
        ng = view(al(32), [8, 4], [1, 8])
        be = view(al(32), [8, 4], [1, 8])
        t8 = view(al(32), [8, 4], [1, 8])
        nbe = view(al(32), [8, 4], [1, 8])
        kde = view(al(32), [8, 4], [1, 8])
        egc = view(al(32), [8, 4], [1, 8])
        tl = [load_small(al_, row(I["gdn_a_log_2"][l, :], 8)), load_small(dtb, row(I["gdn_dt_bias_2"][l, :], 8))]
        ta = act(al_, al_, ACT.Exp, w=tl)
        vtt(gg, gab[:, :, 0:8], view(dtb, [0, 4], [1, 8]), ADD, tl)
        t = vcopy(t8, gg)
        act(t8, t8, ACT.Abs, w=[t])
        act(t8, t8, ACT.Exp, scale=-1.0)
        ta2 = act(t8, t8, ACT.Ln, bias=1.0)
        vts(gg, gg, 0.0, None, MAX)
        vtt(gg, gg, t8, ADD, [ta2])
        stt(gg, gg, -1.0, view(al_, [0, 4], [1, 8]), MUL, MUL, [ta])
        t = vts(ng, gg, -1.0, None, MUL)
        t = act(be, gab[:, :, 8:16], ACT.Sigmoid, w=[t])
        b, pv, bw = bank()
        mm(pv[:, 0:32], C["UI"], view(gg, [1, 32]), True, True, bw + [(V, V.n)])
        t = mm(pv[:, 32:64], C["blk"], view(gg, [1, 32]), True, True, (), True)
        act(view(egc, [1, 32]), pv[:, 0:32], ACT.Exp, w=[t])
        tg = scopy(view(t8, [1, 32]), pv[:, 0:32])
        gc = t8
        tg = vtt(view(kde, [1, 32]), pv[:, 32:64], view(t8, [1, 32]), SUB, [tg])
        rel(b, tg)
        tg = act(kde, kde, ACT.Exp, w=[tg])
        stt(nbe, be, -1.0, egc, MUL, MUL, [tg])
        nb_ = view(al(32), [8, 4], [1, 8])
        vts(nb_, be, -1.0, None, MUL)
        egl = view(al(64), [8, 8], [1, 8])
        b, pv, bw = bank()
        for c_ in range(8):
            t = mm(pv[:, 8 * c_:8 * c_ + 8], C[f"half{c_ % 2}"], gg[:, c_ // 2, :], True, True,
                   bw + [(V, V.n)] if c_ == 0 else (), c_ == 7)
        t_egl = act(view(egl, [1, 64]), pv[:, 0:64], ACT.Exp, w=[t])
        rel(b, t_egl)
        for i in range(4):
            b, pv, bw = bank()
            for f in range(4):
                t = tr(pv[:, 128 * f:128 * f + 128], qk[:, 4 + f, 128 * i:128 * i + 128], bw if f == 0 else (), f == 3)
            tk_ = vtt(view(ktok[:, i, :], [64, 8], [1, 64]), view(pv, [64, 8], [1, 64]), view(kde[:, i, :], [1, 8], [0, 64]),
                      MUL, [t, tg])
            rel(b, tk_)
            vtt(view(vtok[:, i, :], [64, 8], [1, 64]), view(vtok[:, i, :], [64, 8], [1, 64]),
                view(be[:, i, :], [1, 8], [0, 64]), MUL)
        lend = borrow()
        Og = view(al(4 * 512), [512, 4], [1, 512])
        St = [al(512), al(512), tmp_op[:, 0:512]]
        PCM = view(lend(512), [64, 8], [1, 64])
        Xs, Us, t1s = lend(512), lend(512), lend(512)
        TTs, QDs = [[lend(n) for _ in range(4)] for n in (1024, 512)]
        vset(St[0], 0.0)
        done = {}

        def prep(tiles, D_, NA, NAb, AT, T, X):
            tz = vset(NAb, 0.0)
            ends = [tz]
            for ti in tiles:
                for q in (V, S):
                    q.wait(ends)
                TT, QD = TTs[ti], QDs[ti]
                c_ = lambda p: slice(128 * ti + 64 * p, 128 * ti + 64 * p + 64)
                hv = lambda x: view(x[:, ti, :], [1, 8], [0, 64])
                g4 = lambda x, g: view(x[:, 64 * g:64 * g + 64], [128, 4], [1, 64])
                q4 = lambda x: view(x[:, 0:256], [64, 4], [1, 64])
                t = vtt(h8(NA), mask8("SU", 1), hv(ng), MUL)
                b, pv, bw = bank()
                mm(pv, C["blk"], NA, True, False, bw + [t])
                t = mm(pv, C["ident"], mask8("SI", 1), False, True, (), True)
                t = vtt(h8(D_), h8(pv), hv(gc), ADD, [t])
                rel(b, t)
                td = act(D_, D_, ACT.Exp, w=[t])
                yield
                for g in range(2):
                    hp = HALF[g]
                    b, pv, bw = bank()
                    for p in (0, 1):
                        for i in range(4):
                            t = mm(pv[HALF[p], 64 * i:64 * i + 64], qk[hp, 4 + i, c_(p)], qk[hp, 4 + i, c_(p)], True, True,
                                   bw if i + p == 0 else (), i == 3 and p == 1)
                    t1 = vtt(g4(NA, g), q4(pv), g4(D_, g), MUL, [t, td])
                    rel(b, t1)
                t1 = vtt(h8(NA), h8(NA), hv(nb_), MUL)
                for p in (0, 1):
                    t2 = scopy(diag(NAb, p), h8(NA[HALF[p]]), [t1])
                for g in range(2):
                    hp = HALF[g]
                    b, pv, bw = bank()
                    for p in (0, 1):
                        for i in range(4):
                            t = mm(pv[HALF[p], 64 * i:64 * i + 64], qk[hp, i, c_(p)], qk[hp, 4 + i, c_(p)], True, True,
                                   bw if i + p == 0 else (), i == 3 and p == 1)
                    t1 = vtt(g4(D_, g), q4(pv), g4(D_, g), MUL, [t])
                    rel(b, t1)
                d8 = lambda x: view(x, [128, 8], [1, 128])
                vcopy(d8(T), rep(C["ident"], 8))
                vcopy(d8(TT), rep(C["ident"], 8))
                cpred(d8(T), rep(C["M0"], 8).bitcast(U32), d8(NAb), [t2])
                yield
                for q_ in (0, 1):
                    b, pv, bw = bank()
                    for h in range(4):
                        c0 = 512 * q_ + 128 * h
                        t = tr(pv[:, 128 * h:128 * h + 128], NAb[:, c0:c0 + 128], bw + [t2] if h == 0 else (), h == 3)
                    t3 = scopy(AT[:, 512 * q_:512 * q_ + 512], pv, [t])
                    rel(b, t3)
                t4 = cpred(d8(TT), rep(C["N0"], 8).bitcast(U32), d8(AT), [t3])
                S.wait([t4])
                for p in (0, 1):
                    t2 = scopy(diag(NAb, p), h8(D_[HALF[p]]), [t1])
                yield
                for q_ in (0, 1):
                    b, pv, bw = bank()
                    for h in range(4):
                        c0 = 512 * q_ + 128 * h
                        t = tr(pv[:, 128 * h:128 * h + 128], NAb[:, c0:c0 + 128], bw + [t2] if h == 0 else (), h == 3)
                    for p in (0, 1):
                        tq = scopy(view(QD[HALF[p], 256 * q_:256 * q_ + 64], [64, 4], [1, 64]),
                                   view(pv[HALF[p], 64 * p:64 * p + 64], [128, 4], [1, 64]), [t])
                    rel(b, tq)
                for x in invert(T, TT, AT, X, True, [t4]):
                    if x:
                        w_inv = x
                    yield
                done[ti] = w_inv + [tq]
                ends = [(P, P.n), (V, V.n), (S, S.n)]

        def recur():
            cur = 0
            pending = []
            col = lambda x, r_: view(x[r_, ti, :], [1, 8], [0, 64])
            for ti in range(4):
                while ti not in done:
                    yield
                TT, QD = TTs[ti], QDs[ti]
                for p in (0, 1):
                    r_ = HALF[p]
                    rt = slice(128 * ti + 64 * p, 128 * ti + 64 * p + 64)
                    S0, S1 = St[cur], St[(cur + 1) % 3]
                    ch = 2 * ti + p
                    egb = view(egl[:, ch, :], [2, 4], [1, 2], [0, 64])
                    G.op(lambda egb=egb: nc.gpsimd.tensor_tensor(view(PCM, [128, 4], [64, 2], [1, 64]), egb,
                                                                 view(C["blk"], [0, 4], [64, 2], [1, 64]), MUL),
                         [t_egl, (V, V.n), (P, P.n)])
                    tg = G.op(lambda S0=S0, S1=S1: nc.gpsimd.tensor_tensor(h8(S1), h8(S0), PCM, MUL))
                    b, pv, bw = bank()
                    for i in range(4):
                        t = mm(pv[r_, 128 * i:128 * i + 128], qk[:, 4 + i, rt], S0[:, 128 * i:128 * i + 128], True, True,
                               bw + done[ti] + [(V, V.n)] if i == 0 else (), i == 3)
                    vtt(h8(Xs[r_, :]), h8(pv[r_, :]), col(nbe, r_), MUL, [t])
                    t = vtt(Xs[r_, :], Xs[r_, :], vtok[r_, ti, :], ADD)
                    rel(b, t)
                    if pending:
                        pending.pop()()
                    yield
                    b, pv, bw = bank()
                    for h in range(8):
                        t = mm(pv[r_, 64 * h:64 * h + 64], TT[r_, 128 * h + 64 * p:128 * h + 64 * p + 64], Xs[r_, 64 * h:64 * h + 64], True, True,
                               bw + [t] if h == 0 else (), h == 7)
                    tu = scopy(Us[r_, :], pv[r_, :], [t])
                    rel(b, tu)
                    yield
                    b, pv, bw = bank()
                    for i in range(4):
                        f_ = slice(128 * i, 128 * i + 128)
                        t = mm(pv[:, f_], ktok[r_, ti, f_], Us[r_, f_], True, True, bw + [tu] if i == 0 else (), i == 3)
                    vtt(view(t1s, [128, 4], [1, 128]), view(pv, [128, 4], [1, 128]), rep(C["blk"], 4), MUL, [t])
                    ts_ = vtt(S1, S1, t1s, ADD, [tg])
                    rel(b, ts_)

                    def output(ti=ti, r_=r_, rt=rt, S0=S0, QD=QD):
                        b, pv, bw = bank()
                        b2, pv2, bw2 = bank()
                        for i in range(4):
                            mm(pv[r_, 128 * i:128 * i + 128], qk[:, i, rt], S0[:, 128 * i:128 * i + 128], True, True,
                               bw if i == 0 else ())
                        for h in range(8):
                            t = mm(pv2[r_, 64 * h:64 * h + 64], QD[r_, 64 * h:64 * h + 64], Us[r_, 64 * h:64 * h + 64], True, True,
                                   bw2 if h == 0 else (), h == 7)
                        y_ = Og[r_, ti, :]
                        vtt(h8(y_), h8(pv[r_, :]), view(egc[r_, ti, :], [1, 8], [0, 64]), MUL, [t])
                        t = vtt(y_, y_, pv2[r_, :], ADD)
                        rel(b, t)
                        rel(b2, t)
                    pending.append(output)
                    cur = (cur + 1) % 3
                    yield
            pending.pop()()
        sizes = (512, 512, 1024, 1024, 1024, 1024)
        interleave(prep((0, 2), *[lend(n) for n in sizes]), prep((1, 3), *[lend(n) for n in sizes]), recur(), lag=4)
        barrier()
        top[0] = m1_
        catT = view(al(8 * 512), [512, 8], [1, 512])
        m1_ = top[0]
        nr = t1s[:, 0:64]
        tn = load_small(nr, row(I["gdn_norm_w_2"][l, :], 64))
        for i in range(4):
            y_ = Og[:, i, :]
            group_norm(y_, 8, 64, 1e-6, small, Xs, False)
            vtt(view(y_, [64, 8], [1, 64]), view(y_, [64, 8], [1, 64]), view(nr, [0, 8], [1, 64]), MUL, [tn])
            t = vtt(y_, y_, gz[:, i, :], MUL)
        to_fm([Og[:, i, :] for i in range(4)], 4, lambda f: catT[:, f, :], None, [t])
        ring_back(barrier())
        top[0] = m1_

        sqk_ = view(al(4 * 512), [512, 4], [1, 512])
        sv = view(al(4 * 256), [256, 4], [1, 256])
        mq = view(al(4 * 256), [256, 4], [1, 256])
        ckv = view(al(4 * 128), [128, 4], [1, 128])
        krT = al(512)
        osb = view(al(4 * 256), [256, 4], [1, 256])
        gemm_fm(Wm, 2064, 512, 8, hh, lambda m: [(0, 512)],
                lambda m, g, pv, t: scopy(sqk_[:, m, :], pv, [t], scale=0.125 if m < 2 else 1.0))

        def ev_s(c, i, pv, t, n):
            scopy(sv[:, i, :], pv[:, 0:256], [t])
            return scopy(mq[:, i, :], pv[:, 256:512])
        gemm_tm(Wm, 2576, 512, 8, hh, W512, ev_s)
        gemm_tm(Wm, 3088, 128, 8, hh, W512, lambda c, i, pv, t, n: scopy(ckv[:, i, :], pv[:, 0:128], [t]))
        s, wv, wl, tok = chunk(I["kr2"][l], 0, 8, 0, 192)
        b, pv, bw = bank()
        b2, pv2, bw2 = bank()
        for k in range(8):
            mm3(pv[0:96, :], (wv[:, k, 0:96], wl[:, k, 0:96]), (R(hh[:, 0, k, :]), R(hh[:, 1, k, :])), k == 0, k == 7,
                bw + [tok] if k == 0 else ())
        for k in range(8):
            t = mm3(pv2[0:96, :], (wv[:, k, 96:192], wl[:, k, 96:192]), (R(hh[:, 0, k, :]), R(hh[:, 1, k, :])),
                    k == 0, k == 7, bw2 if k == 0 else (), k == 7)
        used(s, t)
        tmpr = al(512)

        def rope(dst, pa, pb, w):
            vtt(tmpr[RP, :], pa, cosT[RP, :], MUL, w)
            vtt(dst, pb, sinT[RP, :], MUL)
            return vtt(dst, dst, tmpr[RP, :], ADD)
        t_kr = rope(krT[RP, :], pv[RP, :], pv2[RP, :], [t])
        rel(b, t_kr)
        rel(b2, t_kr)
        lend = borrow()
        SP_ = [view(lend(4 * 512), [512, 4], [1, 512]) for _ in range(2)]
        WT = [view(lend(4 * 512), [512, 4], [1, 512]) for _ in range(2)]
        eb = [view(lend(4 * 512), [512, 4], [1, 512]) for _ in range(2)]
        wt_free = [(), ()]

        def softplus(h):
            hp = slice(64 * (h % 2), 64 * (h % 2) + 64)
            q_, k_ = sqk_[hp, h // 2, :], sqk_[hp, 2 + h // 2, :]
            SPh, E_ = SP_[h % 2], eb[h % 2]
            for s_ in range(4):
                lo = 128 * s_
                N = 512 - lo
                b, pv, bw = bank()
                t = mm(pv[:, 0:N], k_[:, lo:lo + 128], q_[:, lo:512], True, True, bw, True)
                ta = act(E_[:, s_, lo:512], pv[:, 0:N], ACT.Abs, w=[t] + list(wt_free[h % 2]))
                rel(b, vts(SPh[:, s_, lo:512], pv[:, 0:N], 0.0, None, MAX, w=[ta] + list(wt_free[h % 2])))
                act(E_[:, s_, lo:512], E_[:, s_, lo:512], ACT.Exp, scale=-1.0)
            for s_ in range(4):
                lo = 128 * s_
                ta = act(E_[:, s_, lo:512], E_[:, s_, lo:512], ACT.Ln, bias=1.0)
                vtt(SPh[:, s_, lo:512], SPh[:, s_, lo:512], E_[:, s_, lo:512], ADD, [ta])
                tv = vtt(SPh[:, s_, lo:lo + 128], SPh[:, s_, lo:lo + 128], C["US128"], MUL)
            return tv

        def attend(h, tv):
            hp = slice(64 * (h % 2), 64 * (h % 2) + 64)
            q_, k_ = sqk_[hp, h // 2, :], sqk_[hp, 2 + h // 2, :]
            SPh, W_ = SP_[h % 2], WT[h % 2]
            for s_ in range(4):
                lo = 128 * s_
                N = 512 - lo
                b, pv, bw = bank()
                mm(pv[:, 0:N], k_[:, lo:lo + 128], q_[:, lo:512], True, False, bw + [tv])
                mm(pv[:, 0:N], C["nLI128"], SPh[:, s_, lo:512], False, False)
                for j_ in range(s_ + 1, 4):
                    o_ = 128 * (j_ - s_)
                    mm(pv[:, o_:N], C["none"], SPh[:, j_, 128 * j_:512], False, False)
                t = mm(pv[:, 0:128], C["ident"], C["negGE"], False, True, (), True)
                ta = act(W_[:, s_, lo:512], pv[:, 0:N], ACT.Exp, w=[t] + list(wt_free[h % 2]))
                rel(b, ta)

            def out_():
                b, pv, bw = bank()
                for i in range(4):
                    for s_ in range(i + 1):
                        t = mm(pv[:, 64 * i:64 * i + 64], W_[:, s_, 128 * i:128 * i + 128], sv[:, s_, 64 * h:64 * h + 64],
                               s_ == 0, s_ == i, bw + [ta] if i + s_ == 0 else (), i == 3 and s_ == 3)
                wt_free[h % 2] = (t,)
                tv = vcopy(osb[:, :, 64 * h:64 * h + 64], view(pv, [64, 4], [1, 64]), [t])
                rel(b, tv)
                return tv
            return out_
        tv_ = softplus(0)
        for h in range(4):
            nxt = softplus(h + 1) if h < 3 else None
            tv = attend(h, tv_)()
            tv_ = nxt
        to_fm([osb[:, i, :] for i in range(4)], 2, lambda f: catT[:, 4 + f, :], None, [tv])
        barrier()
        lend = borrow()

        mqT = view(lend(2 * 512), [512, 2], [1, 512])
        ckT = lend(512)
        for i in range(4):
            group_norm(mq[:, i, :], 1, 256, 1e-6, small, tmpr, False)
            t = group_norm(ckv[:, i, :], 1, 128, 1e-6, small, tmpr, False)
        qn, kn = VC[f"qn{l}"], VC[f"kn{l}"]
        to_fm([mq[:, i, :] for i in range(4)], 2, lambda f: mqT[:, f, :],
              lambda f, o, i_, tt: act(o, i_, ACT.Copy, scale=qn[:, f:f + 1], w=[tt]), [t])
        t_cT = to_fm([ckv[:, i, :] for i in range(4)], 1, lambda f: ckT,
                     lambda f, o, i_, tt: act(o, i_, ACT.Copy, scale=kn[:, 0:1], w=[tt]), [t])
        uq = view(lend(768), [384, 2], [1, 384])
        usw = view(lend(256), [128, 2], [1, 128])
        ukv = lend(512)
        tw = [load_small(uq, I["mla_w_uq_2"][l].rearrange("(k p) c -> p k c", p=128)),
              load_small(usw, I["uq_sw"][l].rearrange("(k p) c -> p k c", p=128)),
              load_small(ukv, I["mla_w_ukv_2"][l])]
        qh = view(lend(4 * 512), [512, 4], [1, 512])
        kh = view(lend(4 * 512), [512, 4], [1, 512])
        for h in range(4):
            b, pv, bw = bank()
            b2, pv2, bw2 = bank()
            b3, pv3, bw3 = bank()
            for k in range(2):
                mm(pv[0:96, :], uq[:, k, 96 * h:96 * h + 96], mqT[:, k, :], k == 0, k == 1, bw + tw + [t_cT] if k == 0 else ())
            for k in range(2):
                mm(pv2[RP, :], usw[:, k, 32 * h:32 * h + 32], mqT[:, k, :], k == 0, k == 1, bw2 if k == 0 else ())
            t = mm(pv3[0:64, :], ukv[:, 128 * h:128 * h + 64], ckT, True, True, bw3, True)
            ta = scopy(qh[0:64, h, :], pv[0:64, :], [t])
            ta = scopy(kh[0:64, h, :], pv3[0:64, :])
            rel(b3, ta)
            tv = rope(qh[RP, h, :], pv[RP, :], pv2[RP, :], [ta])
            vcopy(kh[RP, h, :], krT[RP, :])
            rel(b, tv, ta)
            rel(b2, tv)
        vm = view(lend(4 * 256), [256, 4], [1, 256])
        for i in range(4):
            b, pv, bw = bank()
            t = mm(pv, ckT[:, 128 * i:128 * i + 128], ukv, True, True, bw, True)
            tv = vcopy(view(vm[:, i, :], [64, 4], [1, 64]), view(pv[:, 64:65], [128, 4], [1, 64]), [t])
            rel(b, tv)
        om = view(lend(4 * 256), [256, 4], [1, 256])
        pr = [lend(512), lend(512)]
        pT = [view(lend(512), [128, 4], [1, 128]) for _ in range(2)]
        pr_f, pT_f = [(), ()], [(), ()]
        SC = 96 ** -0.5
        n = 0
        st = lend(8 * 16)
        for h in range(4):
            for i in range(4):
                N = 128 * (i + 1)
                z_ = n % 2
                sc_ = st[:, 8 * (n % 16):8 * (n % 16) + 8]
                b, pv, bw = bank()
                mm(pv[:, 0:N], qh[0:96, h, 128 * i:128 * i + 128], kh[0:96, h, 0:N], True, False, bw + [(V, V.n)] if n == 0 else bw)
                t = mm(pv[:, N - 128:N], C["ident"], C["negLT"], False, True, (), True)
                tm = vred(sc_[:, 0:1], pv[:, 0:N], MAX, [t])
                tm = vts(sc_[:, 1:2], sc_[:, 0:1], -SC, None, MUL)
                ta = act(pr[z_][:, 0:N], pv[:, 0:N], ACT.Exp, scale=SC, bias=sc_[:, 1:2], w=[tm] + list(pr_f[z_]),
                         acc=sc_[:, 2:3])
                rel(b, ta)
                tr_ = recip(sc_[:, 3:4], sc_[:, 2:3], [ta])
                b, pv, bw = bank()
                for s_ in range(i + 1):
                    t = tr(pv[:, 128 * s_:128 * s_ + 128], pr[z_][:, 128 * s_:128 * s_ + 128],
                           bw + [ta] if s_ == 0 else (), s_ == i)
                pr_f[z_] = (t,)
                ta = scopy(view(pT[z_], [1, N]), pv[:, 0:N], [t] + list(pT_f[z_]))
                rel(b, ta)
                b, pv, bw = bank()
                for s_ in range(i + 1):
                    t = mm(pv[:, 0:64], pT[z_][:, s_, :], vm[:, s_, 64 * h:64 * h + 64], s_ == 0, s_ == i,
                           bw + [ta] if s_ == 0 else (), s_ == i)
                pT_f[z_] = (t,)
                tv = vts(om[:, i, 64 * h:64 * h + 64], pv[:, 0:64], sc_[:, 3:4], None, MUL, w=[t])
                rel(b, tv)
                n += 1
        t = to_fm([om[:, i, :] for i in range(4)], 2, lambda f: catT[:, 6 + f, :], None, [tv])
        ring_back(barrier())
        ct = split_x(catT, hh)

        def ev(c, i, pv, t, n):
            x_ = hX[:, i, c:c + 512]
            return stt(x_, x_, ALPHA, pv, MUL, ADD, [t])
        gemm_tm(I["mix_w_o_2"][l], 0, 1024, 8, hh, W512, ev, xt=ct)
        barrier()
        top[0] = m0_
        layer_norm_all(l, 1)

    hT_from_x()
    for l in range(2):
        ffn(l, "ffa_w_in_2", "ffa_w_out_2", 0)
        mixer(l)
        ffn(l, "ffb_w_in_2", "ffb_w_out_2", 2)
        m_ = top[0]
        pTl = view(al(1024), [512, 2], [1, 512])
        pop = opnd(2, 512)
        sg = view(al(4 * 512), [512, 4], [1, 512])
        t_p = load_small(pTl, I["pT"][l].rearrange("(k p) c -> p k c", p=128))
        pt = split_x(pTl, pop, [t_p])
        for hf in range(2):
            gemm_tm(I["ple_w_gate_2"][l], 512 * hf, 512, 8, hh, W512,
                    lambda c, i, pv, t, n: act(sg[:, i, :], pv, ACT.Sigmoid, w=[t, (V, V.n)]))

            def ev_p(c, i, pv, t, n, hf=hf):
                t1 = vtt(sg[:, i, :], sg[:, i, :], pv, MUL, [t, (S, S.n)])
                x_ = hX[:, i, 512 * hf:512 * hf + 512]
                vtt(x_, x_, sg[:, i, :], ADD)
                return t1
            gemm_tm(I["ple_w_proj_2"][l], 512 * hf, 512, 2, pop, W512, ev_p, pt)
        barrier()
        top[0] = m_
        if l == 0:
            hT_from_x()
    for i in range(4):
        load_small(out[0, 128 * i:128 * i + 128, :], hX[:, i, :], [(V, V.n)])


_WEIGHTS = ["x", "ctx", "b_ada", "w_ada", "w_in", "rw_w2", "rw_a2", "rw_g2", "rw_lnw", "rw_lnb", "ml_nw",
            "p_a", "p_b", "p_c", "w_out", "w_mlp1", "w_mlp2", "g_final", "positions_2", "ffa_w_in_2", "ffa_w_out_2",
            "mix_w_in_2", "gdn_a_log_2", "gdn_dt_bias_2", "gdn_norm_w_2", "mla_w_uq_2", "mla_w_ukv_2", "mix_w_o_2",
            "ffb_w_in_2", "ffb_w_out_2", "ln_g_2", "ln_b_2", "ple_w_gate_2", "ple_w_proj_2"]
_SQUEEZE = {"w_ada", "w_in", "p_a", "p_b", "p_c", "w_out", "w_mlp1", "w_mlp2"}


def _fm(v):
    v = np.asarray(v)
    return np.ascontiguousarray(v.reshape(-1, 128).T)


def arrays_of(inputs):
    a = {k: np.ascontiguousarray(inputs[k]) for k in _WEIGHTS}
    for k in _SQUEEZE:
        a[k] = a[k][0]
    g = {k: np.asarray(inputs[k]) for k in ("c", "c_ctx", "b_ada", "g_norm1", "g_norm2", "mu_prev", "mu_next", "rw_w0",
                                             "rw_a0", "rw_kk", "rw_ka", "rw_rk", "cv_dw", "cv_db", "cv_lnw", "cv_lnb",
                                             "gdn_conv_w_2", "mla_q_norm_w_2", "mla_kv_norm_w_2", "ml_ib", "ml_fb",
                                             "p_2", "mla_w_uq_2", "mix_w_in_2")}
    cdw = np.transpose(g["cv_dw"][0].reshape(31, 4, 128), (2, 1, 0)).reshape(128, 124)
    gcw = [np.transpose(g["gdn_conv_w_2"][l].reshape(4, 12, 128), (2, 1, 0)).reshape(128, 48) for l in range(2)]
    parts = [_fm(g["c"]), _fm(g["c_ctx"]), _fm(g["b_ada"]), _fm(g["g_norm1"]), _fm(g["g_norm2"]), _fm(g["mu_prev"]),
             _fm(g["mu_next"]), _fm(g["rw_w0"]), _fm(g["rw_a0"]), _fm(g["rw_kk"]), _fm(g["rw_ka"]), _fm(g["rw_rk"]),
             cdw, _fm(g["cv_db"]), _fm(g["cv_lnw"]), _fm(g["cv_lnb"]), gcw[0], gcw[1],
             _fm(g["mla_q_norm_w_2"][0]), _fm(g["mla_q_norm_w_2"][1]),
             _fm(g["mla_kv_norm_w_2"][0]), _fm(g["mla_kv_norm_w_2"][1])]
    a["vecs"] = np.ascontiguousarray(np.concatenate(parts, axis=1))
    a["mlgb"] = np.ascontiguousarray(np.stack([g["ml_ib"][0], g["ml_fb"][0]], axis=1).reshape(16))
    a["pT"] = np.ascontiguousarray(np.transpose(g["p_2"][:, 0], (0, 2, 1)))
    u = g["mla_w_uq_2"].reshape(2, 256, 4, 96)
    a["uq_sw"] = np.ascontiguousarray(np.concatenate([u[..., 80:96], u[..., 64:80]], axis=-1).reshape(2, 256, 128))
    r = g["mix_w_in_2"][:, :, 3216:3248]
    z64 = np.zeros(r.shape[:2] + (64,), r.dtype)
    a["kr2"] = np.ascontiguousarray(np.concatenate([z64, r, z64, r[..., 16:32], r[..., 0:16]], axis=-1))
    a["consts"] = const_tables()[1]
    return a


def kernel(**inputs):
    import concourse.bacc as _bacc
    from concourse.bass_utils import run_bass_kernel_spmd as _run

    nc = _bacc.Bacc("TRN2", target_bir_lowering=False, num_devices=1)
    arrays = arrays_of(inputs)
    I = {k: nc.dram_tensor(f"in_{k}", v.shape, mybir.dt.from_np(v.dtype), kind="ExternalInput").ap()
         for k, v in arrays.items()}
    out = nc.dram_tensor("out", (1, 512, 1024), F32, kind="ExternalOutput").ap()
    I["spill"] = nc.dram_tensor("spill", (128, 8, 512), F32, kind="Internal").ap()
    build(nc, I, out)
    r = _run(nc, [{f"in_{k}": v for k, v in arrays.items()}], core_ids=[0])
    return r.results[0]["out"]
```
